# Optimizing a Trainium2 kernel written in Bass

```python
import jax, jax.numpy as jnp
from jax import lax
import numpy as np

D_MODEL = 1024
BATCH = 1
SEQ = 2048
DEPTH = 1

HEAD_DIM = 64
ATT_Q_HEADS = 6
ATT_KV_HEADS = 2
ATT_GROUP = ATT_Q_HEADS // ATT_KV_HEADS
RET_HEADS = 6
POOL_WIDTH = D_MODEL - (ATT_Q_HEADS + RET_HEADS) * HEAD_DIM
POOL_WINDOWS = (2, 4, 8, 16)
POOL_GROUPS = len(POOL_WINDOWS)
POOL_GROUP_WIDTH = POOL_WIDTH // POOL_GROUPS
WINDOW = 128
BLOCK = 128
RET_CHUNK = 128
N_BUCKETS = 32
MAX_DISTANCE = 128
D_FF = 4 * D_MODEL
RMS_EPS = 1e-6
ROPE_BASE = 10000.0
NEG_INF = -1e30

ATT_Q_W = ATT_Q_HEADS * HEAD_DIM
ATT_KV_W = ATT_KV_HEADS * HEAD_DIM
RET_W = RET_HEADS * HEAD_DIM
IN_SIZES = (ATT_Q_W, ATT_KV_W, ATT_KV_W, RET_W, RET_W, RET_W, RET_W, POOL_WIDTH)
IN_WIDTH = sum(IN_SIZES)
SPLIT_POINTS = tuple(int(v) for v in np.cumsum(IN_SIZES)[:-1])
MIX_WIDTH = ATT_Q_W + RET_W + POOL_WIDTH

kernel_name = "hybrid_swa_retention_pool_block"

def rms_norm(x, g):
    xf = x.astype(jnp.float32)
    y = xf * lax.rsqrt(jnp.mean(xf * xf, axis=-1, keepdims=True) + RMS_EPS)
    return (y * g.astype(jnp.float32)).astype(x.dtype)

def t5_bucket(dist):
    max_exact = N_BUCKETS // 2
    n = np.maximum(dist, 0)
    large = max_exact + (np.log(np.maximum(n, 1) / max_exact)
                         / np.log(MAX_DISTANCE / max_exact)
                         * (N_BUCKETS - max_exact)).astype(np.int64)
    large = np.minimum(large, N_BUCKETS - 1)
    return np.where(n < max_exact, n, large).astype(np.int32)

def sliding_window_attention(q, k, v, sinks, rel_bias):
    B, S = q.shape[0], q.shape[1]
    N = S // BLOCK
    qb = q.reshape(B, N, BLOCK, ATT_KV_HEADS, ATT_GROUP, HEAD_DIM)
    kb = k.reshape(B, N, BLOCK, ATT_KV_HEADS, HEAD_DIM)
    vb = v.reshape(B, N, BLOCK, ATT_KV_HEADS, HEAD_DIM)

    def with_prev(t):
        prev = jnp.pad(t, ((0, 0), (1, 0), (0, 0), (0, 0), (0, 0)))[:, :-1]
        return jnp.concatenate([prev, t], axis=2)

    kk, vv = with_prev(kb), with_prev(vb)

    i = np.arange(BLOCK)[:, None]
    j = np.arange(2 * BLOCK)[None, :]
    dist = BLOCK + i - j
    band = (dist >= 0) & (dist < WINDOW)
    in_cur = j >= BLOCK
    blk = jnp.arange(N)[:, None, None]
    valid = jnp.asarray(band)[None] & ((blk > 0) | jnp.asarray(in_cur)[None])

    bias = rel_bias.astype(jnp.float32)[t5_bucket(dist)]
    bias = jnp.transpose(bias, (2, 0, 1)).reshape(ATT_KV_HEADS, ATT_GROUP, BLOCK, 2 * BLOCK)

    scores = jnp.einsum('bnihgd,bnjhd->bnhgij', qb, kk).astype(jnp.float32)
    scores = scores * (HEAD_DIM ** -0.5) + bias
    scores = jnp.where(valid[None, :, None, None], scores, NEG_INF)

    sink = sinks.astype(jnp.float32).reshape(ATT_KV_HEADS, ATT_GROUP)[None, None, :, :, None]
    m = jnp.maximum(scores.max(axis=-1), sink)
    p = jnp.exp(scores - m[..., None])
    denom = p.sum(axis=-1) + jnp.exp(sink - m)
    o = jnp.einsum('bnhgij,bnjhd->bnihgd', p, vv.astype(jnp.float32))
    o = o / jnp.transpose(denom, (0, 1, 4, 2, 3))[..., None]
    return o.reshape(B, S, ATT_Q_W).astype(q.dtype)

def rotary(x, pos):
    inv = 1.0 / (ROPE_BASE ** jnp.linspace(0.0, 1.0, HEAD_DIM // 2, dtype=jnp.float32))
    ang = pos.astype(jnp.float32)[:, None] * inv[None, :]
    cos = jnp.cos(ang)[None, :, None, :]
    sin = jnp.sin(ang)[None, :, None, :]
    xf = x.astype(jnp.float32).reshape(x.shape[:-1] + (HEAD_DIM // 2, 2))
    x1, x2 = xf[..., 0], xf[..., 1]
    return jnp.stack([x1 * cos - x2 * sin, x1 * sin + x2 * cos], axis=-1).reshape(x.shape)

def retention(q, k, v, g):
    B, S = q.shape[0], q.shape[1]
    C = RET_CHUNK
    N = S // C
    H, d = RET_HEADS, HEAD_DIM
    pos = jnp.arange(S)
    qf = rotary(q, pos)
    kf = rotary(k, pos) * (d ** -0.5)
    vf = v.astype(jnp.float32)

    lg = jnp.log(1.0 - 2.0 ** (-5.0 - jnp.arange(H, dtype=jnp.float32)))
    idx = jnp.arange(C, dtype=jnp.float32)
    diff = idx[:, None] - idx[None, :]
    dmask = jnp.where(diff >= 0, jnp.exp(lg[:, None, None] * jnp.maximum(diff, 0.0)), 0.0)

    qc = qf.reshape(B, N, C, H, d)
    kc = kf.reshape(B, N, C, H, d)
    vc = vf.reshape(B, N, C, H, d)

    inner = jnp.einsum('bnihd,bnjhd->bnhij', qc, kc) * dmask
    inner = jnp.einsum('bnhij,bnjhe->bnihe', inner, vc)

    zeta = jnp.exp(lg[:, None] * (C - 1.0 - idx)[None, :])
    U = jnp.einsum('bnjhd,bnjhe,hj->nbhde', kc, vc, zeta)
    g_chunk = jnp.exp(lg * C)[None, :, None, None]

    def step(R, u):
        return R * g_chunk + u, R

    _, R_prev = lax.scan(step, jnp.zeros((B, H, d, d), jnp.float32), U)
    xi = jnp.exp(lg[None, :] * (idx[:, None] + 1.0))
    cross = jnp.einsum('bnihd,nbhde->bnihe', qc, R_prev) * xi[None, None, :, :, None]

    o = inner + cross
    o = o * lax.rsqrt(jnp.mean(o * o, axis=-1, keepdims=True) + RMS_EPS)
    o = o.reshape(B, S, H, d)
    out = jax.nn.silu(g.astype(jnp.float32)) * o
    return out.reshape(B, S, RET_W).astype(q.dtype)

def pool_mixer(u, pool_w, pool_scale):
    B, S = u.shape[0], u.shape[1]
    uf = u.astype(jnp.float32)
    csp = jnp.pad(jnp.cumsum(uf, axis=1), ((0, 0), (1, 0), (0, 0)))
    t = jnp.arange(S)
    groups = []
    for gi, w in enumerate(POOL_WINDOWS):
        sl = slice(gi * POOL_GROUP_WIDTH, (gi + 1) * POOL_GROUP_WIDTH)
        lo = jnp.maximum(t + 1 - w, 0)
        win_sum = csp[:, 1:, sl] - csp[:, lo, sl]
        cnt = (t + 1 - lo).astype(jnp.float32)[None, :, None]
        groups.append(win_sum / cnt - uf[..., sl])
    pooled = jnp.stack(groups, axis=2)
    mixed = jnp.einsum('bsgc,gcd->bsgd', pooled, pool_w.astype(jnp.float32))
    mixed = mixed.reshape(B, S, POOL_WIDTH) * pool_scale.astype(jnp.float32)
    return mixed.astype(u.dtype)

def mixer_sublayer(x, norm_g, w_in, sinks, rel_bias, pool_w, pool_scale, w_out):
    B, S = x.shape[0], x.shape[1]
    h = rms_norm(x, norm_g)
    z = h @ w_in
    qa, ka, va, qr, kr, vr, gr, up = jnp.split(z, SPLIT_POINTS, axis=-1)
    ya = sliding_window_attention(
        qa.reshape(B, S, ATT_Q_HEADS, HEAD_DIM),
        ka.reshape(B, S, ATT_KV_HEADS, HEAD_DIM),
        va.reshape(B, S, ATT_KV_HEADS, HEAD_DIM), sinks, rel_bias)
    yr = retention(qr.reshape(B, S, RET_HEADS, HEAD_DIM),
                   kr.reshape(B, S, RET_HEADS, HEAD_DIM),
                   vr.reshape(B, S, RET_HEADS, HEAD_DIM),
                   gr.reshape(B, S, RET_HEADS, HEAD_DIM))
    yp = pool_mixer(up, pool_w, pool_scale)
    y = jnp.concatenate([ya, yr, yp], axis=-1)
    return x + y @ w_out

def mlp_sublayer(x, norm_g, w_up, w_down):
    h = rms_norm(x, norm_g)
    return x + jnp.square(jax.nn.relu(h @ w_up)) @ w_down

def setup_inputs(seed: int = 0) -> dict:
    key = jax.random.key(seed)
    ks = jax.random.split(key, 12)
    f32 = jnp.float32
    nrm = lambda k, s: jax.random.normal(k, s, dtype=f32)
    return {
        "x": nrm(ks[0], (BATCH, SEQ, D_MODEL)),
        "attn_norm_g": 1.0 + 0.1 * nrm(ks[1], (DEPTH, D_MODEL)),
        "w_in": nrm(ks[2], (DEPTH, D_MODEL, IN_WIDTH)) * D_MODEL ** -0.5,
        "attn_sinks": 0.5 * nrm(ks[3], (DEPTH, ATT_Q_HEADS)),
        "rel_bias": 0.5 * nrm(ks[4], (N_BUCKETS, ATT_Q_HEADS)),
        "pool_w": nrm(ks[5], (DEPTH, POOL_GROUPS, POOL_GROUP_WIDTH, POOL_GROUP_WIDTH)) * POOL_GROUP_WIDTH ** -0.5,
        "pool_scale": 1.0 + 0.1 * nrm(ks[6], (DEPTH, POOL_WIDTH)),
        "w_out": nrm(ks[7], (DEPTH, MIX_WIDTH, D_MODEL)) * MIX_WIDTH ** -0.5,
        "mlp_norm_g": 1.0 + 0.1 * nrm(ks[8], (DEPTH, D_MODEL)),
        "w_up": nrm(ks[9], (DEPTH, D_MODEL, D_FF)) * D_MODEL ** -0.5,
        "w_down": nrm(ks[10], (DEPTH, D_FF, D_MODEL)) * D_FF ** -0.5,
        "final_norm_g": 1.0 + 0.1 * nrm(ks[11], (D_MODEL,)),
    }

def reference(x, attn_norm_g, w_in, attn_sinks, rel_bias, pool_w, pool_scale, w_out,
              mlp_norm_g, w_up, w_down, final_norm_g):
    for layer in range(DEPTH):
        x = mixer_sublayer(x, attn_norm_g[layer], w_in[layer], attn_sinks[layer], rel_bias,
                           pool_w[layer], pool_scale[layer], w_out[layer])
        x = mlp_sublayer(x, mlp_norm_g[layer], w_up[layer], w_down[layer])
    return rms_norm(x, final_norm_g)


_drawn_inputs = setup_inputs


def setup_inputs(seed=0):
    import zlib

    import numpy as np

    out = dict(_drawn_inputs(seed))
    spreads = {}
    factors = {'attn_sinks': 8.0}
    for name, (base, spread) in spreads.items():
        noise = np.random.default_rng([zlib.crc32(name.encode()), seed]).standard_normal(out[name].shape)
        drawn = base * np.exp(spread * noise) if base else spread * noise
        out[name] = __import__('jax').numpy.asarray(drawn.astype(out[name].dtype))
    for name, factor in factors.items():
        out[name] = (out[name] * factor).astype(out[name].dtype)
    return out
```

```python
from contextlib import ExitStack

import numpy as np

import concourse.bass as bass
from concourse import mybir

P = 128
D = 1024
SEQ = 2048
HEAD = 64
NQH, NKV, NRET = 6, 2, 6
GROUP = NQH // NKV
POOLW = 256
WINDOWS = (2, 4, 8, 16)
FF = 4 * D
EPS = 1e-6
NEG = -1e30
NBUCKET = 32
MAXDIST = 128
SCALE = HEAD ** -0.5

C = D // P
QT = 512
NQ = SEQ // QT
NB = QT // P
HT = 1024
NH = SEQ // HT
HB = HT // P
RING = 6
STAGE = 3
NU = 27
NG = FF // (2 * P)
TABW = 2 * NB * HEAD + 32
PADW = 16

F32 = mybir.dt.float32
F32R = mybir.dt.float32r
ALU = mybir.AluOpType
ACT = mybir.ActivationFunctionType
AX = mybir.AxisListType.X

CST = {}
_at = 0
for _name, _width in (("ident", P), ("mask", NRET * P), ("gchunk", 3 * P), ("zeta", NRET), ("xi2", NRET),
                      ("xih", NRET), ("invw", 2), ("mhalf", 8), ("eps", 8)):
    CST[_name] = (_at, _at + _width)
    _at += _width
CSTW = _at

T_GROUP, T_UP1, T_OA, T_OR, NT = 6, 22, 23, 31, 39


def last_tile_of_unit(u):
    if u < 6:
        return u
    if u < 18:
        return T_GROUP + 4 * ((u - 6) // 3) + 3
    return T_UP1 if u == 18 else (T_OR - 1 if u < 22 else NT - 1)


def slot_owner(u):
    if u >= RING:
        return True, u - RING
    return False, max(v for v in range(NU) if v % RING == u)


class Events:

    def __init__(self, sem, per, by=1):
        self.sem, self.per, self.by = sem, per, by

    @property
    def primed(self):
        return self.per * self.by

    def now(self, r, i):
        return r * (self.per * self.by) + (self.per + i + 1) * self.by

    def before(self, r, i):
        return r * (self.per * self.by) + (i + 1) * self.by


def build(nc, x, wmix, wmlp, cst, tab, onehot, gmix, gmlp, gfin, sinks, rel_bias, pool_w, pool_scale, out):
    x2_dram = nc.dram_tensor("x2_dram", (SEQ, D), F32).ap()
    rows_dram = nc.dram_tensor("bias_rows_dram", (NQH, P * 384), F32).ap()

    with ExitStack() as ctx:
        def sb(name, shape, dt=F32, stack=ctx):
            return stack.enter_context(nc.sbuf_tensor(name, shape, dt))

        def ps(name):
            return ctx.enter_context(nc.psum_tensor(name, [P, 512], F32))

        def sem(name):
            return ctx.enter_context(nc.semaphore(name))

        ring_hi = sb("ring_hi", [P, RING, 1024], F32R)
        ring_lo = sb("ring_lo", [P, RING, 1024], F32R)
        stage = sb("stage", [P, STAGE, 1024])
        ident = sb("ident", [P, P])
        mhalf = sb("mhalf", [P, 8])
        epsc = sb("epsc", [P, 8])
        gmix_sb = sb("gmix_sb", [P, C])
        gmlp_sb = sb("gmlp_sb", [P, C])
        ssum = sb("ssum", [P, 8])
        var = sb("var", [P, 8])
        rstd = sb("rstd", [P, 8])

        with ExitStack() as mem:
            def ms(name, shape, dt=F32):
                return sb(name, shape, dt, mem)
            xq = ms("xq", [P, NB, D])
            hT_hi = ms("hT_hi", [P, C, QT], F32R)
            hT_lo = ms("hT_lo", [P, C, QT], F32R)
            yA_hi = ms("yA_hi", [P, 3, QT], F32R)
            yA_lo = ms("yA_lo", [P, 3, QT], F32R)
            qT = ms("qT", [P, 3, QT])
            kT = ms("kT", [P, P + QT])
            vT = ms("vT", [P, QT])
            vtok = ms("vtok", [P, NB + 1, P])
            up = ms("up", [P, 2, PADW + QT])
            zt = ms("zt", [P, NB, 4 * 3 * P])
            bias = ms("bias", [P, NQH, 2 * P])
            bias0 = ms("bias0", [P, NQH, 2 * P])
            cmask = ms("cmask", [P, NRET * P])
            gch = ms("gch", [P, 3 * P])
            R = ms("R", [P, 3 * P])
            tabs = ms("tabs", [P, TABW])
            small = ms("small", [P, 32])
            nsink = ms("nsink", [P, NQH])
            sinkb = ms("sinkb", [P, NQH])
            pscale = ms("pscale", [P, 2])
            poolw = ms("poolw", [P, 2, P])
            sc = ms("sc", [P, 2, 3 * 2 * P])
            pt = ms("pt", [P, 2, 2 * 3 * P])
            rmax = ms("rmax", [P, 2, 3])
            nmax = ms("nmax", [P, 2, 3])
            sde = ms("sde", [P, 2, 3])
            ses = ms("ses", [P, 2, 3])
            rsum = ms("rsum", [P, 2, 3])
            rinv = ms("rinv", [P, 2, 3])
            rotA = ms("rotA", [P, 6 * P])
            qk = ms("qk", [P, 6 * P])
            kz = ms("kz", [P, 3 * P])
            osb = ms("osb", [P, 3 * P])
            ss6 = ms("ss6", [P, 6])
            v6 = ms("v6", [P, 6])
            r6 = ms("r6", [P, 6])
            s6 = ms("s6", [P, 6])
            pooled = ms("pooled", [P, QT])
            p16 = ms("p16", [P, PADW])
            sc_flat = sc[:, :, :].rearrange("p a b -> p (a b)")
            pt_flat = pt[:, :, :].rearrange("p a b -> p (a b)")
            qkT = sc_flat[:, 0:768]
            Pm = sc_flat[:, 768:1536]
            sq = pt_flat[:, 0:384]
            th = pt_flat[:, 384:768]
            gate = pt_flat[:, 768:1152]
            yv = pt_flat[:, 1152:1536]
            xn_a, xn_b = sc_flat[:, 0:1024], pt_flat[:, 0:1024]
            xn = (xn_a, xn_b)
            tn = (sc_flat[:, 1024:1536], pt_flat[:, 1024:1536])
            qT_flat = qT[:, :, :].rearrange("p a b -> p (a b)")
            win_a = qT_flat[:, 0:PADW + QT]
            win_b = qT_flat[:, PADW + QT:2 * (PADW + QT)]
            relb = zt[0:NBUCKET + 1, 0, 0:NQH]
            relw = zt[0:NBUCKET + 1, 1, 0:NQH * P].rearrange("p (h m) -> p h m", h=NQH)
            oneh = zt[0:NBUCKET + 1, 0, 64:64 + 384]
            rrow = zt[:, 2:4, :].rearrange("p a b -> p (a b)")[:, 0:NQH * 384].rearrange("p (h m) -> p h m", h=NQH)

        with ExitStack() as mem:
            def ml(name, shape, dt=F32):
                return sb(name, shape, dt, mem)
            x2 = ml("x2", [P, HB, D])
            h2T_hi = ml("h2T_hi", [P, C, HT], F32R)
            h2T_lo = ml("h2T_lo", [P, C, HT], F32R)
            u_hi = ml("u_hi", [P, 2, HT], F32R)
            u_lo = ml("u_lo", [P, 2, HT], F32R)
            fg = ml("fg", [P, D])
            xn2 = ml("xn2", [P, 2, D])
            tn2 = ml("tn2", [P, 2, QT])
            relu = ml("relu", [P, 2, QT])
            rsq = ml("rsq", [P, 2, QT])

        bank = [ps(f"bank{i}") for i in range(8)]
        dense = bank[0:3]
        S0, S1, T0, T1, OB = bank[3], bank[4], bank[5], bank[6], bank[7]
        up_bank = (bank[5], bank[6])
        down_bank = bank[0:4]

        s_const = sem("s_const")
        s_ident = sem("s_ident")
        s_rel = sem("s_rel")
        s_relw = sem("s_relw")
        s_browmm = sem("s_browmm")
        s_brow = sem("s_brow")
        s_rowst = sem("s_rowst")
        s_bias = sem("s_bias")
        s_init = sem("s_init")
        s_pm = sem("s_pm")

        x_full = [Events(sem(f"x_full{b}"), 1, 16) for b in range(NB)]
        x2_stored = [Events(sem(f"x2_stored{b}"), 1, 16) for b in range(NB)]
        tab_full = Events(sem("tab_full"), 1, 16)
        st_full = [Events(sem(f"st_full{s}"), NU // STAGE, 16) for s in range(STAGE)]
        sq_done = Events(sem("sq_done"), 4)
        var_done = Events(sem("var_done"), 4)
        rstd_done = Events(sem("rstd_done"), 4)
        xn_done = Events(sem("xn_done"), 4)
        xtr_done = Events(sem("xtr_done"), 8)
        tn_done = Events(sem("tn_done"), 8)
        xhi_done = Events(sem("xhi_done"), 8)
        xlo_done = Events(sem("xlo_done"), 8)
        whi_done = Events(sem("whi_done"), NU)
        wlo_done = Events(sem("wlo_done"), NU)
        tile_done = Events(sem("tile_done"), NT)
        z_evac = Events(sem("z_evac"), T_OA)
        x2_evac = Events(sem("x2_evac"), NT - T_OA)
        carried = Events(sem("carried"), 4)
        vtr_done = Events(sem("vtr_done"), 1)
        v_evac = Events(sem("v_evac"), 1)
        s_done = Events(sem("s_done"), 8)
        sc_done = Events(sem("sc_done"), 16)
        max_done = Events(sem("max_done"), 8)
        nmax_done = Events(sem("nmax_done"), 8)
        sde_done = Events(sem("sde_done"), 8)
        exp_done = Events(sem("exp_done"), 32)
        den_done = Events(sem("den_done"), 8)
        rinv_done = Events(sem("rinv_done"), 8)
        pn_done = Events(sem("pn_done"), 24)
        ptr_done = Events(sem("ptr_done"), 8)
        pt_evac = Events(sem("pt_evac"), 16)
        o_done = Events(sem("o_done"), 8)
        yAhi_done = Events(sem("yAhi_done"), 8)
        yAlo_done = Events(sem("yAlo_done"), 8)
        rotA_done = Events(sem("rotA_done"), 4)
        rotB_done = Events(sem("rotB_done"), 8)
        qk_done = Events(sem("qk_done"), 4)
        kz_done = Events(sem("kz_done"), 4)
        qktr_done = Events(sem("qktr_done"), 8)
        qkT_evac = Events(sem("qkT_evac"), 8)
        rs_done = Events(sem("rs_done"), 8)
        pm_done = Events(sem("pm_done"), 8)
        ro_done = Events(sem("ro_done"), 4)
        ru_done = Events(sem("ru_done"), 4)
        rg_done = Events(sem("rg_done"), 4)
        R_done = Events(sem("R_done"), 8)
        osb_done = Events(sem("osb_done"), 4)
        sqr_done = Events(sem("sqr_done"), 4)
        th_done = Events(sem("th_done"), 4)
        ss6_done = Events(sem("ss6_done"), 4)
        v6_done = Events(sem("v6_done"), 8)
        r6_done = Events(sem("r6_done"), 4)
        s6_done = Events(sem("s6_done"), 4)
        gate_done = Events(sem("gate_done"), 4)
        ya_done = Events(sem("ya_done"), 4)
        y_done = Events(sem("y_done"), 4)
        ytr_done = Events(sem("ytr_done"), 4)
        yRhi_done = Events(sem("yRhi_done"), 4)
        yRlo_done = Events(sem("yRlo_done"), 4)
        win_done = Events(sem("win_done"), 6)
        pool16_done = Events(sem("pool16_done"), 8)
        pooled_done = Events(sem("pooled_done"), 4)
        mix_done = Events(sem("mix_done"), 2)
        yPhi_done = Events(sem("yPhi_done"), 2)
        yPlo_done = Events(sem("yPlo_done"), 2)
        fg_full = sem("fg_full")
        m_x_full = [Events(sem(f"m_x_full{b}"), 1, 16) for b in range(HB)]
        m_out = [Events(sem(f"m_out{b}"), 1, 16) for b in range(HB)]
        m_st_full = [Events(sem(f"m_st_full{s}"), 2, 16) for s in range(2)]
        m_sq = Events(sem("m_sq"), 2 * HB)
        m_var = Events(sem("m_var"), 2 * HB)
        m_rstd = Events(sem("m_rstd"), 2 * HB)
        m_xn = Events(sem("m_xn"), HB)
        m_xtr = Events(sem("m_xtr"), 2 * HB)
        m_tn = Events(sem("m_tn"), 2 * HB)
        m_xhi = Events(sem("m_xhi"), 2 * HB)
        m_xlo = Events(sem("m_xlo"), 2 * HB)
        m_whi = Events(sem("m_whi"), 4)
        m_wlo = Events(sem("m_wlo"), 4)
        m_up = Events(sem("m_up"), 4)
        m_relu = Events(sem("m_relu"), 4)
        m_rsq = Events(sem("m_rsq"), 4)
        m_uhi = Events(sem("m_uhi"), 4)
        m_ulo = Events(sem("m_ulo"), 4)
        m_down = Events(sem("m_down"), 16)
        m_acc = Events(sem("m_acc"), 16)
        m_fin = Events(sem("m_fin"), HB)

        def cview(name):
            a, b = CST[name]
            return cst[:, a:b]

        zeta = small[:, 0:6]
        xi2 = small[:, 6:12]
        xih = small[:, 12:18]
        invw = small[:, 18:20]

        def cos_of(b):
            return tabs[:, b * HEAD:(b + 1) * HEAD]

        def sin_of(b):
            return tabs[:, NB * HEAD + b * HEAD:NB * HEAD + (b + 1) * HEAD]

        def icnt_of(cc):
            return tabs[:, 2 * NB * HEAD + 16 * cc:2 * NB * HEAD + 16 * cc + 16]

        block = ctx.enter_context(nc.Block())

        @block.sync
        def _(sp):
            for e in [*x2_stored, *m_out]:
                sp.sem_inc(e.sem, e.primed)
            for e in [*x_full, tab_full, *st_full, *m_x_full]:
                sp.sem_inc(e.sem, e.primed)
            for e in m_st_full:
                sp.sem_inc(e.sem, 16)
            sp.dma_start(ident[:, :], cview("ident")).then_inc(s_ident, 16)
            sp.dma_start(mhalf[:, :], cview("mhalf")).then_inc(s_ident, 16)
            sp.dma_start(epsc[:, :], cview("eps")).then_inc(s_ident, 16)
            sp.dma_start(gmix_sb[:, :], gmix).then_inc(s_ident, 16)
            sp.dma_start(gmlp_sb[:, :], gmlp).then_inc(s_ident, 16)
            sp.wait_ge(s_init, 1)
            sp.dma_start(relb[0:NBUCKET, :], rel_bias).then_inc(s_rel, 16)
            sp.dma_start(oneh, onehot).then_inc(s_rel, 16)
            sp.dma_start(cmask[:, :], cview("mask")).then_inc(s_const, 16)
            sp.dma_start(gch[:, :], cview("gchunk")).then_inc(s_const, 16)
            sp.dma_start(small[:, 0:20], cst[:, CST["zeta"][0]:CST["invw"][1]]).then_inc(s_const, 16)
            sp.dma_start(sinkb[:, :], sinks.to_broadcast([P, NQH])).then_inc(s_const, 16)
            sp.dma_start(pscale[:, :], pool_scale).then_inc(s_const, 16)
            sp.wait_ge(s_pm, 1)
            for g in range(4):
                a = HEAD * (g % 2)
                sp.dma_start(poolw[a:a + HEAD, g // 2, a:a + HEAD], pool_w[g]).then_inc(s_const, 16)
            sp.wait_ge(s_brow, NQH)
            sp.dma_start(rows_dram.rearrange("h (p m) -> p h m", m=384), rrow).then_inc(s_rowst, 16)
            sp.wait_ge(s_rowst, 16)
            for h in range(NQH):
                src = rows_dram[h:h + 1, P - 1:P - 1 + P * 383].rearrange("a (p m) -> (a p) m", m=383)
                sp.dma_start(bias[:, h, :], src[:, 0:2 * P]).then_inc(s_bias, 16)

            with sp.Fori(0, NQ) as q:
                for b in range(NB):
                    sp.wait_ge(x2_stored[b].sem, x2_stored[b].before(q, 0))
                    sp.dma_start(xq[:, b, :], x[bass.ds(q * QT + b * P, P), :]).then_inc(x_full[b].sem, 16)
                sp.wait_ge(qk_done.sem, qk_done.before(q, 3))
                sp.wait_ge(pool16_done.sem, pool16_done.before(q, 7))
                sp.dma_start(tabs[:, :], tab[bass.ds(q * P, P), :]).then_inc(tab_full.sem, 16)
                for u in range(NU):
                    if u >= STAGE:
                        sp.wait_ge(wlo_done.sem, wlo_done.now(q, u - STAGE))
                    else:
                        sp.wait_ge(wlo_done.sem, wlo_done.before(q, NU - STAGE + u))
                    sp.dma_start(stage[:, u % STAGE, :], wmix[u]).then_inc(st_full[u % STAGE].sem, 16)
                for b in range(NB):
                    sp.wait_ge(x2_evac.sem, x2_evac.now(q, 8 + 2 * b + 1))
                    sp.dma_start(x2_dram[bass.ds(q * QT + b * P, P), :], xq[:, b, :]).then_inc(x2_stored[b].sem, 16)

            for b in range(NB):
                sp.wait_ge(x2_stored[b].sem, x2_stored[b].now(NQ - 1, 0))
            sp.dma_start(fg[:, :], gfin.to_broadcast([P, D])).then_inc(fg_full, 16)
            sp.wait_ge(wlo_done.sem, wlo_done.now(NQ - 1, NU - 1))
            for s in range(2):
                sp.dma_start(stage[:, s, :], wmlp[4 * NG - 2 + s]).then_inc(m_st_full[s].sem, 16)
            with sp.Fori(0, NH) as h:
                for b in range(HB):
                    sp.wait_ge(m_out[b].sem, m_out[b].before(h, 0))
                    sp.dma_start(x2[:, b, :], x2_dram[bass.ds(h * HT + b * P, P), :]).then_inc(m_x_full[b].sem, 16)
                with sp.Fori(0, NG) as g:
                    for u in range(4):
                        G = h * NG + g
                        if u >= 2:
                            sp.wait_ge(m_wlo.sem, m_wlo.now(G, u - 2))
                        else:
                            sp.wait_ge(m_wlo.sem, m_wlo.before(G, u + 2))
                        sp.dma_start(stage[:, u % 2, :], wmlp[bass.ds(g * 4 + u, 1)].rearrange("a p n -> (a p) n")).then_inc(m_st_full[u % 2].sem, 16)
                for b in range(HB):
                    sp.wait_ge(m_fin.sem, m_fin.now(h, b))
                    sp.dma_start(out[bass.ds(h * HT + b * P, P), :], x2[:, b, :]).then_inc(m_out[b].sem, 16)
            for b in range(HB):
                sp.wait_ge(m_out[b].sem, m_out[b].now(NH - 1, 0))

        @block.gpsimd
        def _(pool):
            for e in (wlo_done, xlo_done, rstd_done, m_xlo, m_rstd, var_done, m_var, rotB_done, kz_done,
                      rg_done, v6_done, r6_done, s6_done, win_done):
                pool.sem_inc(e.sem, e.primed)
            pool.sem_inc(m_wlo.sem, 2)
            pool.memset(relb, 1.0).then_inc(s_init, 1)
            pool.memset(poolw[:, :, :], 0.0).then_inc(s_pm, 1)
            pool.memset(kT[:, :], 0.0).then_inc(s_pm, 1)
            pool.memset(vtok[:, :, :], 0.0).then_inc(s_pm, 1)
            pool.memset(up[:, :, :], 0.0).then_inc(s_pm, 1)
            pool.memset(R[:, :], 0.0).then_inc(s_pm, 1)
            pool.memset(bias0[:, :, 0:P], NEG).then_inc(s_pm, 1)
            pool.wait_ge(s_bias, 16 * NQH)
            pool.tensor_copy(bias0[:, :, P:2 * P], bias[:, :, P:2 * P]).then_inc(s_pm, 1)
            pool.wait_ge(s_pm, 7)
            pool.wait_ge(s_ident, 80)
            pool.wait_ge(s_const, 16 * 9)

            def split_lo(q, u):
                pool.wait_ge(whi_done.sem, whi_done.now(q, u))
                s = u % RING
                pool.tensor_tensor(ring_lo[:, s, :], stage[:, u % STAGE, :], ring_hi[:, s, :].bitcast(F32),
                                   ALU.subtract).then_inc(wlo_done.sem, 1)

            def inv_rms(q, b):
                pool.wait_ge(sq_done.sem, sq_done.now(q, b))
                pool.tensor_tensor(var[:, b:b + 1], ssum[:, b:b + 1], epsc[:, 0:1], ALU.add).then_inc(var_done.sem, 1)
                pool.wait_ge(var_done.sem, var_done.now(q, b))
                pool.tensor_tensor(rstd[:, b:b + 1], var[:, b:b + 1], mhalf[:, 0:1], ALU.pow).then_inc(rstd_done.sem, 1)

            def x_lo(q, b):
                for j in range(2):
                    n = 2 * b + j
                    pool.wait_ge(xhi_done.sem, xhi_done.now(q, n))
                    pool.tensor_tensor(hT_lo[:, 4 * j:4 * j + 4, b * P:(b + 1) * P],
                                       tn[j].rearrange("p (c t) -> p c t", c=4),
                                       hT_hi[:, 4 * j:4 * j + 4, b * P:(b + 1) * P].bitcast(F32),
                                       ALU.subtract).then_inc(xlo_done.sem, 1)

            def rot_b(q, b):
                if b == 0:
                    pool.wait_ge(tab_full.sem, tab_full.now(q, 0))
                    pool.wait_ge(z_evac.sem, z_evac.now(q, T_GROUP + 7))
                    pool.wait_ge(kz_done.sem, kz_done.before(q, 3))
                    pool.wait_ge(qktr_done.sem, qktr_done.before(q, 7))
                else:
                    pool.wait_ge(kz_done.sem, kz_done.now(q, b - 1))
                    pool.wait_ge(qktr_done.sem, qktr_done.now(q, 2 * b - 1))
                src = zt[:, b, 0:768].rearrange("p (h i two) -> p h i two", h=12, two=2)
                dst = qk[:, :].rearrange("p (h i two) -> p h i two", h=12, two=2)
                sn = sin_of(b).rearrange("p (a i two) -> p a i two", a=1, two=2)
                for e in range(2):
                    pool.tensor_tensor(dst[:, :, :, e], src[:, :, :, 1 - e],
                                       sn[:, :, :, e].to_broadcast([P, 12, 32]), ALU.mult).then_inc(rotB_done.sem, 1)

            def kz_of(q, b):
                pool.wait_ge(qk_done.sem, qk_done.now(q, b))
                if b == 0:
                    pool.wait_ge(ru_done.sem, ru_done.before(q, 3))
                else:
                    pool.wait_ge(ru_done.sem, ru_done.now(q, b - 1))
                pool.tensor_tensor(kz[:, :].rearrange("p (h d) -> p h d", h=6),
                                   qk[:, 384:768].rearrange("p (h d) -> p h d", h=6),
                                   zeta.rearrange("p (h a) -> p h a", a=1).to_broadcast([P, 6, HEAD]),
                                   ALU.mult).then_inc(kz_done.sem, 1)

            def decay_state(q, b):
                pool.wait_ge(ro_done.sem, ro_done.now(q, b))
                pool.tensor_tensor(R[:, :], R[:, :], gch[:, :], ALU.mult).then_inc(rg_done.sem, 1)

            def ret_scale(q, b):
                pool.wait_ge(ss6_done.sem, ss6_done.now(q, b))
                pool.tensor_tensor(v6[:, :], ss6[:, :], xi2, ALU.mult).then_inc(v6_done.sem, 1)
                pool.wait_ge(v6_done.sem, v6_done.now(q, 2 * b))
                pool.tensor_tensor(v6[:, :], v6[:, :], epsc[:, 0:6], ALU.add).then_inc(v6_done.sem, 1)
                pool.wait_ge(v6_done.sem, v6_done.now(q, 2 * b + 1))
                pool.tensor_tensor(r6[:, :], v6[:, :], mhalf[:, 0:6], ALU.pow).then_inc(r6_done.sem, 1)
                pool.wait_ge(r6_done.sem, r6_done.now(q, b))
                pool.tensor_tensor(s6[:, :], r6[:, :], xih, ALU.mult).then_inc(s6_done.sem, 1)

            def windows(q, cc):
                if cc == 0:
                    pool.wait_ge(s_done.sem, s_done.now(q, 7))
                    pool.wait_ge(z_evac.sem, z_evac.now(q, T_UP1))
                else:
                    pool.wait_ge(pooled_done.sem, pooled_done.now(q, 1))
                    pool.wait_ge(pool16_done.sem, pool16_done.now(q, 3))
                src, n0 = up[:, cc, :], 1
                for n, step in enumerate((1, 2) if cc == 0 else (1, 2, 4, 8)):
                    dst = win_a if n % 2 == 0 else win_b
                    lo = 2 * step - 1
                    if n:
                        pool.wait_ge(win_done.sem, win_done.now(q, 2 * cc + n - 1))
                    pool.tensor_tensor(dst[:, lo:PADW + QT], src[:, lo:PADW + QT],
                                       src[:, lo - step:PADW + QT - step], ALU.add).then_inc(win_done.sem, 1)
                    src = dst

            with pool.Fori(0, NQ) as q:
                for b in range(NB + 1):
                    if b < NB:
                        inv_rms(q, b)
                    if b:
                        x_lo(q, b - 1)
                    if b < 3:
                        split_lo(q, 2 * b)
                        split_lo(q, 2 * b + 1)
                for k in range(6):
                    split_lo(q, k + 6)
                for i in range(8):
                    if i % 2 == 1:
                        for u in range(3):
                            split_lo(q, 12 + 3 * (i // 2) + u)
                    if i == 5:
                        rot_b(q, 0)
                        kz_of(q, 0)
                split_lo(q, 24)
                windows(q, 0)
                rot_b(q, 1)
                decay_state(q, 0)
                kz_of(q, 1)
                ret_scale(q, 0)
                windows(q, 1)
                rot_b(q, 2)
                decay_state(q, 1)
                kz_of(q, 2)
                ret_scale(q, 1)
                split_lo(q, 25)
                split_lo(q, 26)
                rot_b(q, 3)
                decay_state(q, 2)
                kz_of(q, 3)
                ret_scale(q, 2)
                decay_state(q, 3)
                ret_scale(q, 3)

            def m_split_lo(G, u):
                pool.wait_ge(m_whi.sem, m_whi.now(G, u))
                pool.tensor_tensor(ring_lo[:, u, :], stage[:, u % 2, :], ring_hi[:, u, :].bitcast(F32),
                                   ALU.subtract).then_inc(m_wlo.sem, 1)

            for u in (2, 3):
                pool.wait_ge(m_whi.sem, m_whi.before(0, u))
                pool.tensor_tensor(ring_lo[:, u, :], stage[:, u % 2, :], ring_hi[:, u, :].bitcast(F32),
                                   ALU.subtract).then_inc(m_wlo.sem, 1)

            with pool.Fori(0, NH) as h:
                def m_inv_rms(n, col):
                    pool.wait_ge(m_sq.sem, m_sq.now(h, n))
                    pool.tensor_tensor(var[:, col:col + 1], ssum[:, col:col + 1], epsc[:, 0:1], ALU.add).then_inc(m_var.sem, 1)
                    pool.wait_ge(m_var.sem, m_var.now(h, n))
                    pool.tensor_tensor(rstd[:, col:col + 1], var[:, col:col + 1], mhalf[:, 0:1], ALU.pow).then_inc(m_rstd.sem, 1)

                for b in range(HB + 1):
                    if b < HB:
                        m_inv_rms(b, b)
                    if b:
                        for j in range(2):
                            n = 2 * (b - 1) + j
                            pool.wait_ge(m_xhi.sem, m_xhi.now(h, n))
                            pool.tensor_tensor(h2T_lo[:, 4 * j:4 * j + 4, (b - 1) * P:b * P],
                                               tn2[:, j, :].rearrange("p (c t) -> p c t", c=4),
                                               h2T_hi[:, 4 * j:4 * j + 4, (b - 1) * P:b * P].bitcast(F32),
                                               ALU.subtract).then_inc(m_xlo.sem, 1)
                with pool.Fori(0, NG) as g:
                    for u in range(4):
                        m_split_lo(h * NG + g, u)
                for b in range(HB):
                    m_inv_rms(HB + b, b)

        @block.scalar
        def _(act):
            for e in (sq_done, xhi_done, whi_done, z_evac, v_evac, exp_done, pt_evac, yAhi_done, qkT_evac,
                      osb_done, sqr_done, th_done, yRhi_done, yPhi_done, m_sq, m_xhi, m_relu, m_uhi):
                act.sem_inc(e.sem, e.primed)
            act.sem_inc(m_whi.sem, 2)
            for h in range(NQH):
                act.wait_ge(s_browmm, h + 1)
                act.activation(rrow[:, h, :], bank[h][:, 0:384], ACT.Copy).then_inc(s_brow, 1)
            act.wait_ge(s_pm, 7)
            act.wait_ge(s_rowst, 16)
            act.wait_ge(s_const, 16 * 9)

            def split_hi(q, u):
                act.wait_ge(st_full[u % STAGE].sem, st_full[u % STAGE].now(q, u // STAGE))
                same, owner = slot_owner(u)
                if same:
                    act.wait_ge(tile_done.sem, tile_done.now(q, last_tile_of_unit(owner)))
                    act.wait_ge(wlo_done.sem, wlo_done.now(q, owner))
                else:
                    act.wait_ge(tile_done.sem, tile_done.before(q, last_tile_of_unit(owner)))
                act.activation(ring_hi[:, u % RING, :], stage[:, u % STAGE, :], ACT.Copy).then_inc(whi_done.sem, 1)

            def square_x(q, b):
                act.wait_ge(x_full[b].sem, x_full[b].now(q, 0))
                if b < 2:
                    act.wait_ge(yRlo_done.sem, yRlo_done.before(q, 3))
                    act.wait_ge(ytr_done.sem, ytr_done.before(q, 3))
                else:
                    act.wait_ge(xtr_done.sem, xtr_done.now(q, 2 * (b - 2) + 1))
                act.activation(xn[b % 2], xq[:, b, :], ACT.Square, scale=D ** -0.5, accum_out=ssum[:, b:b + 1]).then_inc(sq_done.sem, 1)

            def x_hi(q, b):
                for j in range(2):
                    n = 2 * b + j
                    act.wait_ge(tn_done.sem, tn_done.now(q, n))
                    if n == 0:
                        act.wait_ge(tile_done.sem, tile_done.before(q, NT - 1))
                    act.activation(hT_hi[:, 4 * j:4 * j + 4, b * P:(b + 1) * P],
                                   tn[j].rearrange("p (c t) -> p c t", c=4), ACT.Copy).then_inc(xhi_done.sem, 1)

            def evac_T(q, t):
                act.wait_ge(tile_done.sem, tile_done.now(q, t))
                src = dense[t % 3][:, :]
                if t < 3:
                    dst = qT[:, t, :]
                elif t == 3:
                    act.wait_ge(carried.sem, carried.now(q, 0))
                    dst = kT[:, P:P + QT]
                elif t == 4:
                    dst = vT[:, :]
                else:
                    act.wait_ge(carried.sem, carried.now(q, 2))
                    dst = up[:, 0 if t == 5 else 1, PADW:PADW + QT]
                act.activation(dst, src, ACT.Copy).then_inc(z_evac.sem, 1)

            def evac_G(q, t):
                act.wait_ge(tile_done.sem, tile_done.now(q, T_GROUP + t))
                g, b = t // 4, t % 4
                act.activation(zt[:, b, 384 * g:384 * g + 384], dense[(T_GROUP + t) % 3][:, 0:384],
                               ACT.Copy).then_inc(z_evac.sem, 1)

            def exps(q, i):
                b, g = i // 2, i % 2
                k = i % 2
                act.wait_ge(nmax_done.sem, nmax_done.now(q, i))
                for h in range(3):
                    act.activation(sc[:, k, 256 * h:256 * h + 256], sc[:, k, 256 * h:256 * h + 256], ACT.Exp,
                                   bias=nmax[:, k, h:h + 1], accum_out=rsum[:, k, h:h + 1]).then_inc(exp_done.sem, 1)
                act.wait_ge(sde_done.sem, sde_done.now(q, i))
                act.activation(ses[:, k, :], sde[:, k, :], ACT.Exp).then_inc(exp_done.sem, 1)

            def evac_pt(q, i):
                k = i % 2
                act.wait_ge(ptr_done.sem, ptr_done.now(q, i))
                if i >= 2:
                    act.wait_ge(o_done.sem, o_done.now(q, i - 2))
                for half in range(2):
                    act.activation(pt[:, k, 384 * half:384 * half + 384], (T0, T1)[half][:, 0:384],
                                   ACT.Copy).then_inc(pt_evac.sem, 1)

            def yA_high(q, i):
                b, g = i // 2, i % 2
                act.wait_ge(o_done.sem, o_done.now(q, i))
                if i == 0:
                    act.wait_ge(tile_done.sem, tile_done.before(q, T_OR - 1))
                a = HEAD * g
                act.activation(yA_hi[a:a + HEAD, :, b * P:(b + 1) * P],
                               OB[a:a + HEAD, 0:384].rearrange("p (c t) -> p c t", c=3), ACT.Copy).then_inc(yAhi_done.sem, 1)

            def evac_qkT(q, b):
                for k in range(2):
                    act.wait_ge(qktr_done.sem, qktr_done.now(q, 2 * b + k))
                    if k == 0:
                        if b == 0:
                            act.wait_ge(ptr_done.sem, ptr_done.now(q, 7))
                        else:
                            act.wait_ge(ro_done.sem, ro_done.now(q, b - 1))
                    act.activation(qkT[:, 384 * k:384 * k + 384], (T0, T1)[k][:, 0:384], ACT.Copy).then_inc(qkT_evac.sem, 1)

            def ret_out(q, b):
                act.wait_ge(ro_done.sem, ro_done.now(q, b))
                if b:
                    act.wait_ge(ya_done.sem, ya_done.now(q, b - 1))
                    act.wait_ge(gate_done.sem, gate_done.now(q, b - 1))
                act.activation(osb[:, :], OB[:, 0:384], ACT.Copy).then_inc(osb_done.sem, 1)
                if b == 0:
                    act.wait_ge(o_done.sem, o_done.now(q, 7))
                act.activation(sq, OB[:, 0:384], ACT.Square).then_inc(sqr_done.sem, 1)
                act.activation(th, zt[:, b, 1152:1536], ACT.Tanh, scale=0.5).then_inc(th_done.sem, 1)

            def yR_high(q, b):
                act.wait_ge(ytr_done.sem, ytr_done.now(q, b))
                act.activation(hT_hi[:, 0:3, b * P:(b + 1) * P], T0[:, 0:384].rearrange("p (c t) -> p c t", c=3),
                               ACT.Copy).then_inc(yRhi_done.sem, 1)

            def yP_high(q, cc):
                act.wait_ge(mix_done.sem, mix_done.now(q, cc))
                act.activation(hT_hi[:, 3 + cc, :], T1[:, :], ACT.Copy, scale=pscale[:, cc:cc + 1]).then_inc(yPhi_done.sem, 1)

            with act.Fori(0, NQ) as q:
                for b in range(NB + 1):
                    if b < NB:
                        square_x(q, b)
                    if b:
                        x_hi(q, b - 1)
                    if b < 3:
                        split_hi(q, 2 * b)
                        split_hi(q, 2 * b + 1)
                for t in range(6):
                    evac_T(q, t)
                    split_hi(q, t + 6)
                act.wait_ge(vtr_done.sem, vtr_done.now(q, 0))
                act.wait_ge(carried.sem, carried.now(q, 1))
                act.activation(vtok[:, 1:NB + 1, :], T0[:, :].rearrange("p (b d) -> p b d", b=NB), ACT.Copy).then_inc(v_evac.sem, 1)
                for i in range(8):
                    exps(q, i)
                    evac_G(q, 2 * i)
                    if i:
                        yA_high(q, i - 1)
                    evac_G(q, 2 * i + 1)
                    evac_pt(q, i)
                    if i % 2 == 1:
                        for u in range(3):
                            split_hi(q, 12 + 3 * (i // 2) + u)
                yA_high(q, 7)
                evac_T(q, T_UP1)
                split_hi(q, 24)
                evac_qkT(q, 0)
                ret_out(q, 0)
                evac_qkT(q, 1)
                yR_high(q, 0)
                ret_out(q, 1)
                evac_qkT(q, 2)
                yP_high(q, 0)
                split_hi(q, 25)
                split_hi(q, 26)
                yP_high(q, 1)
                yR_high(q, 1)
                ret_out(q, 2)
                evac_qkT(q, 3)
                yR_high(q, 2)
                ret_out(q, 3)
                yR_high(q, 3)

            for u in (2, 3):
                act.wait_ge(m_st_full[u % 2].sem, m_st_full[u % 2].before(0, 1))
                if u == 2:
                    act.wait_ge(tile_done.sem, tile_done.now(NQ - 1, NT - 1))
                act.activation(ring_hi[:, u, :], stage[:, u % 2, :], ACT.Copy).then_inc(m_whi.sem, 1)
            with act.Fori(0, NH) as h:
                for b in range(HB + 1):
                    if b < HB:
                        act.wait_ge(m_x_full[b].sem, m_x_full[b].now(h, 0))
                        if b >= 2:
                            act.wait_ge(m_xtr.sem, m_xtr.now(h, 2 * (b - 2) + 1))
                        else:
                            act.wait_ge(m_xtr.sem, m_xtr.before(h, 2 * HB - 1))
                        act.activation(xn2[:, b % 2, :], x2[:, b, :], ACT.Square, scale=D ** -0.5, accum_out=ssum[:, b:b + 1]).then_inc(m_sq.sem, 1)
                    if b:
                        for j in range(2):
                            n = 2 * (b - 1) + j
                            act.wait_ge(m_tn.sem, m_tn.now(h, n))
                            act.activation(h2T_hi[:, 4 * j:4 * j + 4, (b - 1) * P:b * P],
                                           tn2[:, j, :].rearrange("p (c t) -> p c t", c=4), ACT.Copy).then_inc(m_xhi.sem, 1)
                with act.Fori(0, NG) as g:
                    G = h * NG + g

                    def m_split_hi(u):
                        act.wait_ge(m_st_full[u % 2].sem, m_st_full[u % 2].now(G, u // 2))
                        if u < 2:
                            act.wait_ge(m_down.sem, m_down.before(G, 15))
                        else:
                            act.wait_ge(m_up.sem, m_up.now(G, 2 * (u - 2) + 1))
                        act.activation(ring_hi[:, u, :], stage[:, u % 2, :], ACT.Copy).then_inc(m_whi.sem, 1)

                    def up_high(t):
                        act.wait_ge(m_rsq.sem, m_rsq.now(G, t))
                        if t == 0:
                            act.wait_ge(m_down.sem, m_down.before(G, 15))
                        act.activation(u_hi[:, t // 2, 512 * (t % 2):512 * (t % 2) + 512], rsq[:, t % 2, :],
                                       ACT.Copy).then_inc(m_uhi.sem, 1)

                    def up_relu(t):
                        act.wait_ge(m_up.sem, m_up.now(G, t))
                        if t >= 2:
                            act.wait_ge(m_rsq.sem, m_rsq.now(G, t - 2))
                        else:
                            act.wait_ge(m_rsq.sem, m_rsq.before(G, t + 2))
                        act.activation(relu[:, t % 2, :], up_bank[t % 2][:, :], ACT.Relu).then_inc(m_relu.sem, 1)

                    m_split_hi(0)
                    m_split_hi(1)
                    up_relu(0)
                    up_relu(1)
                    up_high(0)
                    m_split_hi(2)
                    up_relu(2)
                    up_high(1)
                    up_relu(3)
                    up_high(2)
                    up_high(3)
                    m_split_hi(3)
                for b in range(HB):
                    act.wait_ge(m_acc.sem, m_acc.now((h + 1) * NG - 1, 2 * b + 1))
                    if b >= 2:
                        act.wait_ge(m_sq.sem, m_sq.now(h, HB + b - 2))
                    act.activation(xn2[:, b % 2, :], x2[:, b, :], ACT.Square, scale=D ** -0.5, accum_out=ssum[:, b:b + 1]).then_inc(m_sq.sem, 1)

        @block.vector
        def _(dve):
            for e in (carried, xn_done, tn_done, x2_evac, sc_done, max_done, nmax_done, sde_done, den_done, rinv_done, pn_done,
                      yAlo_done, rotA_done, qk_done, pm_done, R_done, ss6_done, gate_done, ya_done, y_done, yRlo_done,
                      pooled_done, pool16_done, yPlo_done, m_xn, m_tn, m_rsq, m_ulo, m_acc, m_fin):
                dve.sem_inc(e.sem, e.primed)
            dve.wait_ge(s_rel, 32)
            dve.tensor_copy(relw, relb.rearrange("p (h a) -> p h a", a=1).to_broadcast([NBUCKET + 1, NQH, P])).then_inc(s_relw, 1)
            dve.wait_ge(s_const, 16 * 9)
            dve.wait_ge(s_pm, 7)
            dve.wait_ge(s_ident, 80)
            dve.tensor_scalar(nsink[:, :], sinkb[:, :], -1.0, None, ALU.mult).then_inc(s_relw, 1)
            dve.wait_ge(s_relw, 2)

            def x_norm(q, b):
                dve.wait_ge(rstd_done.sem, rstd_done.now(q, b))
                dve.tensor_scalar(xn[b % 2], xq[:, b, :], rstd[:, b:b + 1], None, ALU.mult).then_inc(xn_done.sem, 1)

            def x_gain(q, b):
                for j in range(2):
                    n = 2 * b + j
                    dve.wait_ge(xtr_done.sem, xtr_done.now(q, n))
                    if b:
                        dve.wait_ge(xlo_done.sem, xlo_done.now(q, n - 2))
                    g4 = gmix_sb[:, 4 * j:4 * j + 4].rearrange("p (c a) -> p c a", a=1).to_broadcast([P, 4, P])
                    dve.tensor_tensor(tn[j].rearrange("p (c t) -> p c t", c=4),
                                      (T0, T1)[j][:, :].rearrange("p (c t) -> p c t", c=4), g4, ALU.mult).then_inc(tn_done.sem, 1)

            def scores(q, i):
                b, g, k = i // 2, i % 2, i % 2
                src = bias0 if b == 0 else bias
                dve.wait_ge(s_done.sem, s_done.now(q, i))
                if i == 0:
                    dve.wait_ge(xlo_done.sem, xlo_done.now(q, 7))
                elif i >= 2:
                    dve.wait_ge(ptr_done.sem, ptr_done.now(q, i - 2))
                bv = src[:, 3 * g:3 * g + 3, :].rearrange("p h m -> p (h m)")
                dve.scalar_tensor_tensor(out=sc[:, k, 0:512], in0=S0[:, :], scalar=SCALE, in1=bv[:, 0:512],
                                         op0=ALU.mult, op1=ALU.add).then_inc(sc_done.sem, 1)
                dve.scalar_tensor_tensor(out=sc[:, k, 512:768], in0=S1[:, 0:256], scalar=SCALE, in1=bv[:, 512:768],
                                         op0=ALU.mult, op1=ALU.add).then_inc(sc_done.sem, 1)
                dve.wait_ge(sc_done.sem, sc_done.now(q, 2 * i + 1))
                dve.tensor_reduce(rmax[:, k, :], sc[:, k, :].rearrange("p (h m) -> p h m", h=3), AX, ALU.max).then_inc(max_done.sem, 1)
                dve.wait_ge(max_done.sem, max_done.now(q, i))
                dve.scalar_tensor_tensor(out=nmax[:, k, :], in0=rmax[:, k, :], scalar=-1.0, in1=nsink[:, 3 * g:3 * g + 3],
                                         op0=ALU.mult, op1=ALU.min).then_inc(nmax_done.sem, 1)
                dve.wait_ge(nmax_done.sem, nmax_done.now(q, i))
                dve.tensor_tensor(sde[:, k, :], nmax[:, k, :], sinkb[:, 3 * g:3 * g + 3], ALU.add).then_inc(sde_done.sem, 1)

            def softmax(q, i):
                k = i % 2
                dve.wait_ge(exp_done.sem, exp_done.now(q, 4 * i + 3))
                dve.tensor_tensor(rsum[:, k, :], rsum[:, k, :], ses[:, k, :], ALU.add).then_inc(den_done.sem, 1)
                dve.wait_ge(den_done.sem, den_done.now(q, i))
                dve.reciprocal(rinv[:, k, :], rsum[:, k, :]).then_inc(rinv_done.sem, 1)
                dve.wait_ge(rinv_done.sem, rinv_done.now(q, i))
                for h in range(3):
                    v = sc[:, k, 256 * h:256 * h + 256]
                    dve.tensor_scalar(v, v, rinv[:, k, h:h + 1], None, ALU.mult).then_inc(pn_done.sem, 1)

            def yA_low(q, i):
                b, a = i // 2, HEAD * (i % 2)
                dve.wait_ge(yAhi_done.sem, yAhi_done.now(q, i))
                dve.tensor_tensor(yA_lo[a:a + HEAD, :, b * P:(b + 1) * P],
                                  OB[a:a + HEAD, 0:384].rearrange("p (c t) -> p c t", c=3),
                                  yA_hi[a:a + HEAD, :, b * P:(b + 1) * P].bitcast(F32), ALU.subtract).then_inc(yAlo_done.sem, 1)

            def rot_a(q, b):
                if b == 0:
                    dve.wait_ge(z_evac.sem, z_evac.now(q, T_GROUP + 7))
                    dve.wait_ge(tab_full.sem, tab_full.now(q, 0))
                dve.tensor_tensor(rotA[:, :].rearrange("p (h d) -> p h d", h=12),
                                  zt[:, b, 0:768].rearrange("p (h d) -> p h d", h=12),
                                  cos_of(b).rearrange("p (a d) -> p a d", a=1).to_broadcast([P, 12, HEAD]),
                                  ALU.mult).then_inc(rotA_done.sem, 1)

            def rot_add(q, b):
                dve.wait_ge(rotA_done.sem, rotA_done.now(q, b))
                dve.wait_ge(rotB_done.sem, rotB_done.now(q, 2 * b + 1))
                dve.tensor_tensor(qk[:, :], qk[:, :], rotA[:, :], ALU.add).then_inc(qk_done.sem, 1)

            def decay_scores(q, b):
                for k in range(2):
                    dve.wait_ge(rs_done.sem, rs_done.now(q, 2 * b + k))
                    if b and k == 0:
                        dve.wait_ge(ro_done.sem, ro_done.now(q, b - 1))
                    dve.tensor_tensor(Pm[:, 384 * k:384 * k + 384], (S0, S1)[k][:, 0:384],
                                      cmask[:, 384 * k:384 * k + 384], ALU.mult).then_inc(pm_done.sem, 1)

            def state(q, b):
                dve.wait_ge(ru_done.sem, ru_done.now(q, b))
                dve.wait_ge(rg_done.sem, rg_done.now(q, b))
                for k in range(2):
                    a = HEAD * k
                    rv = R[a:a + HEAD, :].rearrange("p (c two d) -> p c two d", c=3, two=2)[:, :, k, :]
                    uv = S0[a:a + HEAD, 0:384].rearrange("p (c two d) -> p c two d", c=3, two=2)[:, :, k, :]
                    dve.tensor_tensor(rv, uv, rv, ALU.add).then_inc(R_done.sem, 1)

            def ret_sums(q, b):
                dve.wait_ge(sqr_done.sem, sqr_done.now(q, b))
                dve.tensor_reduce(ss6[:, :], sq.rearrange("p (h d) -> p h d", h=6), AX, ALU.add).then_inc(ss6_done.sem, 1)

            def ret_y(q, b):
                dve.wait_ge(th_done.sem, th_done.now(q, b))
                if b:
                    dve.wait_ge(y_done.sem, y_done.now(q, b - 1))
                dve.scalar_tensor_tensor(out=gate, in0=th, scalar=1.0, in1=zt[:, b, 1152:1536],
                                         op0=ALU.add, op1=ALU.mult).then_inc(gate_done.sem, 1)
                dve.wait_ge(s6_done.sem, s6_done.now(q, b))
                dve.wait_ge(osb_done.sem, osb_done.now(q, b))
                if b:
                    dve.wait_ge(ytr_done.sem, ytr_done.now(q, b - 1))
                dve.tensor_tensor(yv.rearrange("p (h d) -> p h d", h=6), osb[:, :].rearrange("p (h d) -> p h d", h=6),
                                  s6[:, :].rearrange("p (h a) -> p h a", a=1).to_broadcast([P, 6, HEAD]),
                                  ALU.mult).then_inc(ya_done.sem, 1)
                dve.wait_ge(ya_done.sem, ya_done.now(q, b))
                dve.wait_ge(gate_done.sem, gate_done.now(q, b))
                dve.tensor_tensor(yv, yv, gate, ALU.mult).then_inc(y_done.sem, 1)

            def yR_low(q, b):
                dve.wait_ge(yRhi_done.sem, yRhi_done.now(q, b))
                dve.tensor_tensor(hT_lo[:, 0:3, b * P:(b + 1) * P], T0[:, 0:384].rearrange("p (c t) -> p c t", c=3),
                                  hT_hi[:, 0:3, b * P:(b + 1) * P].bitcast(F32), ALU.subtract).then_inc(yRlo_done.sem, 1)

            def pool_first(q, cc):
                if cc == 0:
                    dve.wait_ge(tab_full.sem, tab_full.now(q, 0))
                    dve.wait_ge(mix_done.sem, mix_done.before(q, 1))
                else:
                    dve.wait_ge(mix_done.sem, mix_done.now(q, 0))
                for k in range(2):
                    a = HEAD * k
                    dve.wait_ge(win_done.sem, win_done.now(q, (0, 1, 4, 5)[2 * cc + k]))
                    w = (win_a, win_b)[k]
                    dve.tensor_tensor(p16[a:a + HEAD, :], w[a:a + HEAD, PADW:2 * PADW], icnt_of(cc)[a:a + HEAD, :],
                                       ALU.mult).then_inc(pool16_done.sem, 1)
                    dve.wait_ge(pool16_done.sem, pool16_done.now(q, 4 * cc + 2 * k))
                    dve.tensor_tensor(pooled[a:a + HEAD, 0:PADW], p16[a:a + HEAD, :], up[a:a + HEAD, cc, PADW:2 * PADW],
                                       ALU.subtract).then_inc(pool16_done.sem, 1)

            def pool_rest(q, cc):
                if cc == 0:
                    dve.wait_ge(mix_done.sem, mix_done.before(q, 1))
                else:
                    dve.wait_ge(mix_done.sem, mix_done.now(q, 0))
                for k in range(2):
                    a = HEAD * k
                    dve.wait_ge(win_done.sem, win_done.now(q, (0, 1, 4, 5)[2 * cc + k]))
                    w = (win_a, win_b)[k]
                    dve.scalar_tensor_tensor(out=pooled[a:a + HEAD, PADW:QT], in0=w[a:a + HEAD, 2 * PADW:PADW + QT],
                                             scalar=invw[a:a + HEAD, cc:cc + 1], in1=up[a:a + HEAD, cc, 2 * PADW:PADW + QT],
                                             op0=ALU.mult, op1=ALU.subtract).then_inc(pooled_done.sem, 1)

            def yP_low(q, cc):
                dve.wait_ge(yPhi_done.sem, yPhi_done.now(q, cc))
                dve.scalar_tensor_tensor(out=hT_lo[:, 3 + cc, :], in0=T1[:, :], scalar=pscale[:, cc:cc + 1],
                                         in1=hT_hi[:, 3 + cc, :].bitcast(F32), op0=ALU.mult, op1=ALU.subtract).then_inc(yPlo_done.sem, 1)

            def evac_x2(q, n):
                b, half = (n % 8) // 2, n % 2
                dve.wait_ge(tile_done.sem, tile_done.now(q, T_OA + n))
                if n >= 8:
                    dve.wait_ge(x2_evac.sem, x2_evac.now(q, n - 8))
                v = xq[:, b, 512 * half:512 * half + 512]
                dve.tensor_tensor(v, dense[(T_OA + n) % 3][:, :], v, ALU.add).then_inc(x2_evac.sem, 1)

            with dve.Fori(0, NQ) as q:
                dve.wait_ge(o_done.sem, o_done.before(q, 7))
                dve.wait_ge(pool16_done.sem, pool16_done.before(q, 7))
                dve.wait_ge(z_evac.sem, z_evac.before(q, T_UP1))
                dve.wait_ge(v_evac.sem, v_evac.before(q, 0))
                dve.tensor_copy(kT[:, 0:P], kT[:, QT:QT + P]).then_inc(carried.sem, 1)
                dve.tensor_copy(vtok[:, 0, :], vtok[:, NB, :]).then_inc(carried.sem, 1)
                dve.tensor_copy(up[:, :, 0:PADW], up[:, :, QT:QT + PADW]).then_inc(carried.sem, 1)
                for b in range(NB + 1):
                    if b < NB:
                        x_norm(q, b)
                    if b:
                        x_gain(q, b - 1)
                for i in range(8):
                    scores(q, i)
                    softmax(q, i)
                    if i == 1:
                        dve.wait_ge(sc_done.sem, sc_done.now(q, 3))
                        dve.tensor_copy(bias0[:, :, 0:P], bias[:, :, 0:P]).then_inc(carried.sem, 1)
                    if i:
                        yA_low(q, i - 1)
                    if i == 5:
                        rot_a(q, 0)
                        rot_add(q, 0)
                yA_low(q, 7)
                evac_x2(q, 0)
                rot_a(q, 1)
                evac_x2(q, 1)
                decay_scores(q, 0)
                pool_first(q, 0)
                pool_rest(q, 0)
                rot_add(q, 1)
                evac_x2(q, 2)
                state(q, 0)
                ret_sums(q, 0)
                ret_y(q, 0)
                evac_x2(q, 3)
                evac_x2(q, 4)
                rot_a(q, 2)
                decay_scores(q, 1)
                yR_low(q, 0)
                rot_add(q, 2)
                evac_x2(q, 5)
                state(q, 1)
                ret_sums(q, 1)
                ret_y(q, 1)
                evac_x2(q, 6)
                yP_low(q, 0)
                pool_first(q, 1)
                pool_rest(q, 1)
                evac_x2(q, 7)
                rot_a(q, 3)
                decay_scores(q, 2)
                yP_low(q, 1)
                yR_low(q, 1)
                rot_add(q, 3)
                evac_x2(q, 8)
                state(q, 2)
                ret_sums(q, 2)
                ret_y(q, 2)
                evac_x2(q, 9)
                decay_scores(q, 3)
                yR_low(q, 2)
                evac_x2(q, 10)
                state(q, 3)
                ret_sums(q, 3)
                ret_y(q, 3)
                evac_x2(q, 11)
                evac_x2(q, 12)
                yR_low(q, 3)
                for n in range(13, 16):
                    evac_x2(q, n)

            with dve.Fori(0, NH) as h:
                for b in range(HB + 1):
                    if b < HB:
                        dve.wait_ge(m_rstd.sem, m_rstd.now(h, b))
                        dve.tensor_scalar(xn2[:, b % 2, :], x2[:, b, :], rstd[:, b:b + 1], None, ALU.mult).then_inc(m_xn.sem, 1)
                    if b:
                        for j in range(2):
                            n = 2 * (b - 1) + j
                            dve.wait_ge(m_xtr.sem, m_xtr.now(h, n))
                            if n >= 2:
                                dve.wait_ge(m_xlo.sem, m_xlo.now(h, n - 2))
                            g4 = gmlp_sb[:, 4 * j:4 * j + 4].rearrange("p (c a) -> p c a", a=1).to_broadcast([P, 4, P])
                            dve.tensor_tensor(tn2[:, j, :].rearrange("p (c t) -> p c t", c=4),
                                              (T0, T1)[j][:, :].rearrange("p (c t) -> p c t", c=4), g4, ALU.mult).then_inc(m_tn.sem, 1)
                with dve.Fori(0, NG) as g:
                    G = h * NG + g

                    def square(t):
                        dve.wait_ge(m_relu.sem, m_relu.now(G, t))
                        if t >= 2:
                            dve.wait_ge(m_ulo.sem, m_ulo.now(G, t - 2))
                        else:
                            dve.wait_ge(m_ulo.sem, m_ulo.before(G, t + 2))
                        dve.tensor_tensor(rsq[:, t % 2, :], relu[:, t % 2, :], relu[:, t % 2, :], ALU.mult).then_inc(m_rsq.sem, 1)

                    def up_low(t):
                        dve.wait_ge(m_uhi.sem, m_uhi.now(G, t))
                        cols = slice(512 * (t % 2), 512 * (t % 2) + 512)
                        dve.tensor_tensor(u_lo[:, t // 2, cols], rsq[:, t % 2, :], u_hi[:, t // 2, cols].bitcast(F32),
                                          ALU.subtract).then_inc(m_ulo.sem, 1)

                    square(0)
                    square(1)
                    up_low(0)
                    square(2)
                    up_low(1)
                    square(3)
                    up_low(2)
                    up_low(3)
                    for n in range(16):
                        dve.wait_ge(m_down.sem, m_down.now(G, n))
                        v = x2[:, n // 2, 512 * (n % 2):512 * (n % 2) + 512]
                        dve.wait_ge(m_acc.sem, m_acc.before(G, n))
                        dve.tensor_tensor(v, down_bank[n % 4][:, :], v, ALU.add).then_inc(m_acc.sem, 1)
                dve.wait_ge(fg_full, 16)
                for b in range(HB):
                    dve.wait_ge(m_rstd.sem, m_rstd.now(h, HB + b))
                    dve.scalar_tensor_tensor(out=x2[:, b, :], in0=x2[:, b, :], scalar=rstd[:, b:b + 1], in1=fg[:, :],
                                             op0=ALU.mult, op1=ALU.mult).then_inc(m_fin.sem, 1)

        @block.tensor
        def _(pe):
            for e in (xtr_done, tile_done, vtr_done, s_done, ptr_done, o_done, qktr_done, rs_done, ro_done, ru_done,
                      ytr_done, mix_done, m_xtr, m_up, m_down):
                pe.sem_inc(e.sem, e.primed)
            pe.wait_ge(s_rel, 32)
            pe.wait_ge(s_relw, 1)
            for h in range(NQH):
                pe.matmul(bank[h][:, 0:384], relw[:, h, :], oneh, start=True, stop=True).then_inc(s_browmm, 1)
            pe.wait_ge(s_ident, 80)
            pe.wait_ge(s_const, 16 * 9)
            pe.wait_ge(s_pm, 7)
            pe.wait_ge(s_brow, NQH)

            def three(dst, pairs):
                n = len(pairs)
                for k, (ah, al, bh, bl) in enumerate(pairs):
                    pe.matmul(dst, al, bh, start=(k == 0), stop=False)
                    pe.matmul(dst, ah, bl, start=False, stop=False)
                    last = pe.matmul(dst, ah, bh, start=False, stop=(k == n - 1))
                return last

            def free_bank(q, t):
                back = t - 3 if t >= 3 else t - 3 + NT
                ev, k = (z_evac, back) if back < T_OA else (x2_evac, back - T_OA)
                if t >= 3:
                    pe.wait_ge(ev.sem, ev.now(q, k))
                else:
                    pe.wait_ge(ev.sem, ev.before(q, k))

            def norm_transposes(q, b):
                pe.wait_ge(xn_done.sem, xn_done.now(q, b))
                for j in range(2):
                    n = 2 * b + j
                    if n >= 2:
                        pe.wait_ge(tn_done.sem, tn_done.now(q, n - 2))
                    elif j == 0:
                        pe.wait_ge(yRlo_done.sem, yRlo_done.before(q, 3))
                    else:
                        pe.wait_ge(qkT_evac.sem, qkT_evac.before(q, 7))
                    for c in range(4):
                        last = pe.transpose((T0, T1)[j][:, c * P:(c + 1) * P], xn[b % 2][:, (4 * j + c) * P:(4 * j + c + 1) * P], ident[:, :])
                    last.then_inc(xtr_done.sem, 1)

            def proj_T(q, t):
                u = t if t < 6 else 18
                s = u % RING
                pe.wait_ge(wlo_done.sem, wlo_done.now(q, u))
                free_bank(q, t)
                wh = ring_hi[:, s, :].rearrange("p (c n) -> p c n", c=C)
                wl = ring_lo[:, s, :].rearrange("p (c n) -> p c n", c=C)
                three(dense[t % 3][:, :], [(wh[:, c, :], wl[:, c, :], hT_hi[:, c, :], hT_lo[:, c, :]) for c in range(C)]
                      ).then_inc(tile_done.sem, 1)

            def proj_G(q, t):
                g, b = t // 4, t % 4
                s = 3 * (g % 2)
                if b == 0:
                    pe.wait_ge(wlo_done.sem, wlo_done.now(q, 6 + 3 * g + 2))
                free_bank(q, T_GROUP + t)
                wh = ring_hi[:, s:s + 3, :].rearrange("p s (c n) -> p c s n", c=C)
                wl = ring_lo[:, s:s + 3, :].rearrange("p s (c n) -> p c s n", c=C)
                tok = slice(b * P, (b + 1) * P)
                three(dense[(T_GROUP + t) % 3][:, 0:384].rearrange("p (s n) -> p s n", s=3),
                      [(hT_hi[:, c, tok], hT_lo[:, c, tok], wh[:, c], wl[:, c]) for c in range(C)]).then_inc(tile_done.sem, 1)

            def out_tile(q, n):
                b, half = (n % 8) // 2, n % 2
                tok, cols = slice(b * P, (b + 1) * P), slice(512 * half, 512 * half + 512)
                if n < 8:
                    pe.wait_ge(yAlo_done.sem, yAlo_done.now(q, 2 * b + 1))
                    srcs = [(yA_hi[:, m, tok], yA_lo[:, m, tok], 19 + m) for m in range(3)]
                else:
                    pe.wait_ge(yRlo_done.sem, yRlo_done.now(q, b))
                    pe.wait_ge(yPlo_done.sem, yPlo_done.now(q, 1))
                    srcs = [(hT_hi[:, m, tok], hT_lo[:, m, tok], 22 + m) for m in range(5)]
                pe.wait_ge(wlo_done.sem, wlo_done.now(q, srcs[-1][2]))
                free_bank(q, T_OA + n)
                three(dense[(T_OA + n) % 3][:, :],
                      [(ah, al, ring_hi[:, u % RING, cols], ring_lo[:, u % RING, cols]) for ah, al, u in srcs]
                      ).then_inc(tile_done.sem, 1)

            def att_scores(q, i):
                b, g = i // 2, i % 2
                a = HEAD * g
                if i == 0:
                    pe.wait_ge(z_evac.sem, z_evac.now(q, 3))
                    pe.wait_ge(pm_done.sem, pm_done.before(q, 7))
                    pe.wait_ge(R_done.sem, R_done.before(q, 7))
                else:
                    pe.wait_ge(sc_done.sem, sc_done.now(q, 2 * i - 1))
                for h in range(3):
                    dst = S0[:, 256 * h:256 * h + 256] if h < 2 else S1[:, 0:256]
                    last = pe.matmul(dst, qT[a:a + HEAD, h, b * P:(b + 1) * P], kT[a:a + HEAD, b * P:(b + 2) * P],
                                     start=True, stop=True)
                last.then_inc(s_done.sem, 1)

            def att_transposes(q, i):
                k = i % 2
                pe.wait_ge(pn_done.sem, pn_done.now(q, 3 * i + 2))
                if i == 0:
                    pe.wait_ge(v_evac.sem, v_evac.now(q, 0))
                    pe.wait_ge(tn_done.sem, tn_done.now(q, 7))
                else:
                    pe.wait_ge(pt_evac.sem, pt_evac.now(q, 2 * i - 1))
                for half in range(2):
                    for h in range(3):
                        last = pe.transpose((T0, T1)[half][:, h * P:(h + 1) * P],
                                            sc[:, k, 256 * h + P * half:256 * h + P * half + P], ident[:, :])
                last.then_inc(ptr_done.sem, 1)

            def att_out(q, i):
                b, k = i // 2, i % 2
                pe.wait_ge(pt_evac.sem, pt_evac.now(q, 2 * i + 1))
                if i:
                    pe.wait_ge(yAlo_done.sem, yAlo_done.now(q, i - 1))
                else:
                    pe.wait_ge(sqr_done.sem, sqr_done.before(q, 3))
                    pe.wait_ge(osb_done.sem, osb_done.before(q, 3))
                    pe.wait_ge(v_evac.sem, v_evac.now(q, 0))
                for half in range(2):
                    last = pe.matmul(OB[:, 0:384], vtok[:, b + half, :], pt[:, k, 384 * half:384 * half + 384],
                                     start=(half == 0), stop=(half == 1))
                last.then_inc(o_done.sem, 1)

            def qk_transposes(q, b):
                pe.wait_ge(qk_done.sem, qk_done.now(q, b))
                if b == 0:
                    pe.wait_ge(pt_evac.sem, pt_evac.now(q, 15))
                elif b == 1:
                    pe.wait_ge(qkT_evac.sem, qkT_evac.now(q, 1))
                else:
                    pe.wait_ge(yRlo_done.sem, yRlo_done.now(q, b - 2))
                    if b == 3:
                        pe.wait_ge(yPlo_done.sem, yPlo_done.now(q, 1))
                    else:
                        pe.wait_ge(qkT_evac.sem, qkT_evac.now(q, 3))
                for k in range(2):
                    for c in range(3):
                        last = pe.transpose((T0, T1)[k][:, c * P:(c + 1) * P], qk[:, 384 * k + c * P:384 * k + (c + 1) * P], ident[:, :])
                    last.then_inc(qktr_done.sem, 1)

            def ret_scores(q, b):
                pe.wait_ge(qkT_evac.sem, qkT_evac.now(q, 2 * b + 1))
                if b:
                    pe.wait_ge(R_done.sem, R_done.now(q, 2 * b - 1))
                    pe.wait_ge(pm_done.sem, pm_done.now(q, 2 * b - 1))
                else:
                    pe.wait_ge(sc_done.sem, sc_done.now(q, 15))
                for h in range(6):
                    a, c = HEAD * (h % 2), h // 2
                    last = pe.matmul((S0, S1)[h % 2][:, P * c:P * c + P],
                                     qkT[a:a + HEAD, 384 + c * P:384 + (c + 1) * P], qkT[a:a + HEAD, c * P:(c + 1) * P],
                                     start=True, stop=True)
                    if c == 2:
                        last.then_inc(rs_done.sem, 1)

            def ret_outs(q, b):
                pe.wait_ge(pm_done.sem, pm_done.now(q, 2 * b + 1))
                if b:
                    pe.wait_ge(R_done.sem, R_done.now(q, 2 * b - 1))
                    pe.wait_ge(sqr_done.sem, sqr_done.now(q, b - 1))
                else:
                    pe.wait_ge(R_done.sem, R_done.before(q, 7))
                    pe.wait_ge(yAlo_done.sem, yAlo_done.now(q, 7))
                for c in range(3):
                    for h in (2 * c, 2 * c + 1):
                        pe.matmul(OB[:, h * HEAD:(h + 1) * HEAD], Pm[:, (3 * (h % 2) + c) * P:(3 * (h % 2) + c + 1) * P],
                                         zt[:, b, 768 + h * HEAD:768 + (h + 1) * HEAD], start=(h % 2 == 0), stop=False,
                                  skip_group_check=True)
                    last = pe.matmul(OB[:, c * P:(c + 1) * P], qkT[:, c * P:(c + 1) * P], R[:, c * P:(c + 1) * P],
                                     start=False, stop=True, skip_group_check=True)
                last.then_inc(ro_done.sem, 1)
                pe.wait_ge(kz_done.sem, kz_done.now(q, b))
                for c in range(3):
                    last = pe.matmul(S0[:, c * P:(c + 1) * P], kz[:, c * P:(c + 1) * P],
                                     zt[:, b, 768 + c * P:768 + (c + 1) * P], start=True, stop=True)
                last.then_inc(ru_done.sem, 1)

            def y_transposes(q, b):
                pe.wait_ge(y_done.sem, y_done.now(q, b))
                pe.wait_ge(qkT_evac.sem, qkT_evac.now(q, 2 * min(b + 1, 3) + 1))
                if b == 3:
                    pe.wait_ge(yRlo_done.sem, yRlo_done.now(q, 2))
                for c in range(3):
                    last = pe.transpose(T0[:, c * P:(c + 1) * P], yv[:, c * P:(c + 1) * P], ident[:, :])
                last.then_inc(ytr_done.sem, 1)

            def pool_mix(q, cc):
                pe.wait_ge(pooled_done.sem, pooled_done.now(q, 2 * cc + 1))
                pe.wait_ge(pool16_done.sem, pool16_done.now(q, 4 * cc + 3))
                if cc == 0:
                    pe.wait_ge(qkT_evac.sem, qkT_evac.now(q, 5))
                else:
                    pe.wait_ge(yPlo_done.sem, yPlo_done.now(q, 0))
                pe.matmul(T1[:, :], poolw[:, cc, :], pooled[:, :], start=True, stop=True).then_inc(mix_done.sem, 1)

            with pe.Fori(0, NQ) as q:
                for b in range(NB):
                    norm_transposes(q, b)
                pe.wait_ge(xlo_done.sem, xlo_done.now(q, 7))
                for t in range(6):
                    proj_T(q, t)
                pe.wait_ge(z_evac.sem, z_evac.now(q, 4))
                pe.wait_ge(tn_done.sem, tn_done.now(q, 7))
                for b in range(NB):
                    last = pe.transpose(T0[:, b * P:(b + 1) * P], vT[:, b * P:(b + 1) * P], ident[:, :])
                last.then_inc(vtr_done.sem, 1)
                for i in range(8):
                    att_scores(q, i)
                    proj_G(q, 2 * i)
                    if i:
                        att_out(q, i - 1)
                    proj_G(q, 2 * i + 1)
                    att_transposes(q, i)
                proj_T(q, T_UP1)
                att_out(q, 7)
                qk_transposes(q, 0)
                out_tile(q, 0)
                out_tile(q, 1)
                ret_scores(q, 0)
                out_tile(q, 2)
                ret_outs(q, 0)
                qk_transposes(q, 1)
                out_tile(q, 3)
                out_tile(q, 4)
                ret_scores(q, 1)
                y_transposes(q, 0)
                out_tile(q, 5)
                ret_outs(q, 1)
                qk_transposes(q, 2)
                out_tile(q, 6)
                pool_mix(q, 0)
                out_tile(q, 7)
                ret_scores(q, 2)
                pool_mix(q, 1)
                y_transposes(q, 1)
                out_tile(q, 8)
                ret_outs(q, 2)
                qk_transposes(q, 3)
                out_tile(q, 9)
                ret_scores(q, 3)
                y_transposes(q, 2)
                out_tile(q, 10)
                ret_outs(q, 3)
                out_tile(q, 11)
                out_tile(q, 12)
                y_transposes(q, 3)
                for n in range(13, 16):
                    out_tile(q, n)

            with pe.Fori(0, NH) as h:
                for b in range(HB):
                    pe.wait_ge(m_xn.sem, m_xn.now(h, b))
                    for j in range(2):
                        n = 2 * b + j
                        if n >= 2:
                            pe.wait_ge(m_tn.sem, m_tn.now(h, n - 2))
                        else:
                            pe.wait_ge(m_relu.sem, m_relu.before(h * NG, 2 + j))
                        for c in range(4):
                            last = pe.transpose((T0, T1)[j][:, c * P:(c + 1) * P], xn2[:, b % 2, (4 * j + c) * P:(4 * j + c + 1) * P], ident[:, :])
                        last.then_inc(m_xtr.sem, 1)
                with pe.Fori(0, NG) as g:
                    G = h * NG + g
                    pe.wait_ge(m_xlo.sem, m_xlo.now(h, 2 * HB - 1))
                    for t in range(4):
                        if t >= 2:
                            pe.wait_ge(m_relu.sem, m_relu.now(G, t - 2))
                        else:
                            pe.wait_ge(m_relu.sem, m_relu.before(G, t + 2))
                        if t % 2 == 0:
                            pe.wait_ge(m_wlo.sem, m_wlo.before(G, 2 + t // 2))
                        cols = slice(512 * (t % 2), 512 * (t % 2) + 512)
                        s = 2 + t // 2
                        wh = ring_hi[:, s, :].rearrange("p (c n) -> p c n", c=C)
                        wl = ring_lo[:, s, :].rearrange("p (c n) -> p c n", c=C)
                        three(up_bank[t % 2][:, :], [(wh[:, c, :], wl[:, c, :], h2T_hi[:, c, cols], h2T_lo[:, c, cols])
                                                     for c in range(C)]).then_inc(m_up.sem, 1)
                    for n in range(16):
                        b, cols = n // 2, slice(512 * (n % 2), 512 * (n % 2) + 512)
                        tok = slice(b * P, (b + 1) * P)
                        if n == 0:
                            pe.wait_ge(m_ulo.sem, m_ulo.now(G, 2))
                            pe.wait_ge(m_wlo.sem, m_wlo.now(G, 1))
                        if n == 8:
                            pe.wait_ge(m_ulo.sem, m_ulo.now(G, 3))
                        if n >= 4:
                            pe.wait_ge(m_acc.sem, m_acc.now(G, n - 4))
                        else:
                            pe.wait_ge(m_acc.sem, m_acc.before(G, n + 12))
                        three(down_bank[n % 4][:, :], [(u_hi[:, k, tok], u_lo[:, k, tok], ring_hi[:, k, cols], ring_lo[:, k, cols])
                                                       for k in range(2)]).then_inc(m_down.sem, 1)


def shape_constants():
    f8 = np.float64
    gamma = 1.0 - 2.0 ** (-5.0 - np.arange(NRET, dtype=f8))
    idx = np.arange(P, dtype=f8)
    c = np.zeros((P, CSTW), np.float32)

    def put(name, v):
        c[:, CST[name][0]:CST[name][1]] = v
    put("ident", np.eye(P))
    mask = np.where(idx[None, None, :] >= idx[:, None, None], gamma[None, :, None] ** -(idx[:, None, None] + 1) * SCALE, 0.0)
    put("mask", np.concatenate([mask[:, 0::2], mask[:, 1::2]], axis=1).reshape(P, -1))
    head = 2 * np.arange(3)[None, :] + (np.arange(P) >= HEAD)[:, None]
    put("gchunk", np.repeat(gamma[head] ** P, P, axis=1))
    put("zeta", SCALE * gamma[None, :] ** (P - 1 - idx[:, None]))
    xi = gamma[None, :] ** (idx[:, None] + 1)
    put("xi2", xi * xi / HEAD)
    put("xih", 0.5 * xi)
    w = np.array(WINDOWS, f8).reshape(2, 2)
    put("invw", np.repeat(1.0 / w.T, HEAD, axis=0))
    put("mhalf", -0.5)
    put("eps", EPS)

    inv = (np.float32(1.0) / (np.float32(10000.0) ** np.linspace(0.0, 1.0, HEAD // 2, dtype=np.float32))).astype(np.float32)
    ang = (np.arange(SEQ, dtype=np.float32)[:, None] * inv[None, :]).astype(f8)
    cos = np.repeat(np.cos(ang), 2, axis=1)
    sin = np.stack([-np.sin(ang), np.sin(ang)], axis=-1).reshape(SEQ, HEAD)
    t = np.zeros((NQ, P, TABW), np.float32)
    t[:, :, 0:NB * HEAD] = cos.reshape(NQ, NB, P, HEAD).transpose(0, 2, 1, 3).reshape(NQ, P, -1)
    t[:, :, NB * HEAD:2 * NB * HEAD] = sin.reshape(NQ, NB, P, HEAD).transpose(0, 2, 1, 3).reshape(NQ, P, -1)
    wp = np.repeat(w, HEAD, axis=1)
    for q in range(NQ):
        cnt = np.minimum(np.arange(PADW)[None, None, :] + 1 + q * QT, wp[:, :, None])
        t[q, :, 2 * NB * HEAD:] = (1.0 / cnt).transpose(1, 0, 2).reshape(P, 32)

    dist = P - (np.arange(384) - (P - 1))
    ok = (dist >= 0) & (dist < P)
    half = NBUCKET // 2
    n = np.maximum(dist, 0)
    large = half + (np.log(np.maximum(n, 1) / half) / np.log(MAXDIST / half) * (NBUCKET - half)).astype(np.int64)
    bucket = np.where(n < half, n, np.minimum(large, NBUCKET - 1))
    one = np.zeros((NBUCKET + 1, 384), np.float32)
    one[bucket[ok], np.arange(384)[ok]] = 1.0
    one[NBUCKET, ~ok] = NEG
    return c, t.reshape(NQ * P, TABW), one


def layout_mixer_weights(w_in, w_out):
    col = 0
    starts = []
    for size in (384, 128, 128, 384, 384, 384, 384, 256):
        starts.append(col)
        col += size
    qa, ka, va, qr, kr, vr, gr, up = starts
    head = [np.arange(h * HEAD, (h + 1) * HEAD) for h in range(NQH)]
    pair = [np.concatenate([head[c], head[c + GROUP]]) for c in range(GROUP)]
    cols = [qa + pair[c] for c in range(GROUP)]
    cols += [s + np.arange(P) for s in (ka, va, up)]
    cols += [s + c * P + np.arange(P) for s in (qr, kr, vr, gr) for c in range(3)]
    cols += [up + P + np.arange(P)]
    units = [w_in[:, k].reshape(C, P, P).transpose(1, 0, 2).reshape(P, C * P) for k in cols]
    rows = [pair[c] for c in range(GROUP)] + [384 + c * P + np.arange(P) for c in range(5)]
    units += [w_out[k, :] for k in rows]
    return np.ascontiguousarray(np.stack(units))


def layout_mlp_weights(w_up, w_down):
    ups = [w_up[:, f * P:(f + 1) * P].reshape(C, P, P).transpose(1, 0, 2).reshape(P, C * P) for f in range(2 * NG)]
    downs = [w_down[f * P:(f + 1) * P, :] for f in range(2 * NG)]
    units = []
    for g in range(NG):
        n = (g + 1) % NG
        units += [downs[2 * g], downs[2 * g + 1], ups[2 * n], ups[2 * n + 1]]
    return np.ascontiguousarray(np.stack(units))


def kernel(x, attn_norm_g, w_in, attn_sinks, rel_bias, pool_w, pool_scale, w_out, mlp_norm_g, w_up, w_down, final_norm_g):
    import concourse.bacc as bacc
    from concourse.bass_utils import run_bass_kernel_spmd

    def a(v):
        return np.asarray(v)

    cst, tab, onehot = shape_constants()
    arrays = {
        "x": a(x).reshape(SEQ, D),
        "wmix": layout_mixer_weights(a(w_in)[0], a(w_out)[0]),
        "wmlp": layout_mlp_weights(a(w_up)[0], a(w_down)[0]),
        "cst": cst, "tab": tab, "onehot": onehot,
        "gmix": a(attn_norm_g).reshape(C, P).T, "gmlp": a(mlp_norm_g).reshape(C, P).T,
        "gfin": a(final_norm_g).reshape(1, D), "sinks": a(attn_sinks).reshape(1, NQH), "rel_bias": a(rel_bias),
        "pool_w": a(pool_w)[0], "pool_scale": a(pool_scale).reshape(2, P).T,
    }
    arrays = {f"in_{k}": np.ascontiguousarray(v) for k, v in arrays.items()}
    nc = bacc.Bacc("TRN2", target_bir_lowering=False, num_devices=1)
    args = [nc.dram_tensor(k, v.shape, mybir.dt.from_np(v.dtype), kind="ExternalInput").ap() for k, v in arrays.items()]
    out = nc.dram_tensor("out", (SEQ, D), F32, kind="ExternalOutput").ap()
    build(nc, *args, out)
    got = run_bass_kernel_spmd(nc, [arrays], core_ids=[0])
    return got.results[0]["out"].reshape(1, SEQ, D)
```

```python
from contextlib import ExitStack

import numpy as np

import concourse.bass as bass
from concourse import mybir

P = 128
D = 1024
SEQ = 2048
HEAD = 64
NQH, NKV, NRET = 6, 2, 6
GROUP = NQH // NKV
POOLW = 256
WINDOWS = (2, 4, 8, 16)
FF = 4 * D
EPS = 1e-6
NEG = -1e30
NBUCKET = 32
MAXDIST = 128
SCALE = HEAD ** -0.5

C = D // P
QT = 512
NQ = SEQ // QT
NB = QT // P
HT = 1024
NH = SEQ // HT
HB = HT // P
RING = 6
STAGE = 3
NU = 27
NG = FF // (2 * P)
TABW = 2 * NB * HEAD + 32
PADW = 16

F32 = mybir.dt.float32
F32R = mybir.dt.float32r
ALU = mybir.AluOpType
ACT = mybir.ActivationFunctionType
AX = mybir.AxisListType.X

CST = {}
_at = 0
for _name, _width in (("ident", P), ("mask", NRET * P), ("gchunk", 3 * P), ("zeta", NRET), ("xi2", NRET),
                      ("xih", NRET), ("invw", 2), ("mhalf", 8), ("eps", 8)):
    CST[_name] = (_at, _at + _width)
    _at += _width
CSTW = _at

T_GROUP, T_UP1, T_OA, T_OR, NT = 6, 22, 23, 31, 39


def last_tile_of_unit(u):
    if u < 6:
        return u
    if u < 18:
        return T_GROUP + 4 * ((u - 6) // 3) + 3
    return T_UP1 if u == 18 else (T_OR - 1 if u < 22 else NT - 1)


def slot_owner(u):
    if u >= RING:
        return True, u - RING
    return False, max(v for v in range(NU) if v % RING == u)


class Events:

    def __init__(self, sem, per, by=1):
        self.sem, self.per, self.by = sem, per, by

    @property
    def primed(self):
        return self.per * self.by

    def now(self, r, i):
        return r * (self.per * self.by) + (self.per + i + 1) * self.by

    def before(self, r, i):
        return r * (self.per * self.by) + (i + 1) * self.by


def build(nc, x, wmix, wmlp, cst, tab, onehot, gmix, gmlp, gfin, sinks, rel_bias, pool_w, pool_scale, out):
    x2_dram = nc.dram_tensor("x2_dram", (SEQ, D), F32).ap()
    rows_dram = nc.dram_tensor("bias_rows_dram", (NQH, P * 384), F32).ap()

    with ExitStack() as ctx:
        def sb(name, shape, dt=F32, stack=ctx):
            return stack.enter_context(nc.sbuf_tensor(name, shape, dt))

        def ps(name):
            return ctx.enter_context(nc.psum_tensor(name, [P, 512], F32))

        def sem(name):
            return ctx.enter_context(nc.semaphore(name))

        ring_hi = sb("ring_hi", [P, RING, 1024], F32R)
        ring_lo = sb("ring_lo", [P, RING, 1024], F32R)
        stage = sb("stage", [P, STAGE, 1024])
        ident = sb("ident", [P, P])
        mhalf = sb("mhalf", [P, 8])
        epsc = sb("epsc", [P, 8])
        ssum = sb("ssum", [P, 8])
        var = sb("var", [P, 8])
        rstd = sb("rstd", [P, 8])
        ssum2 = sb("ssum2", [P, SEQ // P])
        var2 = sb("var2", [P, SEQ // P])
        rstd2 = sb("rstd2", [P, SEQ // P])

        with ExitStack() as mem:
            def ms(name, shape, dt=F32):
                return sb(name, shape, dt, mem)
            xq = ms("xq", [P, NB, D])
            hT_hi = ms("hT_hi", [P, C, QT], F32R)
            hT_lo = ms("hT_lo", [P, C, QT], F32R)
            yA_hi = ms("yA_hi", [P, 3, QT], F32R)
            yA_lo = ms("yA_lo", [P, 3, QT], F32R)
            qT = ms("qT", [P, 3, QT])
            kT = ms("kT", [P, P + QT])
            vT = ms("vT", [P, QT])
            vtok = ms("vtok", [P, NB + 1, P])
            up = ms("up", [P, 2, PADW + QT])
            zt = ms("zt", [P, NB, 4 * 3 * P])
            bias = ms("bias", [P, NQH, 2 * P])
            bias0 = ms("bias0", [P, NQH, 2 * P])
            cmask = ms("cmask", [P, NRET * P])
            gch = ms("gch", [P, 3 * P])
            R = ms("R", [P, 3 * P])
            tabs = ms("tabs", [P, TABW])
            small = ms("small", [P, 32])
            nsink = ms("nsink", [P, NQH])
            sinkb = ms("sinkb", [P, NQH])
            pscale = ms("pscale", [P, 2])
            poolw = ms("poolw", [P, 2, P])
            sc = ms("sc", [P, 2, 3 * 2 * P])
            pt = ms("pt", [P, 2, 2 * 3 * P])
            rmax = ms("rmax", [P, 2, 3])
            nmax = ms("nmax", [P, 2, 3])
            sde = ms("sde", [P, 2, 3])
            ses = ms("ses", [P, 2, 3])
            rsum = ms("rsum", [P, 2, 3])
            rinv = ms("rinv", [P, 2, 3])
            qk = ms("qk", [P, 6 * P])
            grow = ms("grow", [P, D])
            junk = ms("junk", [P, D], mybir.dt.bfloat16)
            ss6 = ms("ss6", [P, 6])
            v6 = ms("v6", [P, 6])
            r6 = ms("r6", [P, 6])
            s6 = ms("s6", [P, 6])
            pooled = ms("pooled", [P, QT])
            p16 = ms("p16", [P, PADW])
            sc_flat = sc[:, :, :].rearrange("p a b -> p (a b)")
            pt_flat = pt[:, :, :].rearrange("p a b -> p (a b)")
            qkT = sc_flat[:, 0:768]
            Pm = sc_flat[:, 768:1536]
            sq = pt_flat[:, 0:384]
            th = pt_flat[:, 384:768]
            gate = pt_flat[:, 768:1152]
            yv = pt_flat[:, 1152:1536]
            xn = (sc_flat[:, 0:1024], pt_flat[:, 0:1024])
            qT_flat = qT[:, :, :].rearrange("p a b -> p (a b)")
            win_a = qT_flat[:, 0:PADW + QT]
            win_b = qT_flat[:, PADW + QT:2 * (PADW + QT)]
            relb = zt[0:NBUCKET + 1, 0, 0:NQH]
            relw = zt[0:NBUCKET + 1, 1, 0:NQH * P].rearrange("p (h m) -> p h m", h=NQH)
            oneh = zt[0:NBUCKET + 1, 0, 64:64 + 384]
            rrow = zt[:, 2:4, :].rearrange("p a b -> p (a b)")[:, 0:NQH * 384].rearrange("p (h m) -> p h m", h=NQH)

        with ExitStack() as mem:
            def ml(name, shape, dt=F32):
                return sb(name, shape, dt, mem)
            x2 = ml("x2", [P, HB, D])
            h2T_hi = ml("h2T_hi", [P, C, HT], F32R)
            h2T_lo = ml("h2T_lo", [P, C, HT], F32R)
            u_hi = ml("u_hi", [P, 2, HT], F32R)
            u_lo = ml("u_lo", [P, 2, HT], F32R)
            fg = ml("fg", [P, D])
            grow2 = ml("grow2", [P, D])
            xn2 = ml("xn2", [P, 4, D])
            sqj = ml("sqj", [P, D], mybir.dt.bfloat16)
            relu = ml("relu", [P, 2, QT])
            rsq = ml("rsq", [P, 2, QT])

        bank = [ps(f"bank{i}") for i in range(8)]
        dense = bank[0:3]
        S0, S1, T0, T1, OB = bank[3], bank[4], bank[5], bank[6], bank[7]
        up_bank = bank[4:8]
        down_bank = bank[0:4]

        s_const = sem("s_const")
        s_ident = sem("s_ident")
        s_rel = sem("s_rel")
        s_relw = sem("s_relw")
        s_browmm = sem("s_browmm")
        s_brow = sem("s_brow")
        s_rowst = sem("s_rowst")
        s_bias = sem("s_bias")
        s_init = sem("s_init")
        s_pm = sem("s_pm")

        x_full = [Events(sem(f"x_full{b}"), 1, 16) for b in range(NB)]
        x2_stored = [Events(sem(f"x2_stored{b}"), 1, 16) for b in range(NB)]
        tab_full = Events(sem("tab_full"), 1, 16)
        st_full = [Events(sem(f"st_full{s}"), NU // STAGE, 16) for s in range(STAGE)]
        sq_done = Events(sem("sq_done"), 4)
        var_done = Events(sem("var_done"), 4)
        rstd_done = Events(sem("rstd_done"), 4)
        xn_done = Events(sem("xn_done"), 4)
        xtr_done = Events(sem("xtr_done"), 8)
        xhi_done = Events(sem("xhi_done"), 8)
        xlo_done = Events(sem("xlo_done"), 8)
        whi_done = Events(sem("whi_done"), NU)
        wlo_done = Events(sem("wlo_done"), NU)
        tile_done = Events(sem("tile_done"), NT)
        z_evac = Events(sem("z_evac"), T_OA)
        x2_evac = Events(sem("x2_evac"), NT - T_OA)
        carried = Events(sem("carried"), 5)
        vtr_done = Events(sem("vtr_done"), 1)
        v_evac = Events(sem("v_evac"), 1)
        s_done = Events(sem("s_done"), 8)
        sc_done = Events(sem("sc_done"), 16)
        max_done = Events(sem("max_done"), 8)
        nmax_done = Events(sem("nmax_done"), 8)
        sde_done = Events(sem("sde_done"), 8)
        exp_done = Events(sem("exp_done"), 32)
        den_done = Events(sem("den_done"), 8)
        rinv_done = Events(sem("rinv_done"), 8)
        pn_done = Events(sem("pn_done"), 24)
        ptr_done = Events(sem("ptr_done"), 8)
        pt_evac = Events(sem("pt_evac"), 16)
        o_done = Events(sem("o_done"), 8)
        yAhi_done = Events(sem("yAhi_done"), 8)
        yAlo_done = Events(sem("yAlo_done"), 8)
        rotA_done = Events(sem("rotA_done"), 4)
        rotB_done = Events(sem("rotB_done"), 8)
        qk_done = Events(sem("qk_done"), 4)
        kz_done = Events(sem("kz_done"), 4)
        qktr_done = Events(sem("qktr_done"), 8)
        qkT_evac = Events(sem("qkT_evac"), 8)
        rs_done = Events(sem("rs_done"), 8)
        pm_done = Events(sem("pm_done"), 8)
        ro_done = Events(sem("ro_done"), 4)
        ru_done = Events(sem("ru_done"), 4)
        rg_done = Events(sem("rg_done"), 4)
        R_done = Events(sem("R_done"), 8)
        osb_done = Events(sem("osb_done"), 4)
        sqr_done = Events(sem("sqr_done"), 4)
        th_done = Events(sem("th_done"), 4)
        ss6_done = Events(sem("ss6_done"), 4)
        v6_done = Events(sem("v6_done"), 8)
        r6_done = Events(sem("r6_done"), 4)
        s6_done = Events(sem("s6_done"), 4)
        gate_done = Events(sem("gate_done"), 4)
        ya_done = Events(sem("ya_done"), 4)
        y_done = Events(sem("y_done"), 4)
        ytr_done = Events(sem("ytr_done"), 4)
        yRhi_done = Events(sem("yRhi_done"), 4)
        yRlo_done = Events(sem("yRlo_done"), 4)
        win_done = Events(sem("win_done"), 6)
        pool16_done = Events(sem("pool16_done"), 8)
        pooled_done = Events(sem("pooled_done"), 4)
        mix_done = Events(sem("mix_done"), 2)
        yPhi_done = Events(sem("yPhi_done"), 2)
        yPlo_done = Events(sem("yPlo_done"), 2)
        fg_full = sem("fg_full")
        m_x_full = [Events(sem(f"m_x_full{b}"), 1, 16) for b in range(HB)]
        m_out = [Events(sem(f"m_out{b}"), 1, 16) for b in range(HB)]
        m_st_full = [Events(sem(f"m_st_full{s}"), 2, 16) for s in range(2)]
        sq2_done = Events(sem("sq2_done"), NB)
        var2_done = Events(sem("var2_done"), NB)
        rstd2_done = Events(sem("rstd2_done"), NB)
        m_raw = [Events(sem(f"m_raw{k}"), 2, 16) for k in range(4)]
        m_sq = Events(sem("m_sq"), HB)
        m_var = Events(sem("m_var"), HB)
        m_rstd = Events(sem("m_rstd"), HB)
        m_xn = Events(sem("m_xn"), HB)
        m_xtr = Events(sem("m_xtr"), 2 * HB)
        m_xhi = Events(sem("m_xhi"), 2 * HB)
        m_xlo = Events(sem("m_xlo"), 2 * HB)
        m_whi = Events(sem("m_whi"), 4)
        m_wlo = Events(sem("m_wlo"), 4)
        m_up = Events(sem("m_up"), 4)
        m_relu = Events(sem("m_relu"), 4)
        m_rsq = Events(sem("m_rsq"), 4)
        m_uhi = Events(sem("m_uhi"), 4)
        m_ulo = Events(sem("m_ulo"), 4)
        m_down = Events(sem("m_down"), 16)
        m_acc = Events(sem("m_acc"), 16)
        m_fin = Events(sem("m_fin"), HB)

        def norm_bank(b, j):
            return ((T0, T1), (S0, S1))[b % 2][j]

        def m_norm_bank(b, j):
            return ((bank[4], bank[5]), (bank[6], bank[7]))[b % 2][j]

        def cview(name):
            a, b = CST[name]
            return cst[:, a:b]

        zeta = small[:, 0:6]
        xi2 = small[:, 6:12]
        xih = small[:, 12:18]
        invw = small[:, 18:20]

        def kz_view(b):
            return zt[:, b, 384:768]

        def osb_view(b):
            return zt[:, b, 0:384]

        def cos_of(b):
            return tabs[:, b * HEAD:(b + 1) * HEAD]

        def sin_of(b):
            return tabs[:, NB * HEAD + b * HEAD:NB * HEAD + (b + 1) * HEAD]

        def icnt_of(cc):
            return tabs[:, 2 * NB * HEAD + 16 * cc:2 * NB * HEAD + 16 * cc + 16]

        block = ctx.enter_context(nc.Block())

        @block.sync
        def _(sp):
            for e in [*x2_stored, *m_out]:
                sp.sem_inc(e.sem, e.primed)
            for e in [tab_full, *st_full, *m_x_full, *m_raw]:
                sp.sem_inc(e.sem, e.primed)
            for e in m_st_full:
                sp.sem_inc(e.sem, 16)
            sp.dma_start(ident[:, :], cview("ident")).then_inc(s_ident, 16)
            sp.dma_start(mhalf[:, :], cview("mhalf")).then_inc(s_ident, 16)
            sp.dma_start(epsc[:, :], cview("eps")).then_inc(s_ident, 16)
            sp.dma_start(grow[:, :], gmix.to_broadcast([P, D])).then_inc(s_ident, 16)
            sp.wait_ge(s_init, 1)
            sp.dma_start(relb[0:NBUCKET, :], rel_bias).then_inc(s_rel, 16)
            sp.dma_start(oneh, onehot).then_inc(s_rel, 16)
            sp.dma_start(cmask[:, :], cview("mask")).then_inc(s_const, 16)
            sp.dma_start(gch[:, :], cview("gchunk")).then_inc(s_const, 16)
            sp.dma_start(small[:, 0:20], cst[:, CST["zeta"][0]:CST["invw"][1]]).then_inc(s_const, 16)
            sp.dma_start(sinkb[:, :], sinks.to_broadcast([P, NQH])).then_inc(s_const, 16)
            sp.dma_start(pscale[:, :], pool_scale).then_inc(s_const, 16)
            sp.wait_ge(s_pm, 1)
            for g in range(4):
                a = HEAD * (g % 2)
                sp.dma_start(poolw[a:a + HEAD, g // 2, a:a + HEAD], pool_w[g]).then_inc(s_const, 16)
            sp.wait_ge(s_brow, NQH)
            sp.dma_start(rows_dram.rearrange("h (p m) -> p h m", m=384), rrow).then_inc(s_rowst, 16)
            sp.wait_ge(s_rowst, 16)
            for h in range(NQH):
                src = rows_dram[h:h + 1, P - 1:P - 1 + P * 383].rearrange("a (p m) -> (a p) m", m=383)
                sp.dma_start(bias[:, h, :], src[:, 0:2 * P]).then_inc(s_bias, 16)

            with sp.Fori(0, NQ) as q:
                sp.wait_ge(qk_done.sem, qk_done.before(q, 3))
                sp.wait_ge(pool16_done.sem, pool16_done.before(q, 7))
                sp.dma_start(tabs[:, :], tab[bass.ds(q * P, P), :]).then_inc(tab_full.sem, 16)
                for u in range(NU):
                    if u >= STAGE:
                        sp.wait_ge(wlo_done.sem, wlo_done.now(q, u - STAGE))
                    else:
                        sp.wait_ge(wlo_done.sem, wlo_done.before(q, NU - STAGE + u))
                    sp.dma_start(stage[:, u % STAGE, :], wmix[u]).then_inc(st_full[u % STAGE].sem, 16)
                for b in range(NB):
                    sp.wait_ge(x2_evac.sem, x2_evac.now(q, 8 + 2 * b + 1))
                    sp.dma_start(x2_dram[bass.ds(q * QT + b * P, P), :], xq[:, b, :]).then_inc(x2_stored[b].sem, 16)

            for b in range(NB):
                sp.wait_ge(x2_stored[b].sem, x2_stored[b].now(NQ - 1, 0))
            sp.wait_ge(rstd2_done.sem, rstd2_done.now(NQ - 1, NB - 1))
            sp.dma_start(grow2[:, :], gmlp.to_broadcast([P, D])).then_inc(fg_full, 16)
            sp.dma_start(fg[:, :], gfin.to_broadcast([P, D])).then_inc(fg_full, 16)

            def load_raw(h, b):
                if h or b >= 4:
                    hp, bp = (h, b - 4) if b >= 4 else (h - 1, b + 4)
                    sp.wait_ge(m_xtr.sem, m_xtr.now(hp, 2 * bp + 1))
                sp.dma_start(xn2[:, b % 4, :], x2_dram[h * HT + b * P:h * HT + (b + 1) * P, :]).then_inc(m_raw[b % 4].sem, 16)

            for b in range(4):
                load_raw(0, b)
            sp.wait_ge(wlo_done.sem, wlo_done.now(NQ - 1, NU - 1))
            for s in range(2):
                sp.dma_start(stage[:, s, :], wmlp[4 * NG - 2 + s]).then_inc(m_st_full[s].sem, 16)
            for b in range(4, HB):
                load_raw(0, b)
            for h in range(NH):
                for b in range(HB):
                    sp.wait_ge(m_out[b].sem, m_out[b].before(h, 0))
                    sp.dma_start(x2[:, b, :], x2_dram[h * HT + b * P:h * HT + (b + 1) * P, :]).then_inc(m_x_full[b].sem, 16)
                if h + 1 < NH:
                    for b in range(4):
                        load_raw(h + 1, b)
                with sp.Fori(0, NG) as g:
                    for u in range(4):
                        G = h * NG + g
                        if u >= 2:
                            sp.wait_ge(m_wlo.sem, m_wlo.now(G, u - 2))
                        else:
                            sp.wait_ge(m_wlo.sem, m_wlo.before(G, u + 2))
                        sp.dma_start(stage[:, u % 2, :], wmlp[bass.ds(g * 4 + u, 1)].rearrange("a p n -> (a p) n")).then_inc(m_st_full[u % 2].sem, 16)
                if h + 1 < NH:
                    for b in range(4, HB):
                        load_raw(h + 1, b)
                for b in range(HB):
                    sp.wait_ge(m_fin.sem, m_fin.now(h, b))
                    sp.dma_start(out[h * HT + b * P:h * HT + (b + 1) * P, :], x2[:, b, :]).then_inc(m_out[b].sem, 16)
            for b in range(HB):
                sp.wait_ge(m_out[b].sem, m_out[b].now(NH - 1, 0))

        @block.gpsimd
        def _(pool):
            for e in (wlo_done, rstd_done, rstd2_done, var2_done, m_rstd, var_done, m_var, rotB_done, kz_done,
                      rg_done, v6_done, r6_done, s6_done, win_done):
                pool.sem_inc(e.sem, e.primed)
            pool.sem_inc(m_wlo.sem, 2)
            pool.memset(relb, 1.0).then_inc(s_init, 1)
            pool.memset(poolw[:, :, :], 0.0).then_inc(s_pm, 1)
            pool.memset(kT[:, :], 0.0).then_inc(s_pm, 1)
            pool.memset(vtok[:, :, :], 0.0).then_inc(s_pm, 1)
            pool.memset(up[:, :, :], 0.0).then_inc(s_pm, 1)
            pool.memset(R[:, :], 0.0).then_inc(s_pm, 1)
            pool.memset(bias0[:, :, 0:P], NEG).then_inc(s_pm, 1)
            pool.wait_ge(s_pm, 6)
            pool.wait_ge(s_ident, 64)

            def split_lo(q, u):
                pool.wait_ge(whi_done.sem, whi_done.now(q, u))
                s = u % RING
                pool.tensor_tensor(ring_lo[:, s, :], stage[:, u % STAGE, :], ring_hi[:, s, :].bitcast(F32),
                                   ALU.subtract).then_inc(wlo_done.sem, 1)

            def inv_rms(q, b):
                pool.wait_ge(sq_done.sem, sq_done.now(q, b))
                pool.tensor_tensor(var[:, b:b + 1], ssum[:, b:b + 1], epsc[:, 0:1], ALU.add).then_inc(var_done.sem, 1)
                pool.wait_ge(var_done.sem, var_done.now(q, b))
                pool.tensor_tensor(rstd[:, b:b + 1], var[:, b:b + 1], mhalf[:, 0:1], ALU.pow).then_inc(rstd_done.sem, 1)

            def inv_rms2(q, b):
                col = bass.ds(q * NB + b, 1)
                pool.wait_ge(sq2_done.sem, sq2_done.now(q, b))
                pool.tensor_tensor(var2[:, col], ssum2[:, col], epsc[:, 0:1], ALU.add).then_inc(var2_done.sem, 1)
                pool.wait_ge(var2_done.sem, var2_done.now(q, b))
                pool.tensor_tensor(rstd2[:, col], var2[:, col], mhalf[:, 0:1], ALU.pow).then_inc(rstd2_done.sem, 1)

            def rot_b(q, b):
                if b == 0:
                    pool.wait_ge(tab_full.sem, tab_full.now(q, 0))
                    pool.wait_ge(z_evac.sem, z_evac.now(q, T_GROUP + 7))
                    pool.wait_ge(kz_done.sem, kz_done.before(q, 3))
                    pool.wait_ge(qktr_done.sem, qktr_done.before(q, 7))
                else:
                    pool.wait_ge(kz_done.sem, kz_done.now(q, b - 1))
                    pool.wait_ge(qktr_done.sem, qktr_done.now(q, 2 * b - 1))
                src = zt[:, b, 0:768].rearrange("p (h i two) -> p h i two", h=12, two=2)
                dst = qk[:, :].rearrange("p (h i two) -> p h i two", h=12, two=2)
                sn = sin_of(b).rearrange("p (a i two) -> p a i two", a=1, two=2)
                for e in range(2):
                    pool.tensor_tensor(dst[:, :, :, e], src[:, :, :, 1 - e],
                                       sn[:, :, :, e].to_broadcast([P, 12, 32]), ALU.mult).then_inc(rotB_done.sem, 1)

            def kz_of(q, b):
                pool.wait_ge(qk_done.sem, qk_done.now(q, b))
                pool.wait_ge(qk_done.sem, qk_done.now(q, b))
                pool.tensor_tensor(kz_view(b).rearrange("p (h d) -> p h d", h=6),
                                   qk[:, 384:768].rearrange("p (h d) -> p h d", h=6),
                                   zeta.rearrange("p (h a) -> p h a", a=1).to_broadcast([P, 6, HEAD]),
                                   ALU.mult).then_inc(kz_done.sem, 1)

            def decay_state(q, b):
                pool.wait_ge(ro_done.sem, ro_done.now(q, b))
                pool.tensor_tensor(R[:, :], R[:, :], gch[:, :], ALU.mult).then_inc(rg_done.sem, 1)

            def ret_scale(q, b):
                pool.wait_ge(ss6_done.sem, ss6_done.now(q, b))
                pool.tensor_tensor(v6[:, :], ss6[:, :], xi2, ALU.mult).then_inc(v6_done.sem, 1)
                pool.wait_ge(v6_done.sem, v6_done.now(q, 2 * b))
                pool.tensor_tensor(v6[:, :], v6[:, :], epsc[:, 0:6], ALU.add).then_inc(v6_done.sem, 1)
                pool.wait_ge(v6_done.sem, v6_done.now(q, 2 * b + 1))
                pool.tensor_tensor(r6[:, :], v6[:, :], mhalf[:, 0:6], ALU.pow).then_inc(r6_done.sem, 1)
                pool.wait_ge(r6_done.sem, r6_done.now(q, b))
                pool.tensor_tensor(s6[:, :], r6[:, :], xih, ALU.mult).then_inc(s6_done.sem, 1)

            def windows(q, cc):
                if cc == 0:
                    pool.wait_ge(s_done.sem, s_done.now(q, 7))
                    pool.wait_ge(z_evac.sem, z_evac.now(q, T_UP1))
                else:
                    pool.wait_ge(pooled_done.sem, pooled_done.now(q, 1))
                    pool.wait_ge(pool16_done.sem, pool16_done.now(q, 3))
                src, n0 = up[:, cc, :], 1
                for n, step in enumerate((1, 2) if cc == 0 else (1, 2, 4, 8)):
                    dst = win_a if n % 2 == 0 else win_b
                    lo = 2 * step - 1
                    if n:
                        pool.wait_ge(win_done.sem, win_done.now(q, 2 * cc + n - 1))
                    pool.tensor_tensor(dst[:, lo:PADW + QT], src[:, lo:PADW + QT],
                                       src[:, lo - step:PADW + QT - step], ALU.add).then_inc(win_done.sem, 1)
                    src = dst

            with pool.Fori(0, NQ) as q:
                for b in range(NB):
                    inv_rms(q, b)
                for u in range(6):
                    split_lo(q, u)
                for k in range(6):
                    split_lo(q, k + 6)
                for i in range(8):
                    if i % 2 == 1:
                        for u in range(3):
                            split_lo(q, 12 + 3 * (i // 2) + u)
                    if i == 5:
                        rot_b(q, 0)
                        kz_of(q, 0)
                split_lo(q, 24)
                windows(q, 0)
                rot_b(q, 1)
                decay_state(q, 0)
                kz_of(q, 1)
                ret_scale(q, 0)
                windows(q, 1)
                rot_b(q, 2)
                decay_state(q, 1)
                kz_of(q, 2)
                ret_scale(q, 1)
                split_lo(q, 25)
                split_lo(q, 26)
                rot_b(q, 3)
                decay_state(q, 2)
                kz_of(q, 3)
                ret_scale(q, 2)
                decay_state(q, 3)
                ret_scale(q, 3)
                for b in range(NB):
                    inv_rms2(q, b)

            def m_split_lo(G, u):
                pool.wait_ge(m_whi.sem, m_whi.now(G, u))
                pool.tensor_tensor(ring_lo[:, u, :], stage[:, u % 2, :], ring_hi[:, u, :].bitcast(F32),
                                   ALU.subtract).then_inc(m_wlo.sem, 1)

            for u in (2, 3):
                pool.wait_ge(m_whi.sem, m_whi.before(0, u))
                pool.tensor_tensor(ring_lo[:, u, :], stage[:, u % 2, :], ring_hi[:, u, :].bitcast(F32),
                                   ALU.subtract).then_inc(m_wlo.sem, 1)

            for h in range(NH):
                with pool.Fori(0, NG) as g:
                    for u in range(4):
                        m_split_lo(h * NG + g, u)
                for b in range(HB):
                    pool.wait_ge(m_sq.sem, m_sq.now(h, b))
                    pool.tensor_tensor(var[:, b:b + 1], ssum[:, b:b + 1], epsc[:, 0:1], ALU.add).then_inc(m_var.sem, 1)
                    pool.wait_ge(m_var.sem, m_var.now(h, b))
                    pool.tensor_tensor(rstd[:, b:b + 1], var[:, b:b + 1], mhalf[:, 0:1], ALU.pow).then_inc(m_rstd.sem, 1)

        @block.scalar
        def _(act):
            for e in (sq_done, xhi_done, whi_done, z_evac, v_evac, exp_done, pt_evac, yAhi_done, qkT_evac,
                      osb_done, sqr_done, th_done, yRhi_done, yPhi_done, sq2_done, *x_full, m_sq, m_xhi, m_relu, m_uhi):
                act.sem_inc(e.sem, e.primed)
            act.sem_inc(m_whi.sem, 2)

            def split_hi(q, u):
                act.wait_ge(st_full[u % STAGE].sem, st_full[u % STAGE].now(q, u // STAGE))
                same, owner = slot_owner(u)
                if same:
                    act.wait_ge(tile_done.sem, tile_done.now(q, last_tile_of_unit(owner)))
                    act.wait_ge(wlo_done.sem, wlo_done.now(q, owner))
                else:
                    act.wait_ge(tile_done.sem, tile_done.before(q, last_tile_of_unit(owner)))
                act.activation(ring_hi[:, u % RING, :], stage[:, u % STAGE, :], ACT.Copy).then_inc(whi_done.sem, 1)

            def load_x(q, b):
                act.wait_ge(x2_stored[b].sem, x2_stored[b].before(q, 0))
                act.wait_ge(sq2_done.sem, sq2_done.before(q, b))
                act.dma_start(xq[:, b, :], x[bass.ds(q * QT + b * P, P), :]).then_inc(x_full[b].sem, 16)

            def square_x(q, b):
                act.wait_ge(x_full[b].sem, x_full[b].now(q, 0))
                if b:
                    act.wait_ge(sq_done.sem, sq_done.now(q, b - 1))
                else:
                    act.wait_ge(sq2_done.sem, sq2_done.before(q, NB - 1))
                act.activation(junk[:, :], xq[:, b, :], ACT.Square, scale=D ** -0.5, accum_out=ssum[:, b:b + 1]).then_inc(sq_done.sem, 1)

            def square_x2(q, b):
                act.wait_ge(x2_evac.sem, x2_evac.now(q, 8 + 2 * b + 1))
                if b:
                    act.wait_ge(sq2_done.sem, sq2_done.now(q, b - 1))
                act.activation(junk[:, :], xq[:, b, :], ACT.Square, scale=D ** -0.5,
                               accum_out=ssum2[:, bass.ds(q * NB + b, 1)]).then_inc(sq2_done.sem, 1)

            def x_hi(q, b):
                for j in range(2):
                    n = 2 * b + j
                    act.wait_ge(xtr_done.sem, xtr_done.now(q, n))
                    if n == 0:
                        act.wait_ge(tile_done.sem, tile_done.before(q, NT - 1))
                    act.activation(hT_hi[:, 4 * j:4 * j + 4, b * P:(b + 1) * P],
                                   norm_bank(b, j)[:, :].rearrange("p (c t) -> p c t", c=4), ACT.Copy).then_inc(xhi_done.sem, 1)

            def evac_T(q, t):
                act.wait_ge(tile_done.sem, tile_done.now(q, t))
                src = dense[t % 3][:, :]
                if t < 3:
                    dst = qT[:, t, :]
                elif t == 3:
                    act.wait_ge(carried.sem, carried.now(q, 0))
                    dst = kT[:, P:P + QT]
                elif t == 4:
                    dst = vT[:, :]
                else:
                    act.wait_ge(carried.sem, carried.now(q, 2))
                    dst = up[:, 0 if t == 5 else 1, PADW:PADW + QT]
                act.activation(dst, src, ACT.Copy).then_inc(z_evac.sem, 1)

            def evac_G(q, t):
                act.wait_ge(tile_done.sem, tile_done.now(q, T_GROUP + t))
                g, b = t // 4, t % 4
                act.activation(zt[:, b, 384 * g:384 * g + 384], dense[(T_GROUP + t) % 3][:, 0:384],
                               ACT.Copy).then_inc(z_evac.sem, 1)

            def exps(q, i):
                b, g = i // 2, i % 2
                k = i % 2
                act.wait_ge(nmax_done.sem, nmax_done.now(q, i))
                for h in range(3):
                    act.activation(sc[:, k, 256 * h:256 * h + 256], sc[:, k, 256 * h:256 * h + 256], ACT.Exp,
                                   bias=nmax[:, k, h:h + 1], accum_out=rsum[:, k, h:h + 1]).then_inc(exp_done.sem, 1)
                act.wait_ge(sde_done.sem, sde_done.now(q, i))
                act.activation(ses[:, k, :], sde[:, k, :], ACT.Exp).then_inc(exp_done.sem, 1)

            def evac_pt(q, i):
                k = i % 2
                act.wait_ge(ptr_done.sem, ptr_done.now(q, i))
                if i >= 2:
                    act.wait_ge(o_done.sem, o_done.now(q, i - 2))
                for half in range(2):
                    act.activation(pt[:, k, 384 * half:384 * half + 384], (T0, T1)[half][:, 0:384],
                                   ACT.Copy).then_inc(pt_evac.sem, 1)

            def yA_high(q, i):
                b, g = i // 2, i % 2
                act.wait_ge(o_done.sem, o_done.now(q, i))
                if i == 0:
                    act.wait_ge(tile_done.sem, tile_done.before(q, T_OR - 1))
                a = HEAD * g
                act.activation(yA_hi[a:a + HEAD, :, b * P:(b + 1) * P],
                               OB[a:a + HEAD, 0:384].rearrange("p (c t) -> p c t", c=3), ACT.Copy).then_inc(yAhi_done.sem, 1)

            def evac_qkT(q, b):
                for k in range(2):
                    act.wait_ge(qktr_done.sem, qktr_done.now(q, 2 * b + k))
                    if k == 0:
                        if b == 0:
                            act.wait_ge(ptr_done.sem, ptr_done.now(q, 7))
                        else:
                            act.wait_ge(ro_done.sem, ro_done.now(q, b - 1))
                    act.activation(qkT[:, 384 * k:384 * k + 384], (T0, T1)[k][:, 0:384], ACT.Copy).then_inc(qkT_evac.sem, 1)

            def ret_out(q, b):
                act.wait_ge(ro_done.sem, ro_done.now(q, b))
                act.wait_ge(qktr_done.sem, qktr_done.now(q, 2 * b + 1))
                if b:
                    act.wait_ge(ya_done.sem, ya_done.now(q, b - 1))
                    act.wait_ge(gate_done.sem, gate_done.now(q, b - 1))
                act.activation(osb_view(b), OB[:, 0:384], ACT.Copy).then_inc(osb_done.sem, 1)
                if b == 0:
                    act.wait_ge(o_done.sem, o_done.now(q, 7))
                act.activation(sq, OB[:, 0:384], ACT.Square).then_inc(sqr_done.sem, 1)
                act.activation(th, zt[:, b, 1152:1536], ACT.Tanh, scale=0.5).then_inc(th_done.sem, 1)

            def yR_high(q, b):
                act.wait_ge(ytr_done.sem, ytr_done.now(q, b))
                act.activation(hT_hi[:, 0:3, b * P:(b + 1) * P], T0[:, 0:384].rearrange("p (c t) -> p c t", c=3),
                               ACT.Copy).then_inc(yRhi_done.sem, 1)

            def yP_high(q, cc):
                act.wait_ge(mix_done.sem, mix_done.now(q, cc))
                act.activation(hT_hi[:, 3 + cc, :], T1[:, :], ACT.Copy, scale=pscale[:, cc:cc + 1]).then_inc(yPhi_done.sem, 1)

            with act.Fori(0, NQ) as q:
                load_x(q, 0)
                load_x(q, 1)
                load_x(q, 2)
                square_x(q, 0)
                square_x(q, 1)
                load_x(q, 3)
                square_x(q, 2)
                square_x(q, 3)
                for b in range(NB):
                    x_hi(q, b)
                    split_hi(q, b)
                split_hi(q, 4)
                split_hi(q, 5)
                for t in range(6):
                    evac_T(q, t)
                    split_hi(q, t + 6)
                act.wait_ge(vtr_done.sem, vtr_done.now(q, 0))
                act.wait_ge(carried.sem, carried.now(q, 1))
                act.activation(vtok[:, 1:NB + 1, :], T0[:, :].rearrange("p (b d) -> p b d", b=NB), ACT.Copy).then_inc(v_evac.sem, 1)
                for i in range(8):
                    exps(q, i)
                    evac_G(q, 2 * i)
                    if i:
                        yA_high(q, i - 1)
                    evac_G(q, 2 * i + 1)
                    evac_pt(q, i)
                    if i % 2 == 1:
                        for u in range(3):
                            split_hi(q, 12 + 3 * (i // 2) + u)
                yA_high(q, 7)
                evac_T(q, T_UP1)
                split_hi(q, 24)
                evac_qkT(q, 0)
                ret_out(q, 0)
                evac_qkT(q, 1)
                yR_high(q, 0)
                ret_out(q, 1)
                evac_qkT(q, 2)
                yP_high(q, 0)
                split_hi(q, 25)
                split_hi(q, 26)
                yP_high(q, 1)
                yR_high(q, 1)
                ret_out(q, 2)
                evac_qkT(q, 3)
                yR_high(q, 2)
                ret_out(q, 3)
                square_x2(q, 0)
                yR_high(q, 3)
                for b in range(1, NB):
                    square_x2(q, b)

            def m_final_squares(h):
                for b in range(HB):
                    act.wait_ge(m_acc.sem, m_acc.now((h + 1) * NG - 1, 2 * b + 1))
                    if b:
                        act.wait_ge(m_sq.sem, m_sq.now(h, b - 1))
                    act.activation(sqj[:, :], x2[:, b, :], ACT.Square, scale=D ** -0.5, accum_out=ssum[:, b:b + 1]).then_inc(m_sq.sem, 1)

            for u in (2, 3):
                act.wait_ge(m_st_full[u % 2].sem, m_st_full[u % 2].before(0, 1))
                if u == 2:
                    act.wait_ge(tile_done.sem, tile_done.now(NQ - 1, NT - 1))
                act.activation(ring_hi[:, u, :], stage[:, u % 2, :], ACT.Copy).then_inc(m_whi.sem, 1)
            for h in range(NH):
                for b in range(HB):
                    for j in range(2):
                        act.wait_ge(m_xtr.sem, m_xtr.now(h, 2 * b + j))
                        act.activation(h2T_hi[:, 4 * j:4 * j + 4, b * P:(b + 1) * P],
                                       m_norm_bank(b, j)[:, :].rearrange("p (c t) -> p c t", c=4), ACT.Copy).then_inc(m_xhi.sem, 1)
                if h:
                    m_final_squares(h - 1)
                with act.Fori(0, NG) as g:
                    G = h * NG + g

                    def m_split_hi(u):
                        act.wait_ge(m_st_full[u % 2].sem, m_st_full[u % 2].now(G, u // 2))
                        if u < 2:
                            act.wait_ge(m_down.sem, m_down.before(G, 15))
                        else:
                            act.wait_ge(m_up.sem, m_up.now(G, u))
                        act.activation(ring_hi[:, u, :], stage[:, u % 2, :], ACT.Copy).then_inc(m_whi.sem, 1)

                    def up_relu(t):
                        act.wait_ge(m_up.sem, m_up.now(G, t))
                        if t >= 2:
                            act.wait_ge(m_rsq.sem, m_rsq.now(G, t - 2))
                        else:
                            act.wait_ge(m_rsq.sem, m_rsq.before(G, t + 2))
                        act.activation(relu[:, t % 2, :], up_bank[t][:, :], ACT.Relu).then_inc(m_relu.sem, 1)

                    def up_high(t):
                        act.wait_ge(m_rsq.sem, m_rsq.now(G, t))
                        if t == 0:
                            act.wait_ge(m_down.sem, m_down.before(G, 15))
                        act.activation(u_hi[:, t % 2, 512 * (t // 2):512 * (t // 2) + 512], rsq[:, t % 2, :],
                                       ACT.Copy).then_inc(m_uhi.sem, 1)

                    m_split_hi(0)
                    m_split_hi(1)
                    for t in range(4):
                        up_relu(t)
                        up_high(t)
                    m_split_hi(2)
                    m_split_hi(3)
            m_final_squares(NH - 1)

        @block.vector
        def _(dve):
            for e in (carried, xn_done, xlo_done, m_xlo, x2_evac, sc_done, max_done, nmax_done, sde_done, den_done, rinv_done, pn_done,
                      yAlo_done, rotA_done, qk_done, pm_done, R_done, ss6_done, gate_done, ya_done, y_done, yRlo_done,
                      pooled_done, pool16_done, yPlo_done, m_xn, m_rsq, m_ulo, m_acc, m_fin):
                dve.sem_inc(e.sem, e.primed)
            dve.wait_ge(s_rel, 32)
            dve.tensor_copy(relw, relb.rearrange("p (h a) -> p h a", a=1).to_broadcast([NBUCKET + 1, NQH, P])).then_inc(s_relw, 1)
            for h in range(NQH):
                dve.wait_ge(s_browmm, h + 1)
                dve.tensor_copy(rrow[:, h, :], bank[h][:, 0:384]).then_inc(s_brow, 1)
            dve.wait_ge(s_ident, 64)
            dve.wait_ge(s_const, 16 * 9)
            dve.wait_ge(s_pm, 6)
            dve.tensor_scalar(nsink[:, :], sinkb[:, :], -1.0, None, ALU.mult).then_inc(s_relw, 1)
            dve.wait_ge(s_relw, 2)

            def x_norm(q, b):
                dve.wait_ge(rstd_done.sem, rstd_done.now(q, b))
                if b >= 2:
                    dve.wait_ge(xtr_done.sem, xtr_done.now(q, 2 * b - 3))
                elif b == 0:
                    dve.wait_ge(ytr_done.sem, ytr_done.before(q, 3))
                dve.scalar_tensor_tensor(out=xn[b % 2], in0=xq[:, b, :], scalar=rstd[:, b:b + 1], in1=grow[:, :],
                                         op0=ALU.mult, op1=ALU.mult).then_inc(xn_done.sem, 1)

            def x_lo(q, b):
                for j in range(2):
                    dve.wait_ge(xhi_done.sem, xhi_done.now(q, 2 * b + j))
                    cols = slice(b * P, (b + 1) * P)
                    dve.tensor_tensor(hT_lo[:, 4 * j:4 * j + 4, cols], norm_bank(b, j)[:, :].rearrange("p (c t) -> p c t", c=4),
                                      hT_hi[:, 4 * j:4 * j + 4, cols].bitcast(F32), ALU.subtract).then_inc(xlo_done.sem, 1)

            def scores(q, i):
                b, g, k = i // 2, i % 2, i % 2
                src = bias0 if b == 0 else bias
                dve.wait_ge(s_done.sem, s_done.now(q, i))
                if i == 0:
                    dve.wait_ge(xtr_done.sem, xtr_done.now(q, 7))
                    dve.wait_ge(s_bias, 16 * NQH)
                    dve.tensor_copy(bias0[:, :, P:2 * P], bias[:, :, P:2 * P]).then_inc(carried.sem, 1)
                    dve.wait_ge(carried.sem, carried.now(q, 3))
                elif i >= 2:
                    dve.wait_ge(ptr_done.sem, ptr_done.now(q, i - 2))
                bv = src[:, 3 * g:3 * g + 3, :].rearrange("p h m -> p (h m)")
                dve.scalar_tensor_tensor(out=sc[:, k, 0:512], in0=S0[:, :], scalar=SCALE, in1=bv[:, 0:512],
                                         op0=ALU.mult, op1=ALU.add).then_inc(sc_done.sem, 1)
                dve.scalar_tensor_tensor(out=sc[:, k, 512:768], in0=S1[:, 0:256], scalar=SCALE, in1=bv[:, 512:768],
                                         op0=ALU.mult, op1=ALU.add).then_inc(sc_done.sem, 1)
                dve.wait_ge(sc_done.sem, sc_done.now(q, 2 * i + 1))
                dve.tensor_reduce(rmax[:, k, :], sc[:, k, :].rearrange("p (h m) -> p h m", h=3), AX, ALU.max).then_inc(max_done.sem, 1)
                dve.wait_ge(max_done.sem, max_done.now(q, i))
                dve.scalar_tensor_tensor(out=nmax[:, k, :], in0=rmax[:, k, :], scalar=-1.0, in1=nsink[:, 3 * g:3 * g + 3],
                                         op0=ALU.mult, op1=ALU.min).then_inc(nmax_done.sem, 1)
                dve.wait_ge(nmax_done.sem, nmax_done.now(q, i))
                dve.tensor_tensor(sde[:, k, :], nmax[:, k, :], sinkb[:, 3 * g:3 * g + 3], ALU.add).then_inc(sde_done.sem, 1)

            def softmax(q, i):
                k = i % 2
                dve.wait_ge(exp_done.sem, exp_done.now(q, 4 * i + 3))
                dve.tensor_tensor(rsum[:, k, :], rsum[:, k, :], ses[:, k, :], ALU.add).then_inc(den_done.sem, 1)
                dve.wait_ge(den_done.sem, den_done.now(q, i))
                dve.reciprocal(rinv[:, k, :], rsum[:, k, :]).then_inc(rinv_done.sem, 1)
                dve.wait_ge(rinv_done.sem, rinv_done.now(q, i))
                for h in range(3):
                    v = sc[:, k, 256 * h:256 * h + 256]
                    dve.tensor_scalar(v, v, rinv[:, k, h:h + 1], None, ALU.mult).then_inc(pn_done.sem, 1)

            def yA_low(q, i):
                b, a = i // 2, HEAD * (i % 2)
                dve.wait_ge(yAhi_done.sem, yAhi_done.now(q, i))
                dve.tensor_tensor(yA_lo[a:a + HEAD, :, b * P:(b + 1) * P],
                                  OB[a:a + HEAD, 0:384].rearrange("p (c t) -> p c t", c=3),
                                  yA_hi[a:a + HEAD, :, b * P:(b + 1) * P].bitcast(F32), ALU.subtract).then_inc(yAlo_done.sem, 1)

            def rot_a(q, b):
                dve.wait_ge(rotB_done.sem, rotB_done.now(q, 2 * b + 1))
                v = zt[:, b, 0:768].rearrange("p (h d) -> p h d", h=12)
                dve.tensor_tensor(v, v, cos_of(b).rearrange("p (a d) -> p a d", a=1).to_broadcast([P, 12, HEAD]),
                                  ALU.mult).then_inc(rotA_done.sem, 1)

            def rot_add(q, b):
                dve.wait_ge(rotA_done.sem, rotA_done.now(q, b))
                dve.tensor_tensor(qk[:, :], qk[:, :], zt[:, b, 0:768], ALU.add).then_inc(qk_done.sem, 1)

            def decay_scores(q, b):
                for k in range(2):
                    dve.wait_ge(rs_done.sem, rs_done.now(q, 2 * b + k))
                    if b and k == 0:
                        dve.wait_ge(ro_done.sem, ro_done.now(q, b - 1))
                    dve.tensor_tensor(Pm[:, 384 * k:384 * k + 384], (S0, S1)[k][:, 0:384],
                                      cmask[:, 384 * k:384 * k + 384], ALU.mult).then_inc(pm_done.sem, 1)

            def state(q, b):
                dve.wait_ge(ru_done.sem, ru_done.now(q, b))
                dve.wait_ge(rg_done.sem, rg_done.now(q, b))
                for k in range(2):
                    a = HEAD * k
                    rv = R[a:a + HEAD, :].rearrange("p (c two d) -> p c two d", c=3, two=2)[:, :, k, :]
                    uv = S0[a:a + HEAD, 0:384].rearrange("p (c two d) -> p c two d", c=3, two=2)[:, :, k, :]
                    dve.tensor_tensor(rv, uv, rv, ALU.add).then_inc(R_done.sem, 1)

            def ret_sums(q, b):
                dve.wait_ge(sqr_done.sem, sqr_done.now(q, b))
                dve.tensor_reduce(ss6[:, :], sq.rearrange("p (h d) -> p h d", h=6), AX, ALU.add).then_inc(ss6_done.sem, 1)

            def ret_y(q, b):
                dve.wait_ge(th_done.sem, th_done.now(q, b))
                if b:
                    dve.wait_ge(y_done.sem, y_done.now(q, b - 1))
                dve.scalar_tensor_tensor(out=gate, in0=th, scalar=1.0, in1=zt[:, b, 1152:1536],
                                         op0=ALU.add, op1=ALU.mult).then_inc(gate_done.sem, 1)
                dve.wait_ge(s6_done.sem, s6_done.now(q, b))
                dve.wait_ge(osb_done.sem, osb_done.now(q, b))
                if b:
                    dve.wait_ge(ytr_done.sem, ytr_done.now(q, b - 1))
                dve.tensor_tensor(yv.rearrange("p (h d) -> p h d", h=6), osb_view(b).rearrange("p (h d) -> p h d", h=6),
                                  s6[:, :].rearrange("p (h a) -> p h a", a=1).to_broadcast([P, 6, HEAD]),
                                  ALU.mult).then_inc(ya_done.sem, 1)
                dve.wait_ge(ya_done.sem, ya_done.now(q, b))
                dve.wait_ge(gate_done.sem, gate_done.now(q, b))
                dve.tensor_tensor(yv, yv, gate, ALU.mult).then_inc(y_done.sem, 1)

            def yR_low(q, b):
                dve.wait_ge(yRhi_done.sem, yRhi_done.now(q, b))
                dve.tensor_tensor(hT_lo[:, 0:3, b * P:(b + 1) * P], T0[:, 0:384].rearrange("p (c t) -> p c t", c=3),
                                  hT_hi[:, 0:3, b * P:(b + 1) * P].bitcast(F32), ALU.subtract).then_inc(yRlo_done.sem, 1)

            def pool_first(q, cc):
                if cc == 0:
                    dve.wait_ge(tab_full.sem, tab_full.now(q, 0))
                    dve.wait_ge(mix_done.sem, mix_done.before(q, 1))
                else:
                    dve.wait_ge(mix_done.sem, mix_done.now(q, 0))
                for k in range(2):
                    a = HEAD * k
                    dve.wait_ge(win_done.sem, win_done.now(q, (0, 1, 4, 5)[2 * cc + k]))
                    w = (win_a, win_b)[k]
                    dve.tensor_tensor(p16[a:a + HEAD, :], w[a:a + HEAD, PADW:2 * PADW], icnt_of(cc)[a:a + HEAD, :],
                                       ALU.mult).then_inc(pool16_done.sem, 1)
                    dve.wait_ge(pool16_done.sem, pool16_done.now(q, 4 * cc + 2 * k))
                    dve.tensor_tensor(pooled[a:a + HEAD, 0:PADW], p16[a:a + HEAD, :], up[a:a + HEAD, cc, PADW:2 * PADW],
                                       ALU.subtract).then_inc(pool16_done.sem, 1)

            def pool_rest(q, cc):
                if cc == 0:
                    dve.wait_ge(mix_done.sem, mix_done.before(q, 1))
                else:
                    dve.wait_ge(mix_done.sem, mix_done.now(q, 0))
                for k in range(2):
                    a = HEAD * k
                    dve.wait_ge(win_done.sem, win_done.now(q, (0, 1, 4, 5)[2 * cc + k]))
                    w = (win_a, win_b)[k]
                    dve.scalar_tensor_tensor(out=pooled[a:a + HEAD, PADW:QT], in0=w[a:a + HEAD, 2 * PADW:PADW + QT],
                                             scalar=invw[a:a + HEAD, cc:cc + 1], in1=up[a:a + HEAD, cc, 2 * PADW:PADW + QT],
                                             op0=ALU.mult, op1=ALU.subtract).then_inc(pooled_done.sem, 1)

            def yP_low(q, cc):
                dve.wait_ge(yPhi_done.sem, yPhi_done.now(q, cc))
                dve.scalar_tensor_tensor(out=hT_lo[:, 3 + cc, :], in0=T1[:, :], scalar=pscale[:, cc:cc + 1],
                                         in1=hT_hi[:, 3 + cc, :].bitcast(F32), op0=ALU.mult, op1=ALU.subtract).then_inc(yPlo_done.sem, 1)

            def evac_x2(q, n):
                b, half = (n % 8) // 2, n % 2
                dve.wait_ge(tile_done.sem, tile_done.now(q, T_OA + n))
                if n >= 8:
                    dve.wait_ge(x2_evac.sem, x2_evac.now(q, n - 8))
                v = xq[:, b, 512 * half:512 * half + 512]
                dve.tensor_tensor(v, dense[(T_OA + n) % 3][:, :], v, ALU.add).then_inc(x2_evac.sem, 1)

            with dve.Fori(0, NQ) as q:
                dve.wait_ge(o_done.sem, o_done.before(q, 7))
                dve.wait_ge(pool16_done.sem, pool16_done.before(q, 7))
                dve.wait_ge(z_evac.sem, z_evac.before(q, T_UP1))
                dve.wait_ge(v_evac.sem, v_evac.before(q, 0))
                dve.tensor_copy(kT[:, 0:P], kT[:, QT:QT + P]).then_inc(carried.sem, 1)
                dve.tensor_copy(vtok[:, 0, :], vtok[:, NB, :]).then_inc(carried.sem, 1)
                dve.tensor_copy(up[:, :, 0:PADW], up[:, :, QT:QT + PADW]).then_inc(carried.sem, 1)
                x_norm(q, 0)
                x_norm(q, 1)
                x_lo(q, 0)
                x_norm(q, 2)
                x_lo(q, 1)
                x_norm(q, 3)
                x_lo(q, 2)
                x_lo(q, 3)
                for i in range(8):
                    scores(q, i)
                    softmax(q, i)
                    if i == 1:
                        dve.wait_ge(sc_done.sem, sc_done.now(q, 3))
                        dve.tensor_copy(bias0[:, :, 0:P], bias[:, :, 0:P]).then_inc(carried.sem, 1)
                    if i:
                        yA_low(q, i - 1)
                    if i == 5:
                        rot_a(q, 0)
                        rot_add(q, 0)
                yA_low(q, 7)
                evac_x2(q, 0)
                evac_x2(q, 1)
                decay_scores(q, 0)
                pool_first(q, 0)
                pool_rest(q, 0)
                rot_a(q, 1)
                rot_add(q, 1)
                evac_x2(q, 2)
                state(q, 0)
                ret_sums(q, 0)
                ret_y(q, 0)
                evac_x2(q, 3)
                evac_x2(q, 4)
                decay_scores(q, 1)
                yR_low(q, 0)
                rot_a(q, 2)
                rot_add(q, 2)
                evac_x2(q, 5)
                state(q, 1)
                ret_sums(q, 1)
                ret_y(q, 1)
                evac_x2(q, 6)
                yP_low(q, 0)
                pool_first(q, 1)
                pool_rest(q, 1)
                evac_x2(q, 7)
                decay_scores(q, 2)
                yP_low(q, 1)
                yR_low(q, 1)
                rot_a(q, 3)
                rot_add(q, 3)
                evac_x2(q, 8)
                state(q, 2)
                ret_sums(q, 2)
                ret_y(q, 2)
                evac_x2(q, 9)
                decay_scores(q, 3)
                yR_low(q, 2)
                evac_x2(q, 10)
                state(q, 3)
                ret_sums(q, 3)
                ret_y(q, 3)
                evac_x2(q, 11)
                evac_x2(q, 12)
                yR_low(q, 3)
                for n in range(13, 16):
                    evac_x2(q, n)

            def m_norm(h, b):
                dve.wait_ge(m_raw[b % 4].sem, m_raw[b % 4].now(h, b // 4))
                v = xn2[:, b % 4, :]
                dve.scalar_tensor_tensor(out=v, in0=v, scalar=rstd2[:, h * HB + b:h * HB + b + 1], in1=grow2[:, :],
                                         op0=ALU.mult, op1=ALU.mult).then_inc(m_xn.sem, 1)

            def m_low(h, b):
                for j in range(2):
                    dve.wait_ge(m_xhi.sem, m_xhi.now(h, 2 * b + j))
                    cols = slice(b * P, (b + 1) * P)
                    dve.tensor_tensor(h2T_lo[:, 4 * j:4 * j + 4, cols], m_norm_bank(b, j)[:, :].rearrange("p (c t) -> p c t", c=4),
                                      h2T_hi[:, 4 * j:4 * j + 4, cols].bitcast(F32), ALU.subtract).then_inc(m_xlo.sem, 1)

            def m_final(h):
                for b in range(HB):
                    dve.wait_ge(m_rstd.sem, m_rstd.now(h, b))
                    dve.scalar_tensor_tensor(out=x2[:, b, :], in0=x2[:, b, :], scalar=rstd[:, b:b + 1], in1=fg[:, :],
                                             op0=ALU.mult, op1=ALU.mult).then_inc(m_fin.sem, 1)

            dve.wait_ge(fg_full, 32)
            for b in range(4):
                m_norm(0, b)
            for h in range(NH):
                for b in range(HB):
                    m_low(h, b)
                    if b + 4 < HB:
                        m_norm(h, b + 4)
                if h:
                    m_final(h - 1)
                if h + 1 < NH:
                    for b in range(4):
                        m_norm(h + 1, b)
                with dve.Fori(0, NG) as g:
                    G = h * NG + g

                    def square(t):
                        dve.wait_ge(m_relu.sem, m_relu.now(G, t))
                        if t >= 2:
                            dve.wait_ge(m_ulo.sem, m_ulo.now(G, t - 2))
                        else:
                            dve.wait_ge(m_ulo.sem, m_ulo.before(G, t + 2))
                        dve.tensor_tensor(rsq[:, t % 2, :], relu[:, t % 2, :], relu[:, t % 2, :], ALU.mult).then_inc(m_rsq.sem, 1)

                    def up_low(t):
                        dve.wait_ge(m_uhi.sem, m_uhi.now(G, t))
                        cols = slice(512 * (t // 2), 512 * (t // 2) + 512)
                        dve.tensor_tensor(u_lo[:, t % 2, cols], rsq[:, t % 2, :], u_hi[:, t % 2, cols].bitcast(F32),
                                          ALU.subtract).then_inc(m_ulo.sem, 1)

                    for t in range(4):
                        square(t)
                        up_low(t)
                    for n in range(16):
                        dve.wait_ge(m_down.sem, m_down.now(G, n))
                        v = x2[:, n // 2, 512 * (n % 2):512 * (n % 2) + 512]
                        if n % 2 == 0:
                            dve.wait_ge(m_x_full[n // 2].sem, m_x_full[n // 2].now(h, 0))
                        dve.wait_ge(m_acc.sem, m_acc.before(G, n))
                        dve.tensor_tensor(v, down_bank[n % 4][:, :], v, ALU.add).then_inc(m_acc.sem, 1)
            m_final(NH - 1)

        @block.tensor
        def _(pe):
            for e in (xtr_done, tile_done, vtr_done, s_done, ptr_done, o_done, qktr_done, rs_done, ro_done, ru_done,
                      ytr_done, mix_done, m_xtr, m_up, m_down):
                pe.sem_inc(e.sem, e.primed)
            pe.wait_ge(s_rel, 32)
            pe.wait_ge(s_relw, 1)
            for h in range(NQH):
                pe.matmul(bank[h][:, 0:384], relw[:, h, :], oneh, start=True, stop=True).then_inc(s_browmm, 1)
            pe.wait_ge(s_ident, 64)
            pe.wait_ge(s_brow, NQH)

            def three(dst, pairs):
                n = len(pairs)
                for k, (ah, al, bh, bl) in enumerate(pairs):
                    pe.matmul(dst, al, bh, start=(k == 0), stop=False)
                    pe.matmul(dst, ah, bl, start=False, stop=False)
                    last = pe.matmul(dst, ah, bh, start=False, stop=(k == n - 1))
                return last

            def free_bank(q, t):
                back = t - 3 if t >= 3 else t - 3 + NT
                ev, k = (z_evac, back) if back < T_OA else (x2_evac, back - T_OA)
                if t >= 3:
                    pe.wait_ge(ev.sem, ev.now(q, k))
                else:
                    pe.wait_ge(ev.sem, ev.before(q, k))

            def norm_transposes(q, b):
                pe.wait_ge(xn_done.sem, xn_done.now(q, b))
                if b >= 2:
                    pe.wait_ge(xlo_done.sem, xlo_done.now(q, 2 * b - 3))
                elif b == 0:
                    pe.wait_ge(yRlo_done.sem, yRlo_done.before(q, 3))
                    pe.wait_ge(qkT_evac.sem, qkT_evac.before(q, 7))
                else:
                    pe.wait_ge(pm_done.sem, pm_done.before(q, 7))
                    pe.wait_ge(R_done.sem, R_done.before(q, 7))
                for j in range(2):
                    for c in range(4):
                        last = pe.transpose(norm_bank(b, j)[:, c * P:(c + 1) * P], xn[b % 2][:, (4 * j + c) * P:(4 * j + c + 1) * P], ident[:, :])
                    last.then_inc(xtr_done.sem, 1)

            def proj_T(q, t):
                u = t if t < 6 else 18
                s = u % RING
                pe.wait_ge(wlo_done.sem, wlo_done.now(q, u))
                free_bank(q, t)
                wh = ring_hi[:, s, :].rearrange("p (c n) -> p c n", c=C)
                wl = ring_lo[:, s, :].rearrange("p (c n) -> p c n", c=C)
                three(dense[t % 3][:, :], [(wh[:, c, :], wl[:, c, :], hT_hi[:, c, :], hT_lo[:, c, :]) for c in range(C)]
                      ).then_inc(tile_done.sem, 1)

            def proj_G(q, t):
                g, b = t // 4, t % 4
                s = 3 * (g % 2)
                if b == 0:
                    pe.wait_ge(wlo_done.sem, wlo_done.now(q, 6 + 3 * g + 2))
                free_bank(q, T_GROUP + t)
                wh = ring_hi[:, s:s + 3, :].rearrange("p s (c n) -> p c s n", c=C)
                wl = ring_lo[:, s:s + 3, :].rearrange("p s (c n) -> p c s n", c=C)
                tok = slice(b * P, (b + 1) * P)
                three(dense[(T_GROUP + t) % 3][:, 0:384].rearrange("p (s n) -> p s n", s=3),
                      [(hT_hi[:, c, tok], hT_lo[:, c, tok], wh[:, c], wl[:, c]) for c in range(C)]).then_inc(tile_done.sem, 1)

            def out_tile(q, n):
                b, half = (n % 8) // 2, n % 2
                tok, cols = slice(b * P, (b + 1) * P), slice(512 * half, 512 * half + 512)
                if n < 8:
                    pe.wait_ge(yAlo_done.sem, yAlo_done.now(q, 2 * b + 1))
                    srcs = [(yA_hi[:, m, tok], yA_lo[:, m, tok], 19 + m) for m in range(3)]
                else:
                    pe.wait_ge(yRlo_done.sem, yRlo_done.now(q, b))
                    pe.wait_ge(yPlo_done.sem, yPlo_done.now(q, 1))
                    srcs = [(hT_hi[:, m, tok], hT_lo[:, m, tok], 22 + m) for m in range(5)]
                pe.wait_ge(wlo_done.sem, wlo_done.now(q, srcs[-1][2]))
                free_bank(q, T_OA + n)
                three(dense[(T_OA + n) % 3][:, :],
                      [(ah, al, ring_hi[:, u % RING, cols], ring_lo[:, u % RING, cols]) for ah, al, u in srcs]
                      ).then_inc(tile_done.sem, 1)

            def att_scores(q, i):
                b, g = i // 2, i % 2
                a = HEAD * g
                if i == 0:
                    pe.wait_ge(z_evac.sem, z_evac.now(q, 3))
                    pe.wait_ge(xlo_done.sem, xlo_done.now(q, 7))
                else:
                    pe.wait_ge(sc_done.sem, sc_done.now(q, 2 * i - 1))
                for h in range(3):
                    dst = S0[:, 256 * h:256 * h + 256] if h < 2 else S1[:, 0:256]
                    last = pe.matmul(dst, qT[a:a + HEAD, h, b * P:(b + 1) * P], kT[a:a + HEAD, b * P:(b + 2) * P],
                                     start=True, stop=True)
                last.then_inc(s_done.sem, 1)

            def att_transposes(q, i):
                k = i % 2
                pe.wait_ge(pn_done.sem, pn_done.now(q, 3 * i + 2))
                if i == 0:
                    pe.wait_ge(v_evac.sem, v_evac.now(q, 0))
                    pe.wait_ge(xlo_done.sem, xlo_done.now(q, 5))
                else:
                    pe.wait_ge(pt_evac.sem, pt_evac.now(q, 2 * i - 1))
                for half in range(2):
                    for h in range(3):
                        last = pe.transpose((T0, T1)[half][:, h * P:(h + 1) * P],
                                            sc[:, k, 256 * h + P * half:256 * h + P * half + P], ident[:, :])
                last.then_inc(ptr_done.sem, 1)

            def att_out(q, i):
                b, k = i // 2, i % 2
                pe.wait_ge(pt_evac.sem, pt_evac.now(q, 2 * i + 1))
                if i:
                    pe.wait_ge(yAlo_done.sem, yAlo_done.now(q, i - 1))
                else:
                    pe.wait_ge(sqr_done.sem, sqr_done.before(q, 3))
                    pe.wait_ge(osb_done.sem, osb_done.before(q, 3))
                    pe.wait_ge(v_evac.sem, v_evac.now(q, 0))
                for half in range(2):
                    last = pe.matmul(OB[:, 0:384], vtok[:, b + half, :], pt[:, k, 384 * half:384 * half + 384],
                                     start=(half == 0), stop=(half == 1))
                last.then_inc(o_done.sem, 1)

            def qk_transposes(q, b):
                pe.wait_ge(qk_done.sem, qk_done.now(q, b))
                if b == 0:
                    pe.wait_ge(pt_evac.sem, pt_evac.now(q, 15))
                elif b == 1:
                    pe.wait_ge(qkT_evac.sem, qkT_evac.now(q, 1))
                else:
                    pe.wait_ge(yRlo_done.sem, yRlo_done.now(q, b - 2))
                    if b == 3:
                        pe.wait_ge(yPlo_done.sem, yPlo_done.now(q, 1))
                    else:
                        pe.wait_ge(qkT_evac.sem, qkT_evac.now(q, 3))
                for k in range(2):
                    for c in range(3):
                        last = pe.transpose((T0, T1)[k][:, c * P:(c + 1) * P], qk[:, 384 * k + c * P:384 * k + (c + 1) * P], ident[:, :])
                    last.then_inc(qktr_done.sem, 1)

            def ret_scores(q, b):
                pe.wait_ge(qkT_evac.sem, qkT_evac.now(q, 2 * b + 1))
                if b:
                    pe.wait_ge(R_done.sem, R_done.now(q, 2 * b - 1))
                    pe.wait_ge(pm_done.sem, pm_done.now(q, 2 * b - 1))
                else:
                    pe.wait_ge(sc_done.sem, sc_done.now(q, 15))
                for h in range(6):
                    a, c = HEAD * (h % 2), h // 2
                    last = pe.matmul((S0, S1)[h % 2][:, P * c:P * c + P],
                                     qkT[a:a + HEAD, 384 + c * P:384 + (c + 1) * P], qkT[a:a + HEAD, c * P:(c + 1) * P],
                                     start=True, stop=True)
                    if c == 2:
                        last.then_inc(rs_done.sem, 1)

            def ret_outs(q, b):
                pe.wait_ge(pm_done.sem, pm_done.now(q, 2 * b + 1))
                if b:
                    pe.wait_ge(R_done.sem, R_done.now(q, 2 * b - 1))
                    pe.wait_ge(sqr_done.sem, sqr_done.now(q, b - 1))
                else:
                    pe.wait_ge(R_done.sem, R_done.before(q, 7))
                    pe.wait_ge(yAlo_done.sem, yAlo_done.now(q, 7))
                for c in range(3):
                    for h in (2 * c, 2 * c + 1):
                        pe.matmul(OB[:, h * HEAD:(h + 1) * HEAD], Pm[:, (3 * (h % 2) + c) * P:(3 * (h % 2) + c + 1) * P],
                                         zt[:, b, 768 + h * HEAD:768 + (h + 1) * HEAD], start=(h % 2 == 0), stop=False,
                                  skip_group_check=True)
                    last = pe.matmul(OB[:, c * P:(c + 1) * P], qkT[:, c * P:(c + 1) * P], R[:, c * P:(c + 1) * P],
                                     start=False, stop=True, skip_group_check=True)
                last.then_inc(ro_done.sem, 1)
                pe.wait_ge(kz_done.sem, kz_done.now(q, b))
                for c in range(3):
                    last = pe.matmul(S0[:, c * P:(c + 1) * P], kz_view(b)[:, c * P:(c + 1) * P],
                                     zt[:, b, 768 + c * P:768 + (c + 1) * P], start=True, stop=True)
                last.then_inc(ru_done.sem, 1)

            def y_transposes(q, b):
                pe.wait_ge(y_done.sem, y_done.now(q, b))
                pe.wait_ge(qkT_evac.sem, qkT_evac.now(q, 2 * min(b + 1, 3) + 1))
                if b == 3:
                    pe.wait_ge(yRlo_done.sem, yRlo_done.now(q, 2))
                for c in range(3):
                    last = pe.transpose(T0[:, c * P:(c + 1) * P], yv[:, c * P:(c + 1) * P], ident[:, :])
                last.then_inc(ytr_done.sem, 1)

            def pool_mix(q, cc):
                pe.wait_ge(pooled_done.sem, pooled_done.now(q, 2 * cc + 1))
                pe.wait_ge(pool16_done.sem, pool16_done.now(q, 4 * cc + 3))
                if cc == 0:
                    pe.wait_ge(qkT_evac.sem, qkT_evac.now(q, 5))
                else:
                    pe.wait_ge(yPlo_done.sem, yPlo_done.now(q, 0))
                pe.matmul(T1[:, :], poolw[:, cc, :], pooled[:, :], start=True, stop=True).then_inc(mix_done.sem, 1)

            with pe.Fori(0, NQ) as q:
                for b in range(NB):
                    norm_transposes(q, b)
                pe.wait_ge(xlo_done.sem, xlo_done.now(q, 7))
                for t in range(6):
                    proj_T(q, t)
                pe.wait_ge(z_evac.sem, z_evac.now(q, 4))
                for b in range(NB):
                    last = pe.transpose(T0[:, b * P:(b + 1) * P], vT[:, b * P:(b + 1) * P], ident[:, :])
                last.then_inc(vtr_done.sem, 1)
                for i in range(8):
                    att_scores(q, i)
                    proj_G(q, 2 * i)
                    if i:
                        att_out(q, i - 1)
                    proj_G(q, 2 * i + 1)
                    att_transposes(q, i)
                proj_T(q, T_UP1)
                att_out(q, 7)
                qk_transposes(q, 0)
                out_tile(q, 0)
                out_tile(q, 1)
                ret_scores(q, 0)
                out_tile(q, 2)
                ret_outs(q, 0)
                qk_transposes(q, 1)
                out_tile(q, 3)
                out_tile(q, 4)
                ret_scores(q, 1)
                y_transposes(q, 0)
                out_tile(q, 5)
                ret_outs(q, 1)
                qk_transposes(q, 2)
                out_tile(q, 6)
                pool_mix(q, 0)
                out_tile(q, 7)
                ret_scores(q, 2)
                pool_mix(q, 1)
                y_transposes(q, 1)
                out_tile(q, 8)
                ret_outs(q, 2)
                qk_transposes(q, 3)
                out_tile(q, 9)
                ret_scores(q, 3)
                y_transposes(q, 2)
                out_tile(q, 10)
                ret_outs(q, 3)
                out_tile(q, 11)
                out_tile(q, 12)
                y_transposes(q, 3)
                for n in range(13, 16):
                    out_tile(q, n)

            for h in range(NH):
                for b in range(HB):
                    pe.wait_ge(m_xn.sem, m_xn.now(h, b))
                    if b >= 2:
                        pe.wait_ge(m_xlo.sem, m_xlo.now(h, 2 * b - 3))
                    else:
                        pe.wait_ge(m_relu.sem, m_relu.before(h * NG, 3))
                    for j in range(2):
                        for c in range(4):
                            last = pe.transpose(m_norm_bank(b, j)[:, c * P:(c + 1) * P],
                                                xn2[:, b % 4, (4 * j + c) * P:(4 * j + c + 1) * P], ident[:, :])
                        last.then_inc(m_xtr.sem, 1)
                with pe.Fori(0, NG) as g:
                    G = h * NG + g
                    pe.wait_ge(m_xlo.sem, m_xlo.now(h, 2 * HB - 1))
                    for t in range(4):
                        pe.wait_ge(m_relu.sem, m_relu.before(G, t))
                        if t < 2:
                            pe.wait_ge(m_wlo.sem, m_wlo.before(G, 2 + t))
                        cols = slice(512 * (t // 2), 512 * (t // 2) + 512)
                        s = 2 + t % 2
                        wh = ring_hi[:, s, :].rearrange("p (c n) -> p c n", c=C)
                        wl = ring_lo[:, s, :].rearrange("p (c n) -> p c n", c=C)
                        three(up_bank[t][:, :], [(wh[:, c, :], wl[:, c, :], h2T_hi[:, c, cols], h2T_lo[:, c, cols])
                                                 for c in range(C)]).then_inc(m_up.sem, 1)
                    for n in range(16):
                        b, cols = n // 2, slice(512 * (n % 2), 512 * (n % 2) + 512)
                        tok = slice(b * P, (b + 1) * P)
                        if n == 0:
                            pe.wait_ge(m_wlo.sem, m_wlo.now(G, 1))
                            pe.wait_ge(m_ulo.sem, m_ulo.now(G, 1))
                        if n == 8:
                            pe.wait_ge(m_ulo.sem, m_ulo.now(G, 3))
                        if n >= 4:
                            pe.wait_ge(m_acc.sem, m_acc.now(G, n - 4))
                        else:
                            pe.wait_ge(m_acc.sem, m_acc.before(G, n + 12))
                        three(down_bank[n % 4][:, :], [(u_hi[:, k, tok], u_lo[:, k, tok], ring_hi[:, k, cols], ring_lo[:, k, cols])
                                                       for k in range(2)]).then_inc(m_down.sem, 1)


def shape_constants():
    f8 = np.float64
    gamma = 1.0 - 2.0 ** (-5.0 - np.arange(NRET, dtype=f8))
    idx = np.arange(P, dtype=f8)
    c = np.zeros((P, CSTW), np.float32)

    def put(name, v):
        c[:, CST[name][0]:CST[name][1]] = v
    put("ident", np.eye(P))
    mask = np.where(idx[None, None, :] >= idx[:, None, None], gamma[None, :, None] ** -(idx[:, None, None] + 1) * SCALE, 0.0)
    put("mask", np.concatenate([mask[:, 0::2], mask[:, 1::2]], axis=1).reshape(P, -1))
    head = 2 * np.arange(3)[None, :] + (np.arange(P) >= HEAD)[:, None]
    put("gchunk", np.repeat(gamma[head] ** P, P, axis=1))
    put("zeta", SCALE * gamma[None, :] ** (P - 1 - idx[:, None]))
    xi = gamma[None, :] ** (idx[:, None] + 1)
    put("xi2", xi * xi / HEAD)
    put("xih", 0.5 * xi)
    w = np.array(WINDOWS, f8).reshape(2, 2)
    put("invw", np.repeat(1.0 / w.T, HEAD, axis=0))
    put("mhalf", -0.5)
    put("eps", EPS)

    inv = (np.float32(1.0) / (np.float32(10000.0) ** np.linspace(0.0, 1.0, HEAD // 2, dtype=np.float32))).astype(np.float32)
    ang = (np.arange(SEQ, dtype=np.float32)[:, None] * inv[None, :]).astype(f8)
    cos = np.repeat(np.cos(ang), 2, axis=1)
    sin = np.stack([-np.sin(ang), np.sin(ang)], axis=-1).reshape(SEQ, HEAD)
    t = np.zeros((NQ, P, TABW), np.float32)
    t[:, :, 0:NB * HEAD] = cos.reshape(NQ, NB, P, HEAD).transpose(0, 2, 1, 3).reshape(NQ, P, -1)
    t[:, :, NB * HEAD:2 * NB * HEAD] = sin.reshape(NQ, NB, P, HEAD).transpose(0, 2, 1, 3).reshape(NQ, P, -1)
    wp = np.repeat(w, HEAD, axis=1)
    for q in range(NQ):
        cnt = np.minimum(np.arange(PADW)[None, None, :] + 1 + q * QT, wp[:, :, None])
        t[q, :, 2 * NB * HEAD:] = (1.0 / cnt).transpose(1, 0, 2).reshape(P, 32)

    dist = P - (np.arange(384) - (P - 1))
    ok = (dist >= 0) & (dist < P)
    half = NBUCKET // 2
    n = np.maximum(dist, 0)
    large = half + (np.log(np.maximum(n, 1) / half) / np.log(MAXDIST / half) * (NBUCKET - half)).astype(np.int64)
    bucket = np.where(n < half, n, np.minimum(large, NBUCKET - 1))
    one = np.zeros((NBUCKET + 1, 384), np.float32)
    one[bucket[ok], np.arange(384)[ok]] = 1.0
    one[NBUCKET, ~ok] = NEG
    return c, t.reshape(NQ * P, TABW), one


def layout_mixer_weights(w_in, w_out):
    col = 0
    starts = []
    for size in (384, 128, 128, 384, 384, 384, 384, 256):
        starts.append(col)
        col += size
    qa, ka, va, qr, kr, vr, gr, up = starts
    head = [np.arange(h * HEAD, (h + 1) * HEAD) for h in range(NQH)]
    pair = [np.concatenate([head[c], head[c + GROUP]]) for c in range(GROUP)]
    cols = [qa + pair[c] for c in range(GROUP)]
    cols += [s + np.arange(P) for s in (ka, va, up)]
    cols += [s + c * P + np.arange(P) for s in (qr, kr, vr, gr) for c in range(3)]
    cols += [up + P + np.arange(P)]
    units = [w_in[:, k].reshape(C, P, P).transpose(1, 0, 2).reshape(P, C * P) for k in cols]
    rows = [pair[c] for c in range(GROUP)] + [384 + c * P + np.arange(P) for c in range(5)]
    units += [w_out[k, :] for k in rows]
    return np.ascontiguousarray(np.stack(units))


def layout_mlp_weights(w_up, w_down):
    ups = [w_up[:, f * P:(f + 1) * P].reshape(C, P, P).transpose(1, 0, 2).reshape(P, C * P) for f in range(2 * NG)]
    downs = [w_down[f * P:(f + 1) * P, :] for f in range(2 * NG)]
    units = []
    for g in range(NG):
        n = (g + 1) % NG
        units += [downs[2 * g], downs[2 * g + 1], ups[2 * n], ups[2 * n + 1]]
    return np.ascontiguousarray(np.stack(units))


def kernel(x, attn_norm_g, w_in, attn_sinks, rel_bias, pool_w, pool_scale, w_out, mlp_norm_g, w_up, w_down, final_norm_g):
    import concourse.bacc as bacc
    from concourse.bass_utils import run_bass_kernel_spmd

    def a(v):
        return np.asarray(v)

    cst, tab, onehot = shape_constants()
    arrays = {
        "x": a(x).reshape(SEQ, D),
        "wmix": layout_mixer_weights(a(w_in)[0], a(w_out)[0]),
        "wmlp": layout_mlp_weights(a(w_up)[0], a(w_down)[0]),
        "cst": cst, "tab": tab, "onehot": onehot,
        "gmix": a(attn_norm_g).reshape(1, D), "gmlp": a(mlp_norm_g).reshape(1, D),
        "gfin": a(final_norm_g).reshape(1, D), "sinks": a(attn_sinks).reshape(1, NQH), "rel_bias": a(rel_bias),
        "pool_w": a(pool_w)[0], "pool_scale": a(pool_scale).reshape(2, P).T,
    }
    arrays = {f"in_{k}": np.ascontiguousarray(v) for k, v in arrays.items()}
    nc = bacc.Bacc("TRN2", target_bir_lowering=False, num_devices=1)
    args = [nc.dram_tensor(k, v.shape, mybir.dt.from_np(v.dtype), kind="ExternalInput").ap() for k, v in arrays.items()]
    out = nc.dram_tensor("out", (SEQ, D), F32, kind="ExternalOutput").ap()
    build(nc, *args, out)
    got = run_bass_kernel_spmd(nc, [arrays], core_ids=[0])
    return got.results[0]["out"].reshape(1, SEQ, D)
```

```python
from contextlib import ExitStack

import numpy as np

import concourse.bass as bass
from concourse import mybir

P = 128
D = 1024
SEQ = 2048
HEAD = 64
NQH, NRET = 6, 6
GROUP = 3
WINDOWS = (2, 4, 8, 16)
FF = 4 * D
EPS = 1e-6
NEG = -1e30
NBUCKET = 32
MAXDIST = 128
SCALE = HEAD ** -0.5

C = D // P
QT = 512
NQ = SEQ // QT
NB = QT // P
HT = 1024
NH = SEQ // HT
HB = HT // P
RING = 6
STAGE = 3
NU = 27
NG = FF // (2 * P)
TABW = 2 * NB * HEAD + 32
PADW = 16

F32 = mybir.dt.float32
F32R = mybir.dt.float32r
ALU = mybir.AluOpType
ACT = mybir.ActivationFunctionType
AX = mybir.AxisListType.X

CST = {}
_at = 0
for _name, _width in (("ident", P), ("mask", NRET * P), ("gchunk", 3 * P), ("zeta", NRET), ("xi2", NRET),
                      ("xih", NRET), ("invw", 2), ("mhalf", 8), ("eps", 8)):
    CST[_name] = (_at, _at + _width)
    _at += _width
CSTW = _at

T_GROUP, T_UP1, T_OA, T_OR, NT = 6, 22, 23, 31, 39


def last_tile_of_unit(u):
    if u < 6:
        return u
    if u < 18:
        return T_GROUP + 4 * ((u - 6) // 3) + 3
    return T_UP1 if u == 18 else (T_OR - 1 if u < 22 else NT - 1)


SLOT = [3, 4, 5, 0, 1, 2] + 2 * [3, 4, 5, 0, 1, 2] + [4, 5, 3, 0, 1, 2, 4, 5, 0]
M_SLOT = (0, 1, 3, 2)


def slot_owner(u):
    same = [v for v in range(min(u, NU)) if SLOT[v] == SLOT[u % NU]]
    if same:
        return True, same[-1]
    return False, max(v for v in range(NU) if SLOT[v] == SLOT[u])


class Events:

    def __init__(self, sem, per, by=1):
        self.sem, self.per, self.by = sem, per, by

    @property
    def primed(self):
        return self.per * self.by

    def now(self, r, i):
        return r * (self.per * self.by) + (self.per + i + 1) * self.by

    def before(self, r, i):
        return r * (self.per * self.by) + (i + 1) * self.by


def build(nc, x, wmix, wmlp, cst, tab, onehot, gmix, gmlp, gfin, sinks, rel_bias, pool_w, pool_scale, out):
    x2_dram = nc.dram_tensor("x2_dram", (SEQ, D), F32).ap()
    rows_dram = nc.dram_tensor("bias_rows_dram", (NQH, P * 384), F32).ap()

    with ExitStack() as ctx:
        def sb(name, shape, dt=F32, stack=ctx):
            return stack.enter_context(nc.sbuf_tensor(name, shape, dt))

        def ps(name):
            return ctx.enter_context(nc.psum_tensor(name, [P, 512], F32))

        def sem(name):
            return ctx.enter_context(nc.semaphore(name))

        ring_hi = sb("ring_hi", [P, RING, 1024], F32R)
        ring_lo = sb("ring_lo", [P, RING, 1024], F32R)
        stage = sb("stage", [P, STAGE, 1024])
        ident = sb("ident", [P, P])
        mhalf = sb("mhalf", [P, 8])
        epsc = sb("epsc", [P, 8])
        ssum = sb("ssum", [P, 8])
        var = sb("var", [P, 8])
        rstd = sb("rstd", [P, 8])
        ssum2 = sb("ssum2", [P, SEQ // P])
        var2 = sb("var2", [P, SEQ // P])
        rstd2 = sb("rstd2", [P, SEQ // P])

        grow = sb("grow", [P, D])
        with ExitStack() as mem:
            xn = sb("xn", [P, NB, D], F32, mem)

        with ExitStack() as mem:
            def ms(name, shape, dt=F32):
                return sb(name, shape, dt, mem)
            yA_hi = ms("yA_hi", [P, 3, QT], F32R)
            yA_lo = ms("yA_lo", [P, 3, QT], F32R)
            sc = ms("sc", [P, 2, 3 * 2 * P])
            xq = ms("xq", [P, NB, D])
            hT_hi = ms("hT_hi", [P, C, QT], F32R)
            hT_lo = ms("hT_lo", [P, C, QT], F32R)
            qT = ms("qT", [P, 3, QT])
            kT = ms("kT", [P, P + QT])
            vT = ms("vT", [P, QT])
            pooled = vT
            vtok = ms("vtok", [P, NB + 1, P])
            up = ms("up", [P, 2, PADW + QT])
            zt = ms("zt", [P, NB, 4 * 3 * P])
            bias = ms("bias", [P, NQH, 2 * P])
            bias0 = ms("bias0", [P, NQH, 2 * P])
            cmask = ms("cmask", [P, NRET * P])
            gch = ms("gch", [P, 3 * P])
            R = ms("R", [P, 3 * P])
            tabs = ms("tabs", [P, TABW])
            small = ms("small", [P, 32])
            nsink = ms("nsink", [P, NQH])
            sinkb = ms("sinkb", [P, NQH])
            pscale = ms("pscale", [P, 2])
            poolw = ms("poolw", [P, 2, P])
            pt = ms("pt", [P, 2, 2 * 3 * P])
            rmax = ms("rmax", [P, 2, 3])
            nmax = ms("nmax", [P, 2, 3])
            sde = ms("sde", [P, 2, 3])
            ses = ms("ses", [P, 2, 3])
            rsum = ms("rsum", [P, 2, 3])
            rinv = ms("rinv", [P, 2, 3])
            qk = ms("qk", [P, 2, 6 * P])
            junk = ms("junk", [P, D], mybir.dt.bfloat16)
            ss6 = ms("ss6", [P, 6])
            v6 = ms("v6", [P, 6])
            r6 = ms("r6", [P, 6])
            s6 = ms("s6", [P, 6])
            p16 = ms("p16", [P, PADW])
            sc_flat = sc[:, :, :].rearrange("p a b -> p (a b)")
            pt_flat = pt[:, :, :].rearrange("p a b -> p (a b)")
            qkT = sc_flat[:, 0:768]
            Pm = sc_flat[:, 768:1536]
            sq = pt_flat[:, 0:384]
            th = pt_flat[:, 384:768]
            gate = pt_flat[:, 768:1152]
            yv = pt_flat[:, 1152:1536]
            qT_flat = qT[:, :, :].rearrange("p a b -> p (a b)")
            win_a = qT_flat[:, 0:PADW + QT]
            win_b = qT_flat[:, PADW + QT:2 * (PADW + QT)]
            relb = zt[0:NBUCKET + 1, 0, 0:NQH]
            relw = zt[0:NBUCKET + 1, 1, 0:NQH * P].rearrange("p (h m) -> p h m", h=NQH)
            oneh = zt[0:NBUCKET + 1, 0, 64:64 + 384]
            rrow = zt[:, 2:4, :].rearrange("p a b -> p (a b)")[:, 0:NQH * 384].rearrange("p (h m) -> p h m", h=NQH)

        with ExitStack() as mem:
            def ml(name, shape, dt=F32):
                return sb(name, shape, dt, mem)
            ml("xn_place", [P, NB, D])
            sqj = ml("sqj", [P, D], mybir.dt.bfloat16)
            x2 = ml("x2", [P, HB, D])
            h2T_hi = ml("h2T_hi", [P, C, HT], F32R)
            h2T_lo = ml("h2T_lo", [P, C, HT], F32R)
            u_hi = ml("u_hi", [P, 2, HT], F32R)
            u_lo = ml("u_lo", [P, 2, HT], F32R)
            fg = ml("fg", [P, D])
            relu = ml("relu", [P, 2, QT])
            rsq = ml("rsq", [P, 2, QT])

        bank = [ps(f"bank{i}") for i in range(8)]
        dense = bank[0:3]
        S0, S1, T0, T1, OB = bank[3], bank[4], bank[5], bank[6], bank[7]
        up_bank = bank[4:8]
        down_bank = bank[0:4]

        s_const = sem("s_const")
        s_ident = sem("s_ident")
        s_gain = sem("s_gain")
        s_rel = sem("s_rel")
        s_relw = sem("s_relw")
        s_browmm = sem("s_browmm")
        s_brow = sem("s_brow")
        s_rowst = sem("s_rowst")
        s_bias = sem("s_bias")
        s_init = sem("s_init")
        s_pm = sem("s_pm")

        xq_full = [Events(sem(f"xq_full{b}"), 1, 16) for b in range(NB)]
        x_full = [Events(sem(f"x_full{b}"), 1, 16) for b in range(NB)]
        x2_stored = [Events(sem(f"x2_stored{b}"), 1, 16) for b in range(NB)]
        tab_full = Events(sem("tab_full"), 1, 16)
        st_full = [Events(sem(f"st_full{s}"), NU // STAGE, 16) for s in range(STAGE)]
        sq_done = Events(sem("sq_done"), 4)
        var_done = Events(sem("var_done"), 4)
        rstd_done = Events(sem("rstd_done"), 4)
        xn_done = Events(sem("xn_done"), 4)
        xtr_done = Events(sem("xtr_done"), 8)
        xhi_done = Events(sem("xhi_done"), 8)
        xlo_done = Events(sem("xlo_done"), 8)
        whi_done = Events(sem("whi_done"), NU)
        wlo_done = Events(sem("wlo_done"), NU)
        tile_done = Events(sem("tile_done"), NT)
        z_evac = Events(sem("z_evac"), T_OA)
        x2_evac = Events(sem("x2_evac"), NT - T_OA)
        carried = Events(sem("carried"), 5)
        vtr_done = Events(sem("vtr_done"), 1)
        v_evac = Events(sem("v_evac"), 1)
        s_done = Events(sem("s_done"), 8)
        sc_done = Events(sem("sc_done"), 16)
        max_done = Events(sem("max_done"), 8)
        nmax_done = Events(sem("nmax_done"), 8)
        sde_done = Events(sem("sde_done"), 8)
        exp_done = Events(sem("exp_done"), 32)
        den_done = Events(sem("den_done"), 8)
        rinv_done = Events(sem("rinv_done"), 8)
        pn_done = Events(sem("pn_done"), 24)
        ptr_done = Events(sem("ptr_done"), 8)
        pt_evac = Events(sem("pt_evac"), 16)
        o_done = Events(sem("o_done"), 8)
        yAhi_done = Events(sem("yAhi_done"), 8)
        yAlo_done = Events(sem("yAlo_done"), 8)
        rotA_done = Events(sem("rotA_done"), 4)
        rotB_done = Events(sem("rotB_done"), 8)
        qk_done = Events(sem("qk_done"), 4)
        kz_done = Events(sem("kz_done"), 4)
        qktr_done = Events(sem("qktr_done"), 8)
        qkT_evac = Events(sem("qkT_evac"), 8)
        rs_done = Events(sem("rs_done"), 8)
        pm_done = Events(sem("pm_done"), 8)
        ro_done = Events(sem("ro_done"), 4)
        ru_done = Events(sem("ru_done"), 4)
        rg_done = Events(sem("rg_done"), 4)
        R_done = Events(sem("R_done"), 8)
        osb_done = Events(sem("osb_done"), 4)
        sqr_done = Events(sem("sqr_done"), 4)
        th_done = Events(sem("th_done"), 4)
        ss6_done = Events(sem("ss6_done"), 4)
        v6_done = Events(sem("v6_done"), 8)
        r6_done = Events(sem("r6_done"), 4)
        s6_done = Events(sem("s6_done"), 4)
        gate_done = Events(sem("gate_done"), 4)
        ya_done = Events(sem("ya_done"), 4)
        y_done = Events(sem("y_done"), 4)
        ytr_done = Events(sem("ytr_done"), 4)
        yRhi_done = Events(sem("yRhi_done"), 4)
        yRlo_done = Events(sem("yRlo_done"), 4)
        win_done = Events(sem("win_done"), 6)
        pool16_done = Events(sem("pool16_done"), 8)
        pooled_done = Events(sem("pooled_done"), 4)
        mix_done = Events(sem("mix_done"), 2)
        yPhi_done = Events(sem("yPhi_done"), 2)
        yPlo_done = Events(sem("yPlo_done"), 2)
        fg_full = sem("fg_full")
        gain2_full = sem("gain2_full")
        m_x_full = [Events(sem(f"m_x_full{b}"), 1, 16) for b in range(HB)]
        m_out = [Events(sem(f"m_out{b}"), 1, 16) for b in range(HB)]
        m_st_full = [Events(sem(f"m_st_full{s}"), 2, 16) for s in range(2)]
        sq2_done = Events(sem("sq2_done"), NB)
        var2_done = Events(sem("var2_done"), NB)
        rstd2_done = Events(sem("rstd2_done"), NB)
        m_raw = [Events(sem(f"m_raw{k}"), 2, 16) for k in range(4)]
        m_sq = Events(sem("m_sq"), HB)
        m_var = Events(sem("m_var"), HB)
        m_rstd = Events(sem("m_rstd"), HB)
        m_xn = Events(sem("m_xn"), HB)
        m_xtr = Events(sem("m_xtr"), 2 * HB)
        m_xhi = Events(sem("m_xhi"), 2 * HB)
        m_xlo = Events(sem("m_xlo"), 2 * HB)
        m_whi = Events(sem("m_whi"), 4)
        m_wlo = Events(sem("m_wlo"), 4)
        m_up = Events(sem("m_up"), 4)
        m_relu = Events(sem("m_relu"), 4)
        m_rsq = Events(sem("m_rsq"), 4)
        m_uhi = Events(sem("m_uhi"), 4)
        m_ulo = Events(sem("m_ulo"), 4)
        m_down = Events(sem("m_down"), 16)
        m_acc = Events(sem("m_acc"), 16)
        m_fin = Events(sem("m_fin"), HB)

        def norm_bank(b, j):
            return ((T0, T1), (S0, S1), (dense[1], dense[2]), (OB, T0))[b][j]

        M_NORM_BANK = ((0, 1), (2, 3), (6, 7), (5, 0), (6, 7), (2, 3), (0, 1), (2, 3))

        def m_norm_bank(b, j):
            return bank[M_NORM_BANK[b][j]]

        def cview(name):
            a, b = CST[name]
            return cst[:, a:b]

        zeta = small[:, 0:6]
        xi2 = small[:, 6:12]
        xih = small[:, 12:18]
        invw = small[:, 18:20]

        def kz_view(b):
            return zt[:, b, 384:768]

        def osb_view(b):
            return zt[:, b, 0:384]

        def cos_of(b):
            return tabs[:, b * HEAD:(b + 1) * HEAD]

        def sin_of(b):
            return tabs[:, NB * HEAD + b * HEAD:NB * HEAD + (b + 1) * HEAD]

        def icnt_of(cc):
            return tabs[:, 2 * NB * HEAD + 16 * cc:2 * NB * HEAD + 16 * cc + 16]

        block = ctx.enter_context(nc.Block())

        @block.sync
        def _(sp):
            for e in m_out:
                sp.sem_inc(e.sem, e.primed)
            for e in [tab_full, *x_full, *st_full, *m_x_full, *m_raw]:
                sp.sem_inc(e.sem, e.primed)
            for e in m_st_full:
                sp.sem_inc(e.sem, 16)
            sp.dma_start(xn[:, 0, :], x[0:P, :]).then_inc(x_full[0].sem, 16)
            sp.dma_start(oneh, onehot).then_inc(s_rel, 16)
            sp.wait_ge(s_init, 1)
            sp.dma_start(relb[0:NBUCKET, :], rel_bias).then_inc(s_rel, 16)
            sp.dma_start(mhalf[:, :], cview("mhalf")).then_inc(s_ident, 16)
            sp.dma_start(epsc[:, :], cview("eps")).then_inc(s_ident, 16)
            sp.dma_start(ident[:, :], cview("ident")).then_inc(s_ident, 16)
            sp.dma_start(grow[:, :], gmix.to_broadcast([P, D])).then_inc(s_gain, 16)
            for b in range(1, NB):
                sp.dma_start(xn[:, b, :], x[b * P:(b + 1) * P, :]).then_inc(x_full[b].sem, 16)
            for u in range(STAGE):
                sp.dma_start(stage[:, u, :], wmix[u]).then_inc(st_full[u].sem, 16)
            sp.dma_start(cmask[:, :], cview("mask")).then_inc(s_const, 16)
            sp.dma_start(gch[:, :], cview("gchunk")).then_inc(s_const, 16)
            sp.dma_start(small[:, 0:20], cst[:, CST["zeta"][0]:CST["invw"][1]]).then_inc(s_const, 16)
            sp.dma_start(sinkb[:, :], sinks.to_broadcast([P, NQH])).then_inc(s_const, 16)
            sp.dma_start(pscale[:, :], pool_scale).then_inc(s_const, 16)
            sp.wait_ge(s_pm, 1)
            for g in range(4):
                a = HEAD * (g % 2)
                sp.dma_start(poolw[a:a + HEAD, g // 2, a:a + HEAD], pool_w[g]).then_inc(s_const, 16)
            sp.wait_ge(s_brow, NQH)
            sp.dma_start(rows_dram.rearrange("h (p m) -> p h m", m=384), rrow).then_inc(s_rowst, 16)
            sp.wait_ge(s_rowst, 16)
            for h in range(NQH):
                src = rows_dram[h:h + 1, P - 1:P - 1 + P * 383].rearrange("a (p m) -> (a p) m", m=383)
                sp.dma_start(bias[:, h, :], src[:, 0:2 * P]).then_inc(s_bias, 16)

            def mixer_loads(q, last):
                sp.wait_ge(qk_done.sem, qk_done.before(q, 3))
                sp.wait_ge(pool16_done.sem, pool16_done.before(q, 7))
                sp.dma_start(tabs[:, :], tab[bass.ds(q * P, P), :]).then_inc(tab_full.sem, 16)

                def load_weights(u):
                    sp.wait_ge(wlo_done.sem, wlo_done.now(q, u - STAGE))
                    sp.dma_start(stage[:, u % STAGE, :], wmix[u % NU]).then_inc(st_full[u % STAGE].sem, 16)

                for u in range(STAGE, NU if last else NU + 1):
                    load_weights(u)
                if last:
                    sp.wait_ge(xn_done.sem, xn_done.now(q, NB - 1))
                    sp.dma_start(grow[:, :], gmlp.to_broadcast([P, D])).then_inc(gain2_full, 16)
                for b in range(NB):
                    if b == 3 and not last:
                        load_weights(NU + 1)
                        load_weights(NU + 2)
                    if b < 3:
                        sp.wait_ge(tile_done.sem, tile_done.now(q, T_OR - 1))
                    else:
                        sp.wait_ge(ro_done.sem, ro_done.now(q, 3))
                    if last:
                        sp.wait_ge(x2_stored[b].sem, x2_stored[b].now(0, 0))
                        sp.dma_start(xn[:, b, :], x2_dram[b * P:(b + 1) * P, :]).then_inc(m_raw[b].sem, 16)
                    else:
                        sp.dma_start(xn[:, b, :], x[bass.ds(q * QT + (NB + b) * P, P), :]).then_inc(x_full[b].sem, 16)

            with sp.Fori(0, NQ - 1) as q:
                mixer_loads(q, False)
            mixer_loads(NQ - 1, True)

            sp.wait_ge(wlo_done.sem, wlo_done.now(NQ - 1, NU - 1))
            for k in range(2):
                sp.dma_start(stage[:, k, :], wmlp[4 * NG - 2 + k]).then_inc(m_st_full[k].sem, 16)

            def load_raw(h, b):
                hp, bp = (h, b - NB) if b >= NB else (h - 1, b + NB)
                sp.wait_ge(m_xtr.sem, m_xtr.now(hp, 2 * bp + 1))
                sp.dma_start(xn[:, b % NB, :], x2_dram[h * HT + b * P:h * HT + (b + 1) * P, :]).then_inc(m_raw[b % NB].sem, 16)

            def load_x2(h, b):
                sp.wait_ge(m_out[b].sem, m_out[b].before(h, 0))
                sp.dma_start(x2[:, b, :], x2_dram[h * HT + b * P:h * HT + (b + 1) * P, :]).then_inc(m_x_full[b].sem, 16)

            def load_unit(G, u, index):
                if u >= 2:
                    sp.wait_ge(m_wlo.sem, m_wlo.now(G, u - 2))
                else:
                    sp.wait_ge(m_wlo.sem, m_wlo.before(G, u + 2))
                sp.dma_start(stage[:, u % 2, :], wmlp[bass.ds(index, 1)].rearrange("a p n -> (a p) n")).then_inc(m_st_full[u % 2].sem, 16)

            def store_out(h, b):
                sp.wait_ge(m_fin.sem, m_fin.now(h, b))
                sp.dma_start(out[h * HT + b * P:h * HT + (b + 1) * P, :], x2[:, b, :]).then_inc(m_out[b].sem, 16)

            for b in range(NB, HB):
                load_raw(0, b)
            for u in range(2):
                load_unit(0, u, u)
            for b in range(NB):
                sp.wait_ge(x2_stored[b].sem, x2_stored[b].now(NQ - 1, 0))
            for h in range(NH):
                for b in range(HB):
                    load_x2(h, b)
                if h == 0:
                    sp.dma_start(fg[:, :], gfin.to_broadcast([P, D])).then_inc(fg_full, 16)
                if h + 1 < NH:
                    for b in range(NB):
                        load_raw(h + 1, b)
                with sp.Fori(0, NG - 1) as g:
                    for u in (2, 3):
                        load_unit(h * NG + g, u, 4 * g + u)
                    for u in (0, 1):
                        load_unit(h * NG + g + 1, u, 4 * g + 4 + u)
                if h + 1 < NH:
                    for u in (2, 3):
                        load_unit(h * NG + NG - 1, u, 4 * NG - 4 + u)
                    for u in (0, 1):
                        load_unit(h * NG + NG, u, u)
                for b in range(HB):
                    store_out(h, b)
                    if h + 1 < NH and b == 5:
                        load_raw(h + 1, 4)
                        load_raw(h + 1, 5)
                if h + 1 < NH:
                    load_raw(h + 1, 6)
                    load_raw(h + 1, 7)
            for b in range(HB):
                sp.wait_ge(m_out[b].sem, m_out[b].now(NH - 1, 0))

        @block.gpsimd
        def _(pool):
            for e in (wlo_done, rstd_done, rstd2_done, var2_done, m_rstd, var_done, m_var, rotB_done, kz_done,
                      rg_done, v6_done, r6_done, s6_done, win_done):
                pool.sem_inc(e.sem, e.primed)
            pool.sem_inc(m_wlo.sem, 2)
            pool.memset(relb, 1.0).then_inc(s_init, 1)
            pool.memset(poolw[:, :, :], 0.0).then_inc(s_pm, 1)
            pool.memset(kT[:, :], 0.0).then_inc(s_pm, 1)
            pool.memset(vtok[:, :, :], 0.0).then_inc(s_pm, 1)
            pool.memset(up[:, :, :], 0.0).then_inc(s_pm, 1)
            pool.memset(R[:, :], 0.0).then_inc(s_pm, 1)
            pool.memset(bias0[:, :, 0:P], NEG).then_inc(s_pm, 1)
            pool.wait_ge(s_pm, 6)
            pool.wait_ge(s_ident, 48)

            def split_lo(q, u):
                pool.wait_ge(whi_done.sem, whi_done.now(q, u))
                if u == 26:
                    pool.wait_ge(wlo_done.sem, wlo_done.now(q, 25))
                s = SLOT[u % NU]
                pool.tensor_tensor(ring_lo[:, s, :], stage[:, u % STAGE, :], ring_hi[:, s, :].bitcast(F32),
                                   ALU.subtract).then_inc(wlo_done.sem, 1)

            def inv_rms(q, n):
                b = n % NB
                pool.wait_ge(sq_done.sem, sq_done.now(q, n))
                pool.tensor_tensor(var[:, b:b + 1], ssum[:, b:b + 1], epsc[:, 0:1], ALU.add).then_inc(var_done.sem, 1)
                pool.wait_ge(var_done.sem, var_done.now(q, n))
                pool.tensor_tensor(rstd[:, b:b + 1], var[:, b:b + 1], mhalf[:, 0:1], ALU.pow).then_inc(rstd_done.sem, 1)

            def inv_rms2(q, b):
                col = bass.ds(q * NB + b, 1)
                pool.wait_ge(sq2_done.sem, sq2_done.now(q, b))
                pool.tensor_tensor(var2[:, col], ssum2[:, col], epsc[:, 0:1], ALU.add).then_inc(var2_done.sem, 1)
                pool.wait_ge(var2_done.sem, var2_done.now(q, b))
                pool.tensor_tensor(rstd2[:, col], var2[:, col], mhalf[:, 0:1], ALU.pow).then_inc(rstd2_done.sem, 1)

            def rot_b(q, b):
                if b == 0:
                    pool.wait_ge(tab_full.sem, tab_full.now(q, 0))
                    pool.wait_ge(z_evac.sem, z_evac.now(q, T_GROUP + 7))
                if b < 2:
                    pool.wait_ge(kz_done.sem, kz_done.before(q, b + 2))
                    pool.wait_ge(qktr_done.sem, qktr_done.before(q, 2 * b + 5))
                else:
                    pool.wait_ge(kz_done.sem, kz_done.now(q, b - 2))
                    pool.wait_ge(qktr_done.sem, qktr_done.now(q, 2 * b - 3))
                src = zt[:, b, 0:768].rearrange("p (h i two) -> p h i two", h=12, two=2)
                dst = qk[:, b % 2, :].rearrange("p (h i two) -> p h i two", h=12, two=2)
                sn = sin_of(b).rearrange("p (a i two) -> p a i two", a=1, two=2)
                for e in range(2):
                    pool.tensor_tensor(dst[:, :, :, e], src[:, :, :, 1 - e],
                                       sn[:, :, :, e].to_broadcast([P, 12, 32]), ALU.mult).then_inc(rotB_done.sem, 1)

            def kz_of(q, b):
                pool.wait_ge(qk_done.sem, qk_done.now(q, b))
                pool.tensor_tensor(kz_view(b).rearrange("p (h d) -> p h d", h=6),
                                   qk[:, b % 2, 384:768].rearrange("p (h d) -> p h d", h=6),
                                   zeta.rearrange("p (h a) -> p h a", a=1).to_broadcast([P, 6, HEAD]),
                                   ALU.mult).then_inc(kz_done.sem, 1)

            def decay_state(q, b):
                pool.wait_ge(ro_done.sem, ro_done.now(q, b))
                pool.tensor_tensor(R[:, :], R[:, :], gch[:, :], ALU.mult).then_inc(rg_done.sem, 1)

            def ret_scale(q, b):
                pool.wait_ge(ss6_done.sem, ss6_done.now(q, b))
                pool.tensor_tensor(v6[:, :], ss6[:, :], xi2, ALU.mult).then_inc(v6_done.sem, 1)
                pool.wait_ge(v6_done.sem, v6_done.now(q, 2 * b))
                pool.tensor_tensor(v6[:, :], v6[:, :], epsc[:, 0:6], ALU.add).then_inc(v6_done.sem, 1)
                pool.wait_ge(v6_done.sem, v6_done.now(q, 2 * b + 1))
                pool.tensor_tensor(r6[:, :], v6[:, :], mhalf[:, 0:6], ALU.pow).then_inc(r6_done.sem, 1)
                pool.wait_ge(r6_done.sem, r6_done.now(q, b))
                pool.tensor_tensor(s6[:, :], r6[:, :], xih, ALU.mult).then_inc(s6_done.sem, 1)

            def windows(q, cc):
                if cc == 0:
                    pool.wait_ge(s_done.sem, s_done.now(q, 7))
                    pool.wait_ge(z_evac.sem, z_evac.now(q, T_UP1))
                else:
                    pool.wait_ge(pooled_done.sem, pooled_done.now(q, 1))
                    pool.wait_ge(pool16_done.sem, pool16_done.now(q, 3))
                src, n0 = up[:, cc, :], 1
                for n, step in enumerate((1, 2) if cc == 0 else (1, 2, 4, 8)):
                    dst = win_a if n % 2 == 0 else win_b
                    lo = 2 * step - 1
                    if n:
                        pool.wait_ge(win_done.sem, win_done.now(q, 2 * cc + n - 1))
                    pool.tensor_tensor(dst[:, lo:PADW + QT], src[:, lo:PADW + QT],
                                       src[:, lo - step:PADW + QT - step], ALU.add).then_inc(win_done.sem, 1)
                    src = dst

            def mixer_pool(q, last):
                for u in range(1, 6):
                    split_lo(q, u)
                for k in range(6):
                    split_lo(q, k + 6)
                for i in range(8):
                    if i == 5:
                        rot_b(q, 0)
                    if i % 2 == 1:
                        for u in range(3):
                            split_lo(q, 12 + 3 * (i // 2) + u)
                    if i == 6:
                        kz_of(q, 0)
                        rot_b(q, 1)
                split_lo(q, 24)
                windows(q, 0)
                kz_of(q, 1)
                decay_state(q, 0)
                ret_scale(q, 0)
                rot_b(q, 2)
                windows(q, 1)
                decay_state(q, 1)
                kz_of(q, 2)
                ret_scale(q, 1)
                split_lo(q, 26)
                rot_b(q, 3)
                decay_state(q, 2)
                kz_of(q, 3)
                ret_scale(q, 2)
                if not last:
                    for n in range(3):
                        inv_rms(q, NB + n)
                decay_state(q, 3)
                ret_scale(q, 3)
                if not last:
                    split_lo(q, NU)
                inv_rms2(q, 0)
                if not last:
                    inv_rms(q, NB + 3)
                for b in range(1, NB):
                    inv_rms2(q, b)

            for b in range(NB):
                inv_rms(0, b)
            split_lo(0, 0)
            with pool.Fori(0, NQ - 1) as q:
                mixer_pool(q, False)
            mixer_pool(NQ - 1, True)

            def m_split_lo(G, u):
                pool.wait_ge(m_whi.sem, m_whi.now(G, u))
                pool.tensor_tensor(ring_lo[:, M_SLOT[u], :], stage[:, u % 2, :], ring_hi[:, M_SLOT[u], :].bitcast(F32),
                                   ALU.subtract).then_inc(m_wlo.sem, 1)

            for u in (2, 3):
                pool.wait_ge(m_whi.sem, m_whi.before(0, u))
                pool.tensor_tensor(ring_lo[:, M_SLOT[u], :], stage[:, u % 2, :], ring_hi[:, M_SLOT[u], :].bitcast(F32),
                                   ALU.subtract).then_inc(m_wlo.sem, 1)

            for h in range(NH):
                with pool.Fori(0, NG - 1) as g:
                    for u in range(4):
                        m_split_lo(h * NG + g, u)
                for u in range(4 if h + 1 < NH else 2):
                    m_split_lo(h * NG + NG - 1, u)
                for b in range(HB):
                    pool.wait_ge(m_sq.sem, m_sq.now(h, b))
                    pool.tensor_tensor(var[:, b:b + 1], ssum[:, b:b + 1], epsc[:, 0:1], ALU.add).then_inc(m_var.sem, 1)
                    pool.wait_ge(m_var.sem, m_var.now(h, b))
                    pool.tensor_tensor(rstd[:, b:b + 1], var[:, b:b + 1], mhalf[:, 0:1], ALU.pow).then_inc(m_rstd.sem, 1)

        @block.scalar
        def _(act):
            for e in (sq_done, xhi_done, whi_done, z_evac, v_evac, exp_done, pt_evac, yAhi_done, qkT_evac,
                      osb_done, sqr_done, th_done, yRhi_done, yPhi_done, sq2_done, *xq_full, *x2_stored, m_sq, m_xhi, m_relu, m_uhi):
                act.sem_inc(e.sem, e.primed)
            act.sem_inc(m_whi.sem, 2)

            def split_hi(q, u):
                act.wait_ge(st_full[u % STAGE].sem, st_full[u % STAGE].now(q, u // STAGE))
                same, owner = slot_owner(u)
                if same:
                    act.wait_ge(tile_done.sem, tile_done.now(q, last_tile_of_unit(owner)))
                    act.wait_ge(wlo_done.sem, wlo_done.now(q, owner))
                else:
                    act.wait_ge(tile_done.sem, tile_done.before(q, last_tile_of_unit(owner)))
                act.activation(ring_hi[:, SLOT[u % NU], :], stage[:, u % STAGE, :], ACT.Copy).then_inc(whi_done.sem, 1)

            def load_x(q, b):
                act.wait_ge(x2_stored[b].sem, x2_stored[b].before(q, 0))
                act.wait_ge(sq2_done.sem, sq2_done.before(q, b))
                act.dma_start(xq[:, b, :], x[bass.ds(q * QT + b * P, P), :]).then_inc(xq_full[b].sem, 16)

            def square_x(q, n):
                b = n % NB
                act.wait_ge(x_full[b].sem, x_full[b].now(q, n // NB))
                if n == NB + 3:
                    act.wait_ge(sq2_done.sem, sq2_done.now(q, 0))
                elif n == NB:
                    act.wait_ge(sq2_done.sem, sq2_done.before(q, NB - 1))
                    act.wait_ge(sq_done.sem, sq_done.now(q, n - 1))
                elif n:
                    act.wait_ge(sq_done.sem, sq_done.now(q, n - 1))
                act.activation(junk[:, :], xn[:, b, :], ACT.Square, scale=D ** -0.5, accum_out=ssum[:, b:b + 1]).then_inc(sq_done.sem, 1)

            def square_x2(q, b, last):
                act.wait_ge(x2_evac.sem, x2_evac.now(q, 8 + 2 * b + 1))
                act.dma_start(x2_dram[bass.ds(q * QT + b * P, P), :], xq[:, b, :]).then_inc(x2_stored[b].sem, 16)
                if b == 0:
                    act.wait_ge(sq_done.sem, sq_done.now(q, NB - 1 if last else NB + 2))
                    act.wait_ge(sq2_done.sem, sq2_done.before(q, NB - 1))
                else:
                    act.wait_ge(sq2_done.sem, sq2_done.now(q, b - 1))
                    if b == 1 and not last:
                        act.wait_ge(sq_done.sem, sq_done.now(q, NB + 3))
                act.activation(junk[:, :], xq[:, b, :], ACT.Square, scale=D ** -0.5,
                               accum_out=ssum2[:, bass.ds(q * NB + b, 1)]).then_inc(sq2_done.sem, 1)

            def x_hi(q, b):
                for j in range(2):
                    n = 2 * b + j
                    act.wait_ge(xtr_done.sem, xtr_done.now(q, n))
                    if n == 0:
                        act.wait_ge(tile_done.sem, tile_done.before(q, NT - 1))
                    act.activation(hT_hi[:, 4 * j:4 * j + 4, b * P:(b + 1) * P],
                                   norm_bank(b, j)[:, :].rearrange("p (c t) -> p c t", c=4), ACT.Copy).then_inc(xhi_done.sem, 1)

            def evac_T(q, t):
                act.wait_ge(tile_done.sem, tile_done.now(q, t))
                src = dense[t % 3][:, :]
                if t < 3:
                    dst = qT[:, t, :]
                elif t == 3:
                    act.wait_ge(carried.sem, carried.now(q, 0))
                    dst = kT[:, P:P + QT]
                elif t == 4:
                    act.wait_ge(mix_done.sem, mix_done.before(q, 1))
                    dst = vT[:, :]
                else:
                    act.wait_ge(carried.sem, carried.now(q, 2))
                    dst = up[:, 0 if t == 5 else 1, PADW:PADW + QT]
                act.activation(dst, src, ACT.Copy).then_inc(z_evac.sem, 1)

            def evac_G(q, t):
                act.wait_ge(tile_done.sem, tile_done.now(q, T_GROUP + t))
                g, b = t // 4, t % 4
                act.activation(zt[:, b, 384 * g:384 * g + 384], dense[(T_GROUP + t) % 3][:, 0:384],
                               ACT.Copy).then_inc(z_evac.sem, 1)

            def exps(q, i):
                b, g = i // 2, i % 2
                k = i % 2
                act.wait_ge(nmax_done.sem, nmax_done.now(q, i))
                for h in range(3):
                    act.activation(sc[:, k, 256 * h:256 * h + 256], sc[:, k, 256 * h:256 * h + 256], ACT.Exp,
                                   bias=nmax[:, k, h:h + 1], accum_out=rsum[:, k, h:h + 1]).then_inc(exp_done.sem, 1)
                act.wait_ge(sde_done.sem, sde_done.now(q, i))
                act.activation(ses[:, k, :], sde[:, k, :], ACT.Exp).then_inc(exp_done.sem, 1)

            def evac_pt(q, i):
                k = i % 2
                act.wait_ge(ptr_done.sem, ptr_done.now(q, i))
                if i >= 2:
                    act.wait_ge(o_done.sem, o_done.now(q, i - 2))
                for half in range(2):
                    act.activation(pt[:, k, 384 * half:384 * half + 384], (T0, T1)[half][:, 0:384],
                                   ACT.Copy).then_inc(pt_evac.sem, 1)

            def yA_high(q, i):
                b, g = i // 2, i % 2
                act.wait_ge(o_done.sem, o_done.now(q, i))
                if i == 0:
                    act.wait_ge(tile_done.sem, tile_done.before(q, T_OR - 1))
                a = HEAD * g
                act.activation(yA_hi[a:a + HEAD, :, b * P:(b + 1) * P],
                               OB[a:a + HEAD, 0:384].rearrange("p (c t) -> p c t", c=3), ACT.Copy).then_inc(yAhi_done.sem, 1)

            def evac_qkT(q, b):
                for k in range(2):
                    act.wait_ge(qktr_done.sem, qktr_done.now(q, 2 * b + k))
                    if k == 0:
                        if b == 0:
                            act.wait_ge(ptr_done.sem, ptr_done.now(q, 7))
                        else:
                            act.wait_ge(ro_done.sem, ro_done.now(q, b - 1))
                    act.activation(qkT[:, 384 * k:384 * k + 384], (T0, T1)[k][:, 0:384], ACT.Copy).then_inc(qkT_evac.sem, 1)

            def ret_out(q, b):
                act.wait_ge(ro_done.sem, ro_done.now(q, b))
                act.wait_ge(qktr_done.sem, qktr_done.now(q, 2 * b + 1))
                if b:
                    act.wait_ge(ya_done.sem, ya_done.now(q, b - 1))
                    act.wait_ge(gate_done.sem, gate_done.now(q, b - 1))
                act.activation(osb_view(b), OB[:, 0:384], ACT.Copy).then_inc(osb_done.sem, 1)
                if b == 0:
                    act.wait_ge(o_done.sem, o_done.now(q, 7))
                act.activation(sq, OB[:, 0:384], ACT.Square).then_inc(sqr_done.sem, 1)
                act.activation(th, zt[:, b, 1152:1536], ACT.Tanh, scale=0.5).then_inc(th_done.sem, 1)

            def yR_high(q, b):
                act.wait_ge(ytr_done.sem, ytr_done.now(q, b))
                act.activation(hT_hi[:, 0:3, b * P:(b + 1) * P], T0[:, 0:384].rearrange("p (c t) -> p c t", c=3),
                               ACT.Copy).then_inc(yRhi_done.sem, 1)

            def yP_high(q, cc):
                act.wait_ge(mix_done.sem, mix_done.now(q, cc))
                act.activation(hT_hi[:, 3 + cc, :], T1[:, :], ACT.Copy, scale=pscale[:, cc:cc + 1]).then_inc(yPhi_done.sem, 1)

            def mixer_act(q, last):
                for b in range(NB):
                    x_hi(q, b)
                split_hi(q, 1)
                split_hi(q, 2)
                for b in range(NB):
                    load_x(q, b)
                split_hi(q, 3)
                split_hi(q, 4)
                split_hi(q, 5)
                for t in range(5):
                    evac_T(q, t)
                    split_hi(q, t + 6)
                exps(q, 0)
                evac_T(q, 5)
                split_hi(q, 11)
                act.wait_ge(vtr_done.sem, vtr_done.now(q, 0))
                act.wait_ge(carried.sem, carried.now(q, 1))
                act.activation(vtok[:, 1:NB + 1, :], T0[:, :].rearrange("p (b d) -> p b d", b=NB), ACT.Copy).then_inc(v_evac.sem, 1)
                for i in range(8):
                    evac_G(q, 2 * i)
                    if i:
                        yA_high(q, i - 1)
                    if i < 7:
                        exps(q, i + 1)
                    evac_G(q, 2 * i + 1)
                    evac_pt(q, i)
                    if i % 2 == 1:
                        for u in range(3):
                            split_hi(q, 12 + 3 * (i // 2) + u)
                yA_high(q, 7)
                evac_T(q, T_UP1)
                split_hi(q, 24)
                evac_qkT(q, 0)
                ret_out(q, 0)
                evac_qkT(q, 1)
                yP_high(q, 0)
                yR_high(q, 0)
                ret_out(q, 1)
                evac_qkT(q, 2)
                split_hi(q, 25)
                yP_high(q, 1)
                split_hi(q, 26)
                yR_high(q, 1)
                ret_out(q, 2)
                evac_qkT(q, 3)
                if not last:
                    square_x(q, NB)
                    square_x(q, NB + 1)
                yR_high(q, 2)
                if not last:
                    square_x(q, NB + 2)
                ret_out(q, 3)
                if not last:
                    split_hi(q, NU)
                square_x2(q, 0, last)
                yR_high(q, 3)
                if not last:
                    square_x(q, NB + 3)
                for b in range(1, NB):
                    square_x2(q, b, last)

            for b in range(NB):
                square_x(0, b)
            split_hi(0, 0)
            with act.Fori(0, NQ - 1) as q:
                mixer_act(q, False)
            mixer_act(NQ - 1, True)

            def m_final_square(h, b):
                act.wait_ge(m_acc.sem, m_acc.now((h + 1) * NG - 1, 2 * b + 1))
                if b:
                    act.wait_ge(m_sq.sem, m_sq.now(h, b - 1))
                act.activation(sqj[:, :], x2[:, b, :], ACT.Square, scale=D ** -0.5, accum_out=ssum[:, b:b + 1]).then_inc(m_sq.sem, 1)

            def m_first_split(u):
                act.wait_ge(m_st_full[u % 2].sem, m_st_full[u % 2].before(0, 1))
                act.activation(ring_hi[:, M_SLOT[u], :], stage[:, u % 2, :], ACT.Copy).then_inc(m_whi.sem, 1)

            def m_split_hi(G, u):
                act.wait_ge(m_st_full[u % 2].sem, m_st_full[u % 2].now(G, u // 2))
                if u < 2:
                    act.wait_ge(m_down.sem, m_down.before(G, 15))
                else:
                    act.wait_ge(m_up.sem, m_up.now(G, u))
                act.activation(ring_hi[:, M_SLOT[u], :], stage[:, u % 2, :], ACT.Copy).then_inc(m_whi.sem, 1)

            def m_hi(h, b):
                for j in range(2):
                    act.wait_ge(m_xtr.sem, m_xtr.now(h, 2 * b + j))
                    act.activation(h2T_hi[:, 4 * j:4 * j + 4, b * P:(b + 1) * P],
                                   m_norm_bank(b, j)[:, :].rearrange("p (c t) -> p c t", c=4), ACT.Copy).then_inc(m_xhi.sem, 1)

            def up_relu(G, t):
                act.wait_ge(m_up.sem, m_up.now(G, t))
                if t >= 2:
                    act.wait_ge(m_rsq.sem, m_rsq.now(G, t - 2))
                else:
                    act.wait_ge(m_rsq.sem, m_rsq.before(G, t + 2))
                act.activation(relu[:, t % 2, :], up_bank[t][:, :], ACT.Relu).then_inc(m_relu.sem, 1)

            def up_high(G, t):
                act.wait_ge(m_rsq.sem, m_rsq.now(G, t))
                if t == 0:
                    act.wait_ge(m_down.sem, m_down.before(G, 15))
                act.activation(u_hi[:, t % 2, 512 * (t // 2):512 * (t // 2) + 512], rsq[:, t % 2, :],
                               ACT.Copy).then_inc(m_uhi.sem, 1)

            def mlp_group_act(G, first=None, last=None):
                m_split_hi(G, 0)
                m_split_hi(G, 1)
                for t in range(4):
                    up_relu(G, t)
                    up_high(G, t)
                    if first is not None and t < 2:
                        m_hi(first, NB + 2 * t)
                        m_hi(first, NB + 2 * t + 1)
                if last != NH - 1:
                    m_split_hi(G, 2)
                    m_split_hi(G, 3)
                if last is not None:
                    for b in range(HB):
                        m_final_square(last, b)

            act.wait_ge(tile_done.sem, tile_done.now(NQ - 1, NT - 1))
            m_first_split(2)
            for h in range(NH):
                m_hi(h, 0)
                m_hi(h, 1)
                if h == 0:
                    m_first_split(3)
                m_hi(h, 2)
                m_hi(h, 3)
                mlp_group_act(h * NG, first=h)
                with act.Fori(1, NG - 1) as g:
                    mlp_group_act(h * NG + g)
                mlp_group_act(h * NG + NG - 1, last=h)

        @block.vector
        def _(dve):
            for e in (carried, xn_done, xlo_done, m_xlo, x2_evac, sc_done, max_done, nmax_done, sde_done, den_done, rinv_done, pn_done,
                      yAlo_done, rotA_done, qk_done, pm_done, R_done, ss6_done, gate_done, ya_done, y_done, yRlo_done,
                      pooled_done, pool16_done, yPlo_done, m_xn, m_rsq, m_ulo, m_acc, m_fin):
                dve.sem_inc(e.sem, e.primed)
            dve.wait_ge(s_rel, 32)
            dve.tensor_copy(relw, relb.rearrange("p (h a) -> p h a", a=1).to_broadcast([NBUCKET + 1, NQH, P])).then_inc(s_relw, 1)
            def x_norm(q, n):
                b = n % NB
                dve.wait_ge(rstd_done.sem, rstd_done.now(q, n))
                dve.scalar_tensor_tensor(out=xn[:, b, :], in0=xn[:, b, :], scalar=rstd[:, b:b + 1], in1=grow[:, :],
                                         op0=ALU.mult, op1=ALU.mult).then_inc(xn_done.sem, 1)

            def x_lo(q, b):
                for j in range(2):
                    dve.wait_ge(xhi_done.sem, xhi_done.now(q, 2 * b + j))
                    cols = slice(b * P, (b + 1) * P)
                    dve.tensor_tensor(hT_lo[:, 4 * j:4 * j + 4, cols], norm_bank(b, j)[:, :].rearrange("p (c t) -> p c t", c=4),
                                      hT_hi[:, 4 * j:4 * j + 4, cols].bitcast(F32), ALU.subtract).then_inc(xlo_done.sem, 1)

            def scores(q, i):
                b, g, k = i // 2, i % 2, i % 2
                src = bias0 if b == 0 else bias
                dve.wait_ge(s_done.sem, s_done.now(q, i))
                if i == 0:
                    dve.wait_ge(xtr_done.sem, xtr_done.now(q, 7))
                    dve.wait_ge(s_bias, 16 * NQH)
                    dve.tensor_copy(bias0[:, :, P:2 * P], bias[:, :, P:2 * P]).then_inc(carried.sem, 1)
                    dve.wait_ge(carried.sem, carried.now(q, 3))
                elif i >= 2:
                    dve.wait_ge(ptr_done.sem, ptr_done.now(q, i - 2))
                bv = src[:, 3 * g:3 * g + 3, :].rearrange("p h m -> p (h m)")
                dve.scalar_tensor_tensor(out=sc[:, k, 0:512], in0=S0[:, :], scalar=SCALE, in1=bv[:, 0:512],
                                         op0=ALU.mult, op1=ALU.add).then_inc(sc_done.sem, 1)
                dve.scalar_tensor_tensor(out=sc[:, k, 512:768], in0=S1[:, 0:256], scalar=SCALE, in1=bv[:, 512:768],
                                         op0=ALU.mult, op1=ALU.add).then_inc(sc_done.sem, 1)
                dve.wait_ge(sc_done.sem, sc_done.now(q, 2 * i + 1))
                dve.tensor_reduce(rmax[:, k, :], sc[:, k, :].rearrange("p (h m) -> p h m", h=3), AX, ALU.max).then_inc(max_done.sem, 1)
                dve.wait_ge(max_done.sem, max_done.now(q, i))
                dve.scalar_tensor_tensor(out=nmax[:, k, :], in0=rmax[:, k, :], scalar=-1.0, in1=nsink[:, 3 * g:3 * g + 3],
                                         op0=ALU.mult, op1=ALU.min).then_inc(nmax_done.sem, 1)
                dve.wait_ge(nmax_done.sem, nmax_done.now(q, i))
                dve.tensor_tensor(sde[:, k, :], nmax[:, k, :], sinkb[:, 3 * g:3 * g + 3], ALU.add).then_inc(sde_done.sem, 1)

            def softmax(q, i):
                k = i % 2
                dve.wait_ge(exp_done.sem, exp_done.now(q, 4 * i + 3))
                dve.tensor_tensor(rsum[:, k, :], rsum[:, k, :], ses[:, k, :], ALU.add).then_inc(den_done.sem, 1)
                dve.wait_ge(den_done.sem, den_done.now(q, i))
                dve.reciprocal(rinv[:, k, :], rsum[:, k, :]).then_inc(rinv_done.sem, 1)
                dve.wait_ge(rinv_done.sem, rinv_done.now(q, i))
                for h in range(3):
                    v = sc[:, k, 256 * h:256 * h + 256]
                    dve.tensor_scalar(v, v, rinv[:, k, h:h + 1], None, ALU.mult).then_inc(pn_done.sem, 1)

            def yA_low(q, i):
                b, a = i // 2, HEAD * (i % 2)
                dve.wait_ge(yAhi_done.sem, yAhi_done.now(q, i))
                dve.tensor_tensor(yA_lo[a:a + HEAD, :, b * P:(b + 1) * P],
                                  OB[a:a + HEAD, 0:384].rearrange("p (c t) -> p c t", c=3),
                                  yA_hi[a:a + HEAD, :, b * P:(b + 1) * P].bitcast(F32), ALU.subtract).then_inc(yAlo_done.sem, 1)

            def rot_a(q, b):
                dve.wait_ge(rotB_done.sem, rotB_done.now(q, 2 * b + 1))
                v = zt[:, b, 0:768].rearrange("p (h d) -> p h d", h=12)
                dve.tensor_tensor(v, v, cos_of(b).rearrange("p (a d) -> p a d", a=1).to_broadcast([P, 12, HEAD]),
                                  ALU.mult).then_inc(rotA_done.sem, 1)

            def rot_add(q, b):
                dve.wait_ge(rotA_done.sem, rotA_done.now(q, b))
                dve.tensor_tensor(qk[:, b % 2, :], qk[:, b % 2, :], zt[:, b, 0:768], ALU.add).then_inc(qk_done.sem, 1)

            def decay_scores(q, b):
                for k in range(2):
                    dve.wait_ge(rs_done.sem, rs_done.now(q, 2 * b + k))
                    if b and k == 0:
                        dve.wait_ge(ro_done.sem, ro_done.now(q, b - 1))
                    dve.tensor_tensor(Pm[:, 384 * k:384 * k + 384], (S0, S1)[k][:, 0:384],
                                      cmask[:, 384 * k:384 * k + 384], ALU.mult).then_inc(pm_done.sem, 1)

            def state(q, b):
                dve.wait_ge(ru_done.sem, ru_done.now(q, b))
                dve.wait_ge(rg_done.sem, rg_done.now(q, b))
                for k in range(2):
                    a = HEAD * k
                    rv = R[a:a + HEAD, :].rearrange("p (c two d) -> p c two d", c=3, two=2)[:, :, k, :]
                    uv = S0[a:a + HEAD, 0:384].rearrange("p (c two d) -> p c two d", c=3, two=2)[:, :, k, :]
                    dve.tensor_tensor(rv, uv, rv, ALU.add).then_inc(R_done.sem, 1)

            def ret_sums(q, b):
                dve.wait_ge(sqr_done.sem, sqr_done.now(q, b))
                dve.tensor_reduce(ss6[:, :], sq.rearrange("p (h d) -> p h d", h=6), AX, ALU.add).then_inc(ss6_done.sem, 1)

            def ret_y(q, b):
                dve.wait_ge(th_done.sem, th_done.now(q, b))
                if b:
                    dve.wait_ge(y_done.sem, y_done.now(q, b - 1))
                dve.scalar_tensor_tensor(out=gate, in0=th, scalar=1.0, in1=zt[:, b, 1152:1536],
                                         op0=ALU.add, op1=ALU.mult).then_inc(gate_done.sem, 1)
                dve.wait_ge(s6_done.sem, s6_done.now(q, b))
                dve.wait_ge(osb_done.sem, osb_done.now(q, b))
                if b:
                    dve.wait_ge(ytr_done.sem, ytr_done.now(q, b - 1))
                dve.tensor_tensor(yv.rearrange("p (h d) -> p h d", h=6), osb_view(b).rearrange("p (h d) -> p h d", h=6),
                                  s6[:, :].rearrange("p (h a) -> p h a", a=1).to_broadcast([P, 6, HEAD]),
                                  ALU.mult).then_inc(ya_done.sem, 1)
                dve.wait_ge(ya_done.sem, ya_done.now(q, b))
                dve.wait_ge(gate_done.sem, gate_done.now(q, b))
                dve.tensor_tensor(yv, yv, gate, ALU.mult).then_inc(y_done.sem, 1)

            def yR_low(q, b):
                dve.wait_ge(yRhi_done.sem, yRhi_done.now(q, b))
                dve.tensor_tensor(hT_lo[:, 0:3, b * P:(b + 1) * P], T0[:, 0:384].rearrange("p (c t) -> p c t", c=3),
                                  hT_hi[:, 0:3, b * P:(b + 1) * P].bitcast(F32), ALU.subtract).then_inc(yRlo_done.sem, 1)

            def pool_first(q, cc):
                if cc == 0:
                    dve.wait_ge(tab_full.sem, tab_full.now(q, 0))
                    dve.wait_ge(mix_done.sem, mix_done.before(q, 1))
                else:
                    dve.wait_ge(mix_done.sem, mix_done.now(q, 0))
                for k in range(2):
                    a = HEAD * k
                    dve.wait_ge(win_done.sem, win_done.now(q, (0, 1, 4, 5)[2 * cc + k]))
                    w = (win_a, win_b)[k]
                    dve.tensor_tensor(p16[a:a + HEAD, :], w[a:a + HEAD, PADW:2 * PADW], icnt_of(cc)[a:a + HEAD, :],
                                       ALU.mult).then_inc(pool16_done.sem, 1)
                    dve.wait_ge(pool16_done.sem, pool16_done.now(q, 4 * cc + 2 * k))
                    dve.tensor_tensor(pooled[a:a + HEAD, 0:PADW], p16[a:a + HEAD, :], up[a:a + HEAD, cc, PADW:2 * PADW],
                                       ALU.subtract).then_inc(pool16_done.sem, 1)

            def pool_rest(q, cc):
                if cc == 0:
                    dve.wait_ge(mix_done.sem, mix_done.before(q, 1))
                else:
                    dve.wait_ge(mix_done.sem, mix_done.now(q, 0))
                for k in range(2):
                    a = HEAD * k
                    dve.wait_ge(win_done.sem, win_done.now(q, (0, 1, 4, 5)[2 * cc + k]))
                    w = (win_a, win_b)[k]
                    dve.scalar_tensor_tensor(out=pooled[a:a + HEAD, PADW:QT], in0=w[a:a + HEAD, 2 * PADW:PADW + QT],
                                             scalar=invw[a:a + HEAD, cc:cc + 1], in1=up[a:a + HEAD, cc, 2 * PADW:PADW + QT],
                                             op0=ALU.mult, op1=ALU.subtract).then_inc(pooled_done.sem, 1)

            def yP_low(q, cc):
                dve.wait_ge(yPhi_done.sem, yPhi_done.now(q, cc))
                dve.scalar_tensor_tensor(out=hT_lo[:, 3 + cc, :], in0=T1[:, :], scalar=pscale[:, cc:cc + 1],
                                         in1=hT_hi[:, 3 + cc, :].bitcast(F32), op0=ALU.mult, op1=ALU.subtract).then_inc(yPlo_done.sem, 1)

            def evac_x2(q, n):
                b, half = (n % 8) // 2, n % 2
                dve.wait_ge(tile_done.sem, tile_done.now(q, T_OA + n))
                if n >= 8:
                    dve.wait_ge(x2_evac.sem, x2_evac.now(q, n - 8))
                else:
                    dve.wait_ge(xq_full[b].sem, xq_full[b].now(q, 0))
                v = xq[:, b, 512 * half:512 * half + 512]
                dve.tensor_tensor(v, dense[(T_OA + n) % 3][:, :], v, ALU.add).then_inc(x2_evac.sem, 1)

            def m_norm(h, b):
                dve.wait_ge(m_raw[b % 4].sem, m_raw[b % 4].now(h, b // 4))
                v = xn[:, b % NB, :]
                dve.scalar_tensor_tensor(out=v, in0=v, scalar=rstd2[:, h * HB + b:h * HB + b + 1], in1=grow[:, :],
                                         op0=ALU.mult, op1=ALU.mult).then_inc(m_xn.sem, 1)

            def split_lo_25(q):
                dve.wait_ge(whi_done.sem, whi_done.now(q, 25))
                dve.wait_ge(wlo_done.sem, wlo_done.now(q, 24))
                dve.tensor_tensor(ring_lo[:, SLOT[25], :], stage[:, 25 % STAGE, :], ring_hi[:, SLOT[25], :].bitcast(F32),
                                  ALU.subtract).then_inc(wlo_done.sem, 1)

            def norm_ahead(q, b, last):
                if not last:
                    x_norm(q, NB + b)
                else:
                    if b == 0:
                        dve.wait_ge(gain2_full, 16)
                    m_norm(0, b)

            def mixer_dve(q, last):
                for b in range(NB):
                    x_lo(q, b)
                dve.wait_ge(o_done.sem, o_done.before(q, 7))
                dve.wait_ge(pool16_done.sem, pool16_done.before(q, 7))
                dve.wait_ge(z_evac.sem, z_evac.before(q, T_UP1))
                dve.wait_ge(v_evac.sem, v_evac.before(q, 0))
                dve.tensor_copy(kT[:, 0:P], kT[:, QT:QT + P]).then_inc(carried.sem, 1)
                dve.tensor_copy(vtok[:, 0, :], vtok[:, NB, :]).then_inc(carried.sem, 1)
                dve.tensor_copy(up[:, :, 0:PADW], up[:, :, QT:QT + PADW]).then_inc(carried.sem, 1)
                scores(q, 0)
                for i in range(8):
                    softmax(q, i)
                    if i:
                        yA_low(q, i - 1)
                    if i < 7:
                        scores(q, i + 1)
                    if i == 1:
                        dve.wait_ge(sc_done.sem, sc_done.now(q, 3))
                        dve.tensor_copy(bias0[:, :, 0:P], bias[:, :, 0:P]).then_inc(carried.sem, 1)
                    if i == 6:
                        rot_a(q, 0)
                        rot_add(q, 0)
                yA_low(q, 7)
                evac_x2(q, 0)
                rot_a(q, 1)
                rot_add(q, 1)
                evac_x2(q, 1)
                decay_scores(q, 0)
                evac_x2(q, 2)
                pool_first(q, 0)
                pool_rest(q, 0)
                state(q, 0)
                ret_sums(q, 0)
                ret_y(q, 0)
                evac_x2(q, 3)
                evac_x2(q, 4)
                decay_scores(q, 1)
                yP_low(q, 0)
                yR_low(q, 0)
                rot_a(q, 2)
                rot_add(q, 2)
                evac_x2(q, 5)
                state(q, 1)
                pool_first(q, 1)
                pool_rest(q, 1)
                ret_sums(q, 1)
                evac_x2(q, 6)
                evac_x2(q, 7)
                split_lo_25(q)
                ret_y(q, 1)
                yP_low(q, 1)
                decay_scores(q, 2)
                yR_low(q, 1)
                rot_a(q, 3)
                rot_add(q, 3)
                evac_x2(q, 8)
                state(q, 2)
                ret_sums(q, 2)
                ret_y(q, 2)
                evac_x2(q, 9)
                decay_scores(q, 3)
                yR_low(q, 2)
                evac_x2(q, 10)
                state(q, 3)
                ret_sums(q, 3)
                ret_y(q, 3)
                evac_x2(q, 11)
                norm_ahead(q, 0, last)
                evac_x2(q, 12)
                yR_low(q, 3)
                norm_ahead(q, 1, last)
                evac_x2(q, 13)
                norm_ahead(q, 2, last)
                evac_x2(q, 14)
                norm_ahead(q, 3, last)
                evac_x2(q, 15)

            dve.wait_ge(s_pm, 6)
            dve.wait_ge(s_gain, 16)
            for h in range(NQH):
                if h == 4:
                    x_norm(0, 0)
                dve.wait_ge(s_browmm, h + 1)
                dve.tensor_copy(rrow[:, h, :], bank[h][:, 0:384]).then_inc(s_brow, 1)
            for b in range(1, NB):
                x_norm(0, b)
            dve.wait_ge(s_const, 16 * 9)
            dve.tensor_scalar(nsink[:, :], sinkb[:, :], -1.0, None, ALU.mult).then_inc(s_relw, 1)
            dve.wait_ge(s_relw, 2)
            with dve.Fori(0, NQ - 1) as q:
                mixer_dve(q, False)
            mixer_dve(NQ - 1, True)

            def m_low(h, b):
                for j in range(2):
                    dve.wait_ge(m_xhi.sem, m_xhi.now(h, 2 * b + j))
                    cols = slice(b * P, (b + 1) * P)
                    dve.tensor_tensor(h2T_lo[:, 4 * j:4 * j + 4, cols], m_norm_bank(b, j)[:, :].rearrange("p (c t) -> p c t", c=4),
                                      h2T_hi[:, 4 * j:4 * j + 4, cols].bitcast(F32), ALU.subtract).then_inc(m_xlo.sem, 1)

            def m_final(h, b):
                if b == 0:
                    dve.wait_ge(fg_full, 16)
                dve.wait_ge(m_rstd.sem, m_rstd.now(h, b))
                dve.scalar_tensor_tensor(out=x2[:, b, :], in0=x2[:, b, :], scalar=rstd[:, b:b + 1], in1=fg[:, :],
                                         op0=ALU.mult, op1=ALU.mult).then_inc(m_fin.sem, 1)

            def square(G, t):
                dve.wait_ge(m_relu.sem, m_relu.now(G, t))
                if t >= 2:
                    dve.wait_ge(m_ulo.sem, m_ulo.now(G, t - 2))
                else:
                    dve.wait_ge(m_ulo.sem, m_ulo.before(G, t + 2))
                dve.tensor_tensor(rsq[:, t % 2, :], relu[:, t % 2, :], relu[:, t % 2, :], ALU.mult).then_inc(m_rsq.sem, 1)

            def up_low(G, t):
                dve.wait_ge(m_uhi.sem, m_uhi.now(G, t))
                cols = slice(512 * (t // 2), 512 * (t // 2) + 512)
                dve.tensor_tensor(u_lo[:, t % 2, cols], rsq[:, t % 2, :], u_hi[:, t % 2, cols].bitcast(F32),
                                  ALU.subtract).then_inc(m_ulo.sem, 1)

            def mlp_group_dve(G, first=None, last=None):
                for t in range(4):
                    square(G, t)
                    up_low(G, t)
                    if first is not None and t < 2:
                        m_low(first, NB + 2 * t)
                        m_low(first, NB + 2 * t + 1)
                    if last is not None and last + 1 < NH:
                        m_norm(last + 1, t)
                for n in range(16):
                    b = n // 2
                    dve.wait_ge(m_down.sem, m_down.now(G, n))
                    v = x2[:, b, 512 * (n % 2):512 * (n % 2) + 512]
                    if first is not None and n % 2 == 0:
                        dve.wait_ge(m_x_full[b].sem, m_x_full[b].now(first, 0))
                    dve.wait_ge(m_acc.sem, m_acc.before(G, n))
                    dve.tensor_tensor(v, down_bank[n % 4][:, :], v, ALU.add).then_inc(m_acc.sem, 1)
                    if last is not None and n % 2 == 1 and b:
                        m_final(last, b - 1)
                if last is not None:
                    m_final(last, HB - 1)

            for h in range(NH):
                for b in range(NB):
                    m_low(h, b)
                for b in range(NB, HB):
                    m_norm(h, b)
                mlp_group_dve(h * NG, first=h)
                with dve.Fori(1, NG - 1) as g:
                    mlp_group_dve(h * NG + g)
                mlp_group_dve(h * NG + NG - 1, last=h)

        @block.tensor
        def _(pe):
            for e in (xtr_done, tile_done, vtr_done, s_done, ptr_done, o_done, qktr_done, rs_done, ro_done, ru_done,
                      ytr_done, mix_done, m_xtr, m_up, m_down):
                pe.sem_inc(e.sem, e.primed)
            pe.wait_ge(s_rel, 32)
            pe.wait_ge(s_relw, 1)
            for h in range(NQH):
                pe.matmul(bank[h][:, 0:384], relw[:, h, :], oneh, start=True, stop=True).then_inc(s_browmm, 1)
            pe.wait_ge(s_ident, 48)
            pe.wait_ge(s_brow, NQH)

            def three(dst, pairs, first=True, final=True):
                n = len(pairs)
                for k, (ah, al, bh, bl) in enumerate(pairs):
                    pe.matmul(dst, al, bh, start=(first and k == 0), stop=False)
                    pe.matmul(dst, ah, bl, start=False, stop=False)
                    last = pe.matmul(dst, ah, bh, start=False, stop=(final and k == n - 1))
                return last

            def free_bank(q, t):
                back = t - 3 if t >= 3 else t - 3 + NT
                ev, k = (z_evac, back) if back < T_OA else (x2_evac, back - T_OA)
                if t >= 3:
                    pe.wait_ge(ev.sem, ev.now(q, k))
                else:
                    pe.wait_ge(ev.sem, ev.before(q, k))

            def norm_transposes(q, b):
                pe.wait_ge(xn_done.sem, xn_done.now(q, b))
                for j in range(2):
                    if b == 0 and j == 0:
                        pe.wait_ge(yRlo_done.sem, yRlo_done.before(q, 3))
                    elif b == 0:
                        pe.wait_ge(qkT_evac.sem, qkT_evac.before(q, 7))
                    elif b == 1 and j == 0:
                        pe.wait_ge(R_done.sem, R_done.before(q, 7))
                    elif b == 1:
                        pe.wait_ge(pm_done.sem, pm_done.before(q, 7))
                    elif b == 2:
                        pe.wait_ge(x2_evac.sem, x2_evac.before(q, 14 + j))
                    elif j == 0:
                        pe.wait_ge(sqr_done.sem, sqr_done.before(q, 3))
                        pe.wait_ge(osb_done.sem, osb_done.before(q, 3))
                    else:
                        pe.wait_ge(xlo_done.sem, xlo_done.now(q, 0))
                    for c in range(4):
                        last = pe.transpose(norm_bank(b, j)[:, c * P:(c + 1) * P], xn[:, b, (4 * j + c) * P:(4 * j + c + 1) * P], ident[:, :])
                    last.then_inc(xtr_done.sem, 1)

            def proj_part(t, cols):
                s = SLOT[t if t < 6 else 18]
                wh = ring_hi[:, s, :].rearrange("p (c n) -> p c n", c=C)
                wl = ring_lo[:, s, :].rearrange("p (c n) -> p c n", c=C)
                return three(dense[t % 3][:, cols], [(wh[:, c, :], wl[:, c, :], hT_hi[:, c, cols], hT_lo[:, c, cols])
                                                     for c in range(C)])

            def proj_T(q, t):
                pe.wait_ge(wlo_done.sem, wlo_done.now(q, t if t < 6 else 18))
                free_bank(q, t)
                proj_part(t, slice(0, QT)).then_inc(tile_done.sem, 1)

            def proj_first(q, half):
                if half == 0:
                    pe.wait_ge(wlo_done.sem, wlo_done.now(q, 0))
                    free_bank(q, 0)
                pe.wait_ge(xlo_done.sem, xlo_done.now(q, 4 * half + 3))
                last = proj_part(0, slice(2 * P * half, 2 * P * (half + 1)))
                if half:
                    last.then_inc(tile_done.sem, 1)

            def proj_G(q, t):
                g, b = t // 4, t % 4
                s = SLOT[6 + 3 * g]
                if b == 0:
                    pe.wait_ge(wlo_done.sem, wlo_done.now(q, 6 + 3 * g + 2))
                free_bank(q, T_GROUP + t)
                wh = ring_hi[:, s:s + 3, :].rearrange("p s (c n) -> p c s n", c=C)
                wl = ring_lo[:, s:s + 3, :].rearrange("p s (c n) -> p c s n", c=C)
                tok = slice(b * P, (b + 1) * P)
                three(dense[(T_GROUP + t) % 3][:, 0:384].rearrange("p (s n) -> p s n", s=3),
                      [(hT_hi[:, c, tok], hT_lo[:, c, tok], wh[:, c], wl[:, c]) for c in range(C)]).then_inc(tile_done.sem, 1)

            def out_tile(q, n):
                b, half = (n % 8) // 2, n % 2
                tok, cols = slice(b * P, (b + 1) * P), slice(512 * half, 512 * half + 512)
                if n < 8:
                    pe.wait_ge(yAlo_done.sem, yAlo_done.now(q, 2 * b + 1))
                    srcs = [(yA_hi[:, m, tok], yA_lo[:, m, tok], 19 + m) for m in range(3)]
                else:
                    pe.wait_ge(yRlo_done.sem, yRlo_done.now(q, b))
                    srcs = [(hT_hi[:, m, tok], hT_lo[:, m, tok], 22 + m) for m in range(5)]
                free_bank(q, T_OA + n)
                dst = dense[(T_OA + n) % 3][:, :]
                pairs = [(ah, al, ring_hi[:, SLOT[u], cols], ring_lo[:, SLOT[u], cols]) for ah, al, u in srcs]
                if n == 0:
                    pe.wait_ge(wlo_done.sem, wlo_done.now(q, 21))
                if n == 8:
                    pe.wait_ge(wlo_done.sem, wlo_done.now(q, 24))
                    three(dst, pairs[0:3], final=False)
                else:
                    three(dst, pairs).then_inc(tile_done.sem, 1)

            def out_tile_8_rest(q):
                dst = dense[(T_OA + 8) % 3][:, :]
                pairs = [(hT_hi[:, m, 0:P], hT_lo[:, m, 0:P], ring_hi[:, SLOT[22 + m], 0:512], ring_lo[:, SLOT[22 + m], 0:512])
                         for m in (3, 4)]
                pe.wait_ge(wlo_done.sem, wlo_done.now(q, 25))
                pe.wait_ge(yPlo_done.sem, yPlo_done.now(q, 1))
                three(dst, pairs[0:1], first=False, final=False)
                pe.wait_ge(wlo_done.sem, wlo_done.now(q, 26))
                three(dst, pairs[1:2], first=False).then_inc(tile_done.sem, 1)

            def att_scores(q, i):
                b, g = i // 2, i % 2
                a = HEAD * g
                if i == 0:
                    pe.wait_ge(z_evac.sem, z_evac.now(q, 3))
                    pe.wait_ge(xlo_done.sem, xlo_done.now(q, 7))
                else:
                    pe.wait_ge(sc_done.sem, sc_done.now(q, 2 * i - 1))
                for h in range(3):
                    dst = S0[:, 256 * h:256 * h + 256] if h < 2 else S1[:, 0:256]
                    last = pe.matmul(dst, qT[a:a + HEAD, h, b * P:(b + 1) * P], kT[a:a + HEAD, b * P:(b + 2) * P],
                                     start=True, stop=True)
                last.then_inc(s_done.sem, 1)

            def att_transposes(q, i):
                k = i % 2
                pe.wait_ge(pn_done.sem, pn_done.now(q, 3 * i + 2))
                if i == 0:
                    pe.wait_ge(v_evac.sem, v_evac.now(q, 0))
                    pe.wait_ge(xlo_done.sem, xlo_done.now(q, 7))
                else:
                    pe.wait_ge(pt_evac.sem, pt_evac.now(q, 2 * i - 1))
                for half in range(2):
                    for h in range(3):
                        last = pe.transpose((T0, T1)[half][:, h * P:(h + 1) * P],
                                            sc[:, k, 256 * h + P * half:256 * h + P * half + P], ident[:, :])
                last.then_inc(ptr_done.sem, 1)

            def att_out(q, i):
                b, k = i // 2, i % 2
                pe.wait_ge(pt_evac.sem, pt_evac.now(q, 2 * i + 1))
                if i:
                    pe.wait_ge(yAlo_done.sem, yAlo_done.now(q, i - 1))
                else:
                    pe.wait_ge(sqr_done.sem, sqr_done.before(q, 3))
                    pe.wait_ge(osb_done.sem, osb_done.before(q, 3))
                    pe.wait_ge(v_evac.sem, v_evac.now(q, 0))
                for half in range(2):
                    last = pe.matmul(OB[:, 0:384], vtok[:, b + half, :], pt[:, k, 384 * half:384 * half + 384],
                                     start=(half == 0), stop=(half == 1))
                last.then_inc(o_done.sem, 1)

            def qk_transposes(q, b):
                pe.wait_ge(qk_done.sem, qk_done.now(q, b))
                if b == 0:
                    pe.wait_ge(pt_evac.sem, pt_evac.now(q, 15))
                elif b == 1:
                    pe.wait_ge(qkT_evac.sem, qkT_evac.now(q, 1))
                else:
                    pe.wait_ge(yRlo_done.sem, yRlo_done.now(q, b - 2))
                    pe.wait_ge(yPlo_done.sem, yPlo_done.now(q, b - 2))
                for k in range(2):
                    for c in range(3):
                        last = pe.transpose((T0, T1)[k][:, c * P:(c + 1) * P], qk[:, b % 2, 384 * k + c * P:384 * k + (c + 1) * P], ident[:, :])
                    last.then_inc(qktr_done.sem, 1)

            def ret_scores(q, b):
                pe.wait_ge(qkT_evac.sem, qkT_evac.now(q, 2 * b + 1))
                if b:
                    pe.wait_ge(R_done.sem, R_done.now(q, 2 * b - 1))
                    pe.wait_ge(pm_done.sem, pm_done.now(q, 2 * b - 1))
                else:
                    pe.wait_ge(sc_done.sem, sc_done.now(q, 15))
                for h in range(6):
                    a, c = HEAD * (h % 2), h // 2
                    last = pe.matmul((S0, S1)[h % 2][:, P * c:P * c + P],
                                     qkT[a:a + HEAD, 384 + c * P:384 + (c + 1) * P], qkT[a:a + HEAD, c * P:(c + 1) * P],
                                     start=True, stop=True)
                    if c == 2:
                        last.then_inc(rs_done.sem, 1)

            def ret_outs(q, b):
                pe.wait_ge(pm_done.sem, pm_done.now(q, 2 * b + 1))
                if b:
                    pe.wait_ge(R_done.sem, R_done.now(q, 2 * b - 1))
                    pe.wait_ge(sqr_done.sem, sqr_done.now(q, b - 1))
                else:
                    pe.wait_ge(R_done.sem, R_done.before(q, 7))
                    pe.wait_ge(yAlo_done.sem, yAlo_done.now(q, 7))
                for c in range(3):
                    for h in (2 * c, 2 * c + 1):
                        pe.matmul(OB[:, h * HEAD:(h + 1) * HEAD], Pm[:, (3 * (h % 2) + c) * P:(3 * (h % 2) + c + 1) * P],
                                         zt[:, b, 768 + h * HEAD:768 + (h + 1) * HEAD], start=(h % 2 == 0), stop=False,
                                  skip_group_check=True)
                    last = pe.matmul(OB[:, c * P:(c + 1) * P], qkT[:, c * P:(c + 1) * P], R[:, c * P:(c + 1) * P],
                                     start=False, stop=True, skip_group_check=True)
                last.then_inc(ro_done.sem, 1)
                pe.wait_ge(kz_done.sem, kz_done.now(q, b))
                for c in range(3):
                    last = pe.matmul(S0[:, c * P:(c + 1) * P], kz_view(b)[:, c * P:(c + 1) * P],
                                     zt[:, b, 768 + c * P:768 + (c + 1) * P], start=True, stop=True)
                last.then_inc(ru_done.sem, 1)

            def y_transposes(q, b):
                pe.wait_ge(y_done.sem, y_done.now(q, b))
                pe.wait_ge(qkT_evac.sem, qkT_evac.now(q, 2 * min(b + 1, 3) + 1))
                if b == 3:
                    pe.wait_ge(yRlo_done.sem, yRlo_done.now(q, 2))
                for c in range(3):
                    last = pe.transpose(T0[:, c * P:(c + 1) * P], yv[:, c * P:(c + 1) * P], ident[:, :])
                last.then_inc(ytr_done.sem, 1)

            def pool_mix(q, cc):
                pe.wait_ge(pooled_done.sem, pooled_done.now(q, 2 * cc + 1))
                pe.wait_ge(pool16_done.sem, pool16_done.now(q, 4 * cc + 3))
                pe.wait_ge(qkT_evac.sem, qkT_evac.now(q, 3 + 2 * cc))
                pe.matmul(T1[:, :], poolw[:, cc, :], pooled[:, :], start=True, stop=True).then_inc(mix_done.sem, 1)

            def mixer_pe(q):
                norm_transposes(q, 0)
                norm_transposes(q, 1)
                norm_transposes(q, 2)
                norm_transposes(q, 3)
                proj_first(q, 0)
                proj_first(q, 1)
                for t in range(1, 5):
                    proj_T(q, t)
                att_scores(q, 0)
                proj_T(q, 5)
                pe.wait_ge(z_evac.sem, z_evac.now(q, 4))
                for b in range(NB):
                    last = pe.transpose(T0[:, b * P:(b + 1) * P], vT[:, b * P:(b + 1) * P], ident[:, :])
                last.then_inc(vtr_done.sem, 1)
                for i in range(8):
                    proj_G(q, 2 * i)
                    if i:
                        att_out(q, i - 1)
                    if i < 7:
                        att_scores(q, i + 1)
                    proj_G(q, 2 * i + 1)
                    att_transposes(q, i)
                proj_T(q, T_UP1)
                att_out(q, 7)
                qk_transposes(q, 0)
                out_tile(q, 0)
                out_tile(q, 1)
                ret_scores(q, 0)
                out_tile(q, 2)
                ret_outs(q, 0)
                qk_transposes(q, 1)
                out_tile(q, 3)
                out_tile(q, 4)
                ret_scores(q, 1)
                pool_mix(q, 0)
                y_transposes(q, 0)
                out_tile(q, 5)
                ret_outs(q, 1)
                qk_transposes(q, 2)
                out_tile(q, 6)
                out_tile(q, 7)
                pool_mix(q, 1)
                out_tile(q, 8)
                ret_scores(q, 2)
                y_transposes(q, 1)
                out_tile_8_rest(q)
                ret_outs(q, 2)
                qk_transposes(q, 3)
                out_tile(q, 9)
                ret_scores(q, 3)
                y_transposes(q, 2)
                out_tile(q, 10)
                ret_outs(q, 3)
                out_tile(q, 11)
                out_tile(q, 12)
                y_transposes(q, 3)
                for n in range(13, 16):
                    out_tile(q, n)

            with pe.Fori(0, NQ - 1) as q:
                mixer_pe(q)
            mixer_pe(NQ - 1)

            def m_transposes(h, b):
                pe.wait_ge(m_xn.sem, m_xn.now(h, b))
                if b == 0 and h == 0:
                    pe.wait_ge(x2_evac.sem, x2_evac.now(NQ - 1, 15))
                elif b < 2:
                    pe.wait_ge(m_acc.sem, m_acc.before(h * NG, 13 + 2 * b))
                elif b == 2:
                    pe.wait_ge(m_relu.sem, m_relu.before(h * NG, 3))
                for j in range(2):
                    users = [2 * a + k for a in range(b) for k in range(2) if M_NORM_BANK[a][k] == M_NORM_BANK[b][j]]
                    if users:
                        pe.wait_ge(m_xlo.sem, m_xlo.now(h, users[-1]))
                    for c in range(4):
                        last = pe.transpose(m_norm_bank(b, j)[:, c * P:(c + 1) * P],
                                            xn[:, b % NB, (4 * j + c) * P:(4 * j + c + 1) * P], ident[:, :])
                    last.then_inc(m_xtr.sem, 1)

            def mlp_group_pe(G, first=None):
                for t in range(4):
                    pe.wait_ge(m_relu.sem, m_relu.before(G, t))
                    if t < 2:
                        pe.wait_ge(m_wlo.sem, m_wlo.before(G, 2 + t))
                    s = M_SLOT[2 + t % 2]
                    wh = ring_hi[:, s, :].rearrange("p (c n) -> p c n", c=C)
                    wl = ring_lo[:, s, :].rearrange("p (c n) -> p c n", c=C)
                    parts = 2 if first is not None and t % 2 == 0 else 1
                    for part in range(parts):
                        if parts == 2:
                            pe.wait_ge(m_xlo.sem, m_xlo.now(first, 4 * t + 4 * part + 3))
                        width = 512 // parts
                        dst = slice(width * part, width * (part + 1))
                        cols = slice(512 * (t // 2) + width * part, 512 * (t // 2) + width * (part + 1))
                        last = three(up_bank[t][:, dst], [(wh[:, c, :], wl[:, c, :], h2T_hi[:, c, cols], h2T_lo[:, c, cols])
                                                          for c in range(C)])
                    last.then_inc(m_up.sem, 1)
                    if first is not None and t < 2:
                        m_transposes(first, NB + 2 * t)
                        m_transposes(first, NB + 2 * t + 1)
                for n in range(16):
                    b, cols = n // 2, slice(512 * (n % 2), 512 * (n % 2) + 512)
                    tok = slice(b * P, (b + 1) * P)
                    if n == 0:
                        pe.wait_ge(m_wlo.sem, m_wlo.now(G, 1))
                        pe.wait_ge(m_ulo.sem, m_ulo.now(G, 1))
                    if n == 8:
                        pe.wait_ge(m_ulo.sem, m_ulo.now(G, 3))
                    if n >= 4:
                        pe.wait_ge(m_acc.sem, m_acc.now(G, n - 4))
                    else:
                        pe.wait_ge(m_acc.sem, m_acc.before(G, n + 12))
                    three(down_bank[n % 4][:, :], [(u_hi[:, k, tok], u_lo[:, k, tok], ring_hi[:, M_SLOT[k], cols],
                                                    ring_lo[:, M_SLOT[k], cols]) for k in range(2)]).then_inc(m_down.sem, 1)

            for h in range(NH):
                for b in range(NB):
                    m_transposes(h, b)
                mlp_group_pe(h * NG, first=h)
                with pe.Fori(1, NG) as g:
                    mlp_group_pe(h * NG + g)


def shape_constants():
    f8 = np.float64
    gamma = 1.0 - 2.0 ** (-5.0 - np.arange(NRET, dtype=f8))
    idx = np.arange(P, dtype=f8)
    c = np.zeros((P, CSTW), np.float32)

    def put(name, v):
        c[:, CST[name][0]:CST[name][1]] = v
    put("ident", np.eye(P))
    mask = np.where(idx[None, None, :] >= idx[:, None, None], gamma[None, :, None] ** -(idx[:, None, None] + 1) * SCALE, 0.0)
    put("mask", np.concatenate([mask[:, 0::2], mask[:, 1::2]], axis=1).reshape(P, -1))
    head = 2 * np.arange(3)[None, :] + (np.arange(P) >= HEAD)[:, None]
    put("gchunk", np.repeat(gamma[head] ** P, P, axis=1))
    put("zeta", SCALE * gamma[None, :] ** (P - 1 - idx[:, None]))
    xi = gamma[None, :] ** (idx[:, None] + 1)
    put("xi2", xi * xi / HEAD)
    put("xih", 0.5 * xi)
    w = np.array(WINDOWS, f8).reshape(2, 2)
    put("invw", np.repeat(1.0 / w.T, HEAD, axis=0))
    put("mhalf", -0.5)
    put("eps", EPS)

    inv = (np.float32(1.0) / (np.float32(10000.0) ** np.linspace(0.0, 1.0, HEAD // 2, dtype=np.float32))).astype(np.float32)
    ang = (np.arange(SEQ, dtype=np.float32)[:, None] * inv[None, :]).astype(f8)
    cos = np.repeat(np.cos(ang), 2, axis=1)
    sin = np.stack([-np.sin(ang), np.sin(ang)], axis=-1).reshape(SEQ, HEAD)
    t = np.zeros((NQ, P, TABW), np.float32)
    t[:, :, 0:NB * HEAD] = cos.reshape(NQ, NB, P, HEAD).transpose(0, 2, 1, 3).reshape(NQ, P, -1)
    t[:, :, NB * HEAD:2 * NB * HEAD] = sin.reshape(NQ, NB, P, HEAD).transpose(0, 2, 1, 3).reshape(NQ, P, -1)
    wp = np.repeat(w, HEAD, axis=1)
    for q in range(NQ):
        cnt = np.minimum(np.arange(PADW)[None, None, :] + 1 + q * QT, wp[:, :, None])
        t[q, :, 2 * NB * HEAD:] = (1.0 / cnt).transpose(1, 0, 2).reshape(P, 32)

    dist = P - (np.arange(384) - (P - 1))
    ok = (dist >= 0) & (dist < P)
    half = NBUCKET // 2
    n = np.maximum(dist, 0)
    large = half + (np.log(np.maximum(n, 1) / half) / np.log(MAXDIST / half) * (NBUCKET - half)).astype(np.int64)
    bucket = np.where(n < half, n, np.minimum(large, NBUCKET - 1))
    one = np.zeros((NBUCKET + 1, 384), np.float32)
    one[bucket[ok], np.arange(384)[ok]] = 1.0
    one[NBUCKET, ~ok] = NEG
    return c, t.reshape(NQ * P, TABW), one


def layout_mixer_weights(w_in, w_out):
    col = 0
    starts = []
    for size in (384, 128, 128, 384, 384, 384, 384, 256):
        starts.append(col)
        col += size
    qa, ka, va, qr, kr, vr, gr, up = starts
    head = [np.arange(h * HEAD, (h + 1) * HEAD) for h in range(NQH)]
    pair = [np.concatenate([head[c], head[c + GROUP]]) for c in range(GROUP)]
    cols = [qa + pair[c] for c in range(GROUP)]
    cols += [s + np.arange(P) for s in (ka, va, up)]
    cols += [s + c * P + np.arange(P) for s in (qr, kr, vr, gr) for c in range(3)]
    cols += [up + P + np.arange(P)]
    units = [w_in[:, k].reshape(C, P, P).transpose(1, 0, 2).reshape(P, C * P) for k in cols]
    rows = [pair[c] for c in range(GROUP)] + [384 + c * P + np.arange(P) for c in range(5)]
    units += [w_out[k, :] for k in rows]
    return np.ascontiguousarray(np.stack(units))


def layout_mlp_weights(w_up, w_down):
    ups = [w_up[:, f * P:(f + 1) * P].reshape(C, P, P).transpose(1, 0, 2).reshape(P, C * P) for f in range(2 * NG)]
    downs = [w_down[f * P:(f + 1) * P, :] for f in range(2 * NG)]
    units = []
    for g in range(NG):
        n = (g + 1) % NG
        units += [downs[2 * g], downs[2 * g + 1], ups[2 * n], ups[2 * n + 1]]
    return np.ascontiguousarray(np.stack(units))


def kernel(x, attn_norm_g, w_in, attn_sinks, rel_bias, pool_w, pool_scale, w_out, mlp_norm_g, w_up, w_down, final_norm_g):
    import concourse.bacc as bacc
    from concourse.bass_utils import run_bass_kernel_spmd

    def a(v):
        return np.asarray(v)

    cst, tab, onehot = shape_constants()
    arrays = {
        "x": a(x).reshape(SEQ, D),
        "wmix": layout_mixer_weights(a(w_in)[0], a(w_out)[0]),
        "wmlp": layout_mlp_weights(a(w_up)[0], a(w_down)[0]),
        "cst": cst, "tab": tab, "onehot": onehot,
        "gmix": a(attn_norm_g).reshape(1, D), "gmlp": a(mlp_norm_g).reshape(1, D),
        "gfin": a(final_norm_g).reshape(1, D), "sinks": a(attn_sinks).reshape(1, NQH), "rel_bias": a(rel_bias),
        "pool_w": a(pool_w)[0], "pool_scale": a(pool_scale).reshape(2, P).T,
    }
    arrays = {f"in_{k}": np.ascontiguousarray(v) for k, v in arrays.items()}
    nc = bacc.Bacc("TRN2", target_bir_lowering=False, num_devices=1)
    args = [nc.dram_tensor(k, v.shape, mybir.dt.from_np(v.dtype), kind="ExternalInput").ap() for k, v in arrays.items()]
    out = nc.dram_tensor("out", (SEQ, D), F32, kind="ExternalOutput").ap()
    build(nc, *args, out)
    got = run_bass_kernel_spmd(nc, [arrays], core_ids=[0])
    return got.results[0]["out"].reshape(1, SEQ, D)
```
